# Optimizing a Trainium2 kernel written in Bass

```python
import jax
import jax.numpy as jnp
from jax import lax
import numpy as np

D_MODEL = 1024
BATCH = 1
SEQ = 512
DEPTH = 1

CHUNK = 64
N_META = 16
Q_BLOCK = 128

A_HEADS = 8
A_HEAD_DIM = 64
A_KV_RANK = 128
IDX_HEADS = 8
IDX_DIM = 64
TOPK_MAX = 256

B_HEADS = 8
B_HEAD_DIM = 64
DECAY_LORA = 64
AAA_LORA = 64
GATE_LORA = 128
B_LNX_EPS = 64e-5

PEER_HEADS = 8
PEER_NKEYS = 128
PEER_QDIM = 256
PEER_HALF = PEER_QDIM // 2
PEER_TOPK = 16
PEER_EXPERTS = PEER_NKEYS * PEER_NKEYS

A_WIDTH = A_HEADS * A_HEAD_DIM
B_WIDTH = B_HEADS * B_HEAD_DIM
N_BRANCH = 2
A_SIZES = (A_WIDTH, A_KV_RANK, IDX_HEADS * IDX_DIM, IDX_DIM, IDX_HEADS)
B_SIZES = (B_WIDTH, B_WIDTH, B_WIDTH, DECAY_LORA, AAA_LORA, GATE_LORA)
B_COLS = sum(B_SIZES)
GATE_COLS = N_BRANCH * D_MODEL
IN_SIZES = A_SIZES + (B_COLS, GATE_COLS)
N_IN = sum(IN_SIZES)
LN_EPS = 1e-5

kernel_name = "hybrid_dsa_rwkv7_peer_block"

def _split(t, sizes):
    idx = np.cumsum(np.array(sizes))[:-1]
    return jnp.split(t, [int(i) for i in idx], axis=-1)

def _layernorm(x, g, b, eps=LN_EPS):
    xf = x.astype(jnp.float32)
    mu = jnp.mean(xf, axis=-1, keepdims=True)
    var = jnp.mean(jnp.square(xf - mu), axis=-1, keepdims=True)
    return ((xf - mu) * lax.rsqrt(var + eps) * g + b).astype(x.dtype)

def _rmsnorm(x, g, eps=1e-6):
    xf = x.astype(jnp.float32)
    return (xf * lax.rsqrt(jnp.mean(xf * xf, axis=-1, keepdims=True) + eps) * g).astype(x.dtype)

def _chunk_ids(n):
    t = jnp.arange(n, dtype=jnp.int32)
    return jnp.where(t < N_META, 0, 1 + (t - N_META) // CHUNK)

def _token_shift(p, mu):
    prev = jnp.pad(p, ((0, 0), (1, 0), (0, 0)))[:, :-1]
    return p + (prev - p) * mu

def _dsa_mixer(q, c_kv, q_idx, k_idx, w_idx, kv_norm_g, w_uk, w_uv, kidx_g, kidx_b, k_sel):
    Bn, T = q.shape[0], q.shape[1]
    c_kv = _rmsnorm(c_kv, kv_norm_g)
    k_idx = _layernorm(k_idx, kidx_g, kidx_b)
    q_abs = jnp.einsum('bthd,rhd->bthr', q, w_uk)
    cid = _chunk_ids(T)
    nblk = T // Q_BLOCK
    w_scale = (IDX_HEADS ** -0.5) * (IDX_DIM ** -0.5)
    att_scale = A_HEAD_DIM ** -0.5

    def blocks(a):
        return jnp.moveaxis(a.reshape((Bn, nblk, Q_BLOCK) + a.shape[2:]), 1, 0)

    def one_block(args):
        qa, qi, wi, qc = args
        logits = jnp.einsum('bqhd,bsd->bqhs', qi, k_idx).astype(jnp.float32)
        score = jnp.einsum('bqh,bqhs->bqs', wi.astype(jnp.float32) * w_scale, jax.nn.relu(logits))
        admissible = cid[None, :] <= qc[:, None]
        score = jnp.where(admissible[None], score, -jnp.inf)
        top_s, top_i = lax.top_k(score, k_sel)
        valid = jnp.isfinite(top_s)
        c_sel = jax.vmap(lambda c, i: c[i])(c_kv, top_i)
        s = jnp.einsum('bqhr,bqkr->bqhk', qa, c_sel).astype(jnp.float32) * att_scale
        s = jnp.where(valid[:, :, None, :], s, -jnp.inf)
        p = jax.nn.softmax(s, axis=-1).astype(c_sel.dtype)
        o_lat = jnp.einsum('bqhk,bqkr->bqhr', p, c_sel)
        return jnp.einsum('bqhr,rhd->bqhd', o_lat, w_uv)

    out = lax.map(one_block, (blocks(q_abs), blocks(q_idx), blocks(w_idx), cid.reshape(nblk, Q_BLOCK)))
    return jnp.moveaxis(out, 0, 1).reshape(Bn, T, A_WIDTH)

def _rwkv7_mixer(r, k, v, wl, al, gl, w0, w2, a0, a2, g2, k_k, k_a, r_k, lnx_g, lnx_b):
    Bn, T = r.shape[0], r.shape[1]
    H, N = B_HEADS, B_HEAD_DIM
    f32 = jnp.float32
    w_log = -jax.nn.softplus(-(w0 + jnp.tanh(wl) @ w2).astype(f32)) - 0.5
    decay = jnp.exp(-jnp.exp(w_log))
    a = jax.nn.sigmoid((a0 + al @ a2).astype(f32))
    g = jax.nn.sigmoid(gl) @ g2
    heads = lambda t: t.reshape(Bn, T, H, N).astype(f32)
    kk = heads(k * k_k)
    kk = kk * lax.rsqrt(jnp.sum(kk * kk, axis=-1, keepdims=True) + 1e-12)
    k = k * (1.0 + (a - 1.0) * k_a)
    rh, kh, vh, ah, dh = heads(r), heads(k), heads(v), heads(a), heads(decay)
    bh = kk * ah

    def step(S, inp):
        r_t, w_t, k_t, v_t, kk_t, b_t = inp
        sa = jnp.einsum('bhvk,bhk->bhv', S, -kk_t)
        S = S * w_t[:, :, None, :] + sa[..., None] * b_t[:, :, None, :] + v_t[..., None] * k_t[:, :, None, :]
        return S, jnp.einsum('bhvk,bhk->bhv', S, r_t)

    tm = lambda t: jnp.moveaxis(t, 1, 0)
    S0 = jnp.zeros((Bn, H, N, N), f32)
    _, y = lax.scan(step, S0, (tm(rh), tm(dh), tm(kh), tm(vh), tm(kk), tm(bh)))
    y = jnp.moveaxis(y, 0, 1)
    mu = jnp.mean(y, axis=-1, keepdims=True)
    var = jnp.mean(jnp.square(y - mu), axis=-1, keepdims=True)
    y = ((y - mu) * lax.rsqrt(var + B_LNX_EPS)).reshape(Bn, T, B_WIDTH) * lnx_g + lnx_b
    bonus = jnp.sum(rh * kh * r_k.reshape(H, N).astype(f32), axis=-1, keepdims=True) * vh
    y = (y + bonus.reshape(Bn, T, B_WIDTH)) * g
    return y.astype(r.dtype)

def _peer(x, wq, subkeys, u, v):
    Bn, T, D = x.shape
    n = Bn * T
    xf = x.reshape(n, D)
    q = (xf @ wq).reshape(n, PEER_HEADS, 2, PEER_HALF)
    s = jnp.einsum('nhpd,hpkd->nhpk', q, subkeys).astype(jnp.float32)
    s_top, i_top = lax.top_k(s, PEER_TOPK)
    cand = s_top[:, :, 0, :, None] + s_top[:, :, 1, None, :]
    cand_idx = i_top[:, :, 0, :, None] * PEER_NKEYS + i_top[:, :, 1, None, :]
    best_s, best_j = lax.top_k(cand.reshape(n, PEER_HEADS, -1), PEER_TOPK)
    expert = jnp.take_along_axis(cand_idx.reshape(n, PEER_HEADS, -1), best_j, axis=-1)
    gate = jax.nn.softmax(best_s, axis=-1)
    nblk = n // Q_BLOCK

    def one_block(args):
        xb, eb, gb = args
        h = jnp.einsum('nd,nhkd->nhk', xb, u[eb]).astype(jnp.float32)
        coef = (gb * jax.nn.gelu(h, approximate=False)).astype(xb.dtype)
        return jnp.einsum('nhk,nhkd->nd', coef, v[eb])

    out = lax.map(one_block, (xf.reshape(nblk, Q_BLOCK, D),
                              expert.reshape(nblk, Q_BLOCK, PEER_HEADS, PEER_TOPK),
                              gate.reshape(nblk, Q_BLOCK, PEER_HEADS, PEER_TOPK)))
    return out.reshape(Bn, T, D)

def setup_inputs(seed: int = 0) -> dict:
    key = jax.random.key(seed)
    ks = iter(jax.random.split(key, 40))
    f32 = jnp.float32
    L, D = DEPTH, D_MODEL
    beta = (8.0 * DEPTH) ** -0.25
    nrm = lambda shape, scale: jax.random.normal(next(ks), shape, f32) * scale
    uni = lambda shape: jax.random.uniform(next(ks), shape, f32)
    return {
        "x": nrm((BATCH, SEQ, D), 1.0),
        "meta": nrm((N_META, D), 1.0),
        "ln_in_g": 1.0 + nrm((D,), 0.02),
        "ln_in_b": nrm((D,), 0.02),
        "w_in": nrm((L, D, N_IN), D ** -0.5),
        "b_gate": nrm((L, GATE_COLS), 0.02),
        "a_kv_norm_g": 1.0 + nrm((L, A_KV_RANK), 0.02),
        "a_w_uk": nrm((L, A_KV_RANK, A_HEADS, A_HEAD_DIM), A_KV_RANK ** -0.5),
        "a_w_uv": nrm((L, A_KV_RANK, A_HEADS, A_HEAD_DIM), A_KV_RANK ** -0.5),
        "a_kidx_g": 1.0 + nrm((L, IDX_DIM), 0.02),
        "a_kidx_b": nrm((L, IDX_DIM), 0.02),
        "b_mu": uni((L, B_COLS)),
        "b_w0": -6.0 + 5.0 * uni((L, B_WIDTH)),
        "b_w2": nrm((L, DECAY_LORA, B_WIDTH), 0.1),
        "b_a0": nrm((L, B_WIDTH), 0.1),
        "b_a2": nrm((L, AAA_LORA, B_WIDTH), 0.1),
        "b_g2": nrm((L, GATE_LORA, B_WIDTH), GATE_LORA ** -0.5),
        "b_k_k": 0.85 + nrm((L, B_WIDTH), 0.02),
        "b_k_a": 1.0 + nrm((L, B_WIDTH), 0.02),
        "b_r_k": nrm((L, B_WIDTH), 0.1),
        "b_lnx_g": 1.0 + nrm((L, B_WIDTH), 0.02),
        "b_lnx_b": nrm((L, B_WIDTH), 0.02),
        "w_pa": nrm((L, A_WIDTH, D), beta * A_WIDTH ** -0.5),
        "w_pb": nrm((L, B_WIDTH, D), beta * B_WIDTH ** -0.5),
        "w_o": nrm((L, D, D), beta * D ** -0.5),
        "ln1_g": 1.0 + nrm((L, D), 0.02),
        "ln1_b": nrm((L, D), 0.02),
        "peer_wq": nrm((L, D, PEER_HEADS * PEER_QDIM), D ** -0.5),
        "peer_subkeys": nrm((L, PEER_HEADS, 2, PEER_NKEYS, PEER_HALF), PEER_HALF ** -0.5),
        "peer_u": nrm((L, PEER_EXPERTS, D), D ** -0.5),
        "peer_v": nrm((L, PEER_EXPERTS, D), beta),
        "ln2_g": 1.0 + nrm((L, D), 0.02),
        "ln2_b": nrm((L, D), 0.02),
    }

def reference(x, meta, ln_in_g, ln_in_b, w_in, b_gate, a_kv_norm_g, a_w_uk, a_w_uv, a_kidx_g, a_kidx_b,
              b_mu, b_w0, b_w2, b_a0, b_a2, b_g2, b_k_k, b_k_a, b_r_k, b_lnx_g, b_lnx_b,
              w_pa, w_pb, w_o, ln1_g, ln1_b, peer_wq, peer_subkeys, peer_u, peer_v, ln2_g, ln2_b):
    Bn, S, D = x.shape
    T = N_META + S
    T_pad = -(-T // Q_BLOCK) * Q_BLOCK
    k_sel = min(TOPK_MAX, S // 4)
    alpha = (2.0 * DEPTH) ** 0.25
    h = jnp.concatenate([jnp.broadcast_to(meta[None].astype(x.dtype), (Bn, N_META, D)), x,
                         jnp.zeros((Bn, T_pad - T, D), x.dtype)], axis=1)
    h = _layernorm(h, ln_in_g, ln_in_b)
    for l in range(DEPTH):
        p = h @ w_in[l]
        aq, ackv, aqi, aki, awi, bcols, gcols = _split(p, IN_SIZES)
        bcols = _token_shift(bcols, b_mu[l])
        br, bk, bv, bwl, bal, bgl = _split(bcols, B_SIZES)
        o_a = _dsa_mixer(aq.reshape(Bn, T_pad, A_HEADS, A_HEAD_DIM), ackv,
                         aqi.reshape(Bn, T_pad, IDX_HEADS, IDX_DIM), aki, awi,
                         a_kv_norm_g[l], a_w_uk[l], a_w_uv[l], a_kidx_g[l], a_kidx_b[l], k_sel)
        o_b = _rwkv7_mixer(br, bk, bv, bwl, bal, bgl, b_w0[l], b_w2[l], b_a0[l], b_a2[l], b_g2[l],
                           b_k_k[l], b_k_a[l], b_r_k[l], b_lnx_g[l], b_lnx_b[l])
        gates = jax.nn.sigmoid((gcols + b_gate[l]).astype(jnp.float32)).astype(h.dtype)
        mixed = gates[..., :D] * (o_a @ w_pa[l]) + gates[..., D:] * (o_b @ w_pb[l])
        h = _layernorm(alpha * h + mixed @ w_o[l], ln1_g[l], ln1_b[l])
        h = _layernorm(alpha * h + _peer(h, peer_wq[l], peer_subkeys[l], peer_u[l], peer_v[l]),
                       ln2_g[l], ln2_b[l])
    return h[:, N_META:T]


_drawn_inputs = setup_inputs


def setup_inputs(seed=0):
    import zlib

    import numpy as np

    out = dict(_drawn_inputs(seed))
    spreads = {}
    factors = {'b_gate': 7.603,
     'a_kv_norm_g': 6.764,
     'a_kidx_g': 4.771,
     'a_kidx_b': 5.097,
     'b_w2': 3.286,
     'b_a0': 3.575,
     'b_k_k': 5.366,
     'b_k_a': 4.524,
     'b_lnx_g': 4.699,
     'b_lnx_b': 4.804,
     'ln2_g': 2.907,
     'ln2_b': 2.743}
    for name, (base, spread) in spreads.items():
        noise = np.random.default_rng([zlib.crc32(name.encode()), seed]).standard_normal(out[name].shape)
        drawn = base * np.exp(spread * noise) if base else spread * noise
        out[name] = jnp.asarray(drawn.astype(out[name].dtype))
    for name, factor in factors.items():
        out[name] = (out[name] * factor).astype(out[name].dtype)
    return out
```

```python
from contextlib import ExitStack

import numpy as np

import concourse.bass as bass
from concourse import mybir

F32 = mybir.dt.float32
BF16 = mybir.dt.bfloat16
U32 = mybir.dt.uint32
ALU = mybir.AluOpType
ACT = mybir.ActivationFunctionType
AX = mybir.AxisListType

P = 128
D = 1024
KD = D // P
META, SEQ, CHUNK = 16, 512, 64
T = META + SEQ
NT = SEQ // P
HALF = T // 2
LN_EPS, RMS_EPS, KK_EPS, LNX_EPS = EPSILONS = 1e-5, 1e-6, 1e-12, 64e-5
ALPHA = 2.0 ** 0.25
HEADS, HD = 8, 64
PAIRS = HEADS * HD // P
KV = 128
TOPK = min(256, SEQ // 4)
ISCALE = HEADS ** -0.5 * HD ** -0.5
ASCALE = HD ** -0.5
EXPERT_KEYS, PEER_HEADS, PEER_TOPK = 128, 8, 16
LOT = 16
MARK, FILL, LOW = -3.4e38, -3.3e38, -1.0e30

CT_R, CT_K, CT_V, CT_WA, CT_G = 0, 4, 8, 12, 13
CT_Q, CT_CKV, CT_QI, CT_KI, CT_GATE = 14, 18, 19, 23, 24
NCT = 40
PW = T + 1

PARAMS = [("ln_in_g", 8), ("ln_in_b", 8), ("mu", 14), ("b_gate", 16), ("kv_g", 1), ("ki_g", 1), ("ki_b", 1),
          ("w0", 4), ("a0", 4), ("k_k", 4), ("k_a", 4), ("r_k", 4), ("lnx_g", 4), ("lnx_b", 4),
          ("ln1_g", 8), ("ln1_b", 8)]
PCOL, _n = {}, 0
for _name, _w in PARAMS:
    PCOL[_name] = _n
    _n += _w
NPARAM = _n

TILES = [(0, META)] + [(META + P * i, P) for i in range(NT)]
WIDTH = [META + P * (i + 1) for i in range(NT)]


class Order:

    def __init__(self, eng, sem):
        self.eng, self.sem, self.n = eng, sem, 0

    def put(self, ins):
        ins.then_inc(self.sem, 1)
        self.n += 1
        return self.n

    def settle(self):
        if self.n:
            self.eng.wait_ge(self.sem, self.n)


def semaphores(nc, ctx, stage):
    made = []

    def sem(name):
        made.append(nc.alloc_semaphore(f"{stage}.{name}"))
        return made[-1]

    def retire():
        nc.clear_and_free_semaphores(made)
        nc.all_engine_barrier()

    ctx.callback(retire)
    return sem


def build(nc, a, out):
    with ExitStack() as ctx:
        def sb(name, shape, dt=F32, at=None):
            return (at or ctx).enter_context(nc.sbuf_tensor(name, shape, dt))

        def semaphore(name, at=None):
            return (at or ctx).enter_context(nc.semaphore(name))

        ps = ctx.enter_context(nc.psum_tensor("ps", [P, 8, 512], F32))
        params = sb("params", [P, NPARAM])
        ident = sb("ident", [P, P])
        ones = sb("ones", [P, P])
        pair_ones = sb("pair_ones", [P, P])
        h_tok = sb("h_tok", [P, NT, D])
        wi_tok = sb("wi_tok", [P, NT, HEADS])
        eps = sb("eps", [P, 4])

        arena = sb("arena", [P, NCT * PW])
        p_all = arena[:, :].rearrange("p (c t) -> p c t", c=NCT)
        h1T = arena[:, 0:KD * SEQ].rearrange("p (k t) -> p k t", k=KD)
        dense = nc.dram_tensor("dense_gates", [SEQ // LOT, P, P * LOT], F32, kind="Internal").ap()

        def par(name, i=0, rows=P):
            c = PCOL[name] + i
            return params[0:rows, c:c + 1]

        with ExitStack() as layer:
            out_gate = sb("out_gate", [P, PAIRS, T], at=layer)
            bonus = sb("bonus", [P, PAIRS, T], at=layer)
            chunk_decay = sb("chunk_decay", [P, PAIRS, 1 + SEQ // CHUNK], at=layer)
            attended = sb("attended", [P, PAIRS, SEQ], at=layer)
            project(nc, a, locals())
            attend(nc, a, locals())
            prepare(nc, a, locals())
            scan_chunks(nc, a, locals())
            join(nc, a, locals())
        route(nc, a, locals())
        experts(nc, a, locals(), out)


def project(nc, a, g):
    ps, params, ident, ones, pair_ones = g["ps"], g["params"], g["ident"], g["ones"], g["pair_ones"]
    h_tok, p_all, wi_tok, par, eps = g["h_tok"], g["p_all"], g["wi_tok"], g["par"], g["eps"]
    RING = 4
    with ExitStack() as ctx:
        sb = lambda name, shape: ctx.enter_context(nc.sbuf_tensor(name, shape, F32))
        sem = semaphores(nc, ctx, "project")
        meta_tok = sb("meta_tok", [META, D])
        hT = sb("hT", [P, KD, T])
        w_ring = sb("w_ring", [P, RING, KD * P])
        wi_w = sb("wi_w", [P, KD, HEADS])
        g_row = sb("g_row", [P, D])
        b_row = sb("b_row", [P, D])
        stats = sb("stats", [P, 5, 2, 6])
        mv = sb("mv", [P, 5, 2])
        std = sb("std", [P, 5])
        rstd = sb("rstd", [P, 5])
        x_landed = [sem(f"x_landed{i}") for i in range(5)]
        params_landed, rows_landed, wiw_landed = sem("params_landed"), sem("rows_landed"), sem("wiw_landed")
        w_landed = [sem(f"w_landed{j}") for j in range(RING)]
        consts_made, zeros_made, var_ready, std_ready = sem("consts_made"), sem("zeros_made"), sem("var_ready"), sem("std_ready")
        ln_done, hT_bank, hT_copied_v, hT_copied_s = sem("ln_done"), sem("hT_bank"), sem("hT_copied_v"), sem("hT_copied_s")
        proj_done, proj_copied, wi_done, wi_copied = sem("proj_done"), sem("proj_copied"), sem("wi_done"), sem("wi_copied")
        pool_order, dve_order, hT_read = sem("pool_order"), sem("dve_order"), sem("hT_read")

        eps_made = sem("eps_made")

        def tok(i):
            return meta_tok[:, :] if i == 0 else h_tok[:, i - 1, :]

        block = ctx.enter_context(nc.Block())

        @block.sync
        def _(sp):
            sp.dma_start(meta_tok[:, :], a["meta"]).then_inc(x_landed[0], 16)
            for i in range(NT):
                sp.dma_start(h_tok[:, i, :], a["x"][0, P * i:P * (i + 1), :]).then_inc(x_landed[i + 1], 16)
            sp.dma_start(params[:, :], a["params"]).then_inc(params_landed, 16)
            for j in range(RING):
                sp.dma_start(w_ring[:, j, :], a["w_in_t"][j]).then_inc(w_landed[j], 16)
            sp.dma_start(wi_w[:, :, :], a["wi_w"]).then_inc(wiw_landed, 16)
            sp.dma_start(g_row[:, :], a["ln_in_g"].partition_broadcast(P)).then_inc(rows_landed, 16)
            sp.dma_start(b_row[:, :], a["ln_in_b"].partition_broadcast(P)).then_inc(rows_landed, 16)
            with sp.Fori(1, NCT // RING) as i:
                for j in range(RING):
                    sp.wait_ge(proj_done, i * RING + (j - RING + 1))
                    sp.dma_start(w_ring[:, j, :], a["w_in_t"][i * RING + j]).then_inc(w_landed[j], 16)

        @block.gpsimd
        def _(pool):
            order = Order(pool, pool_order)
            for n, e in enumerate(EPSILONS):
                nc.gpsimd.memset(eps[:, n:n + 1], e).then_inc(eps_made, 1)
            order.put(nc.gpsimd.memset(ident[:, :], 0.0))
            nc.gpsimd.memset(ones[:, :], 1.0).then_inc(consts_made, 1)
            order.settle()
            nc.gpsimd.affine_select(out=ident[:, :], in_=ident[:, :], compare_op=ALU.not_equal, fill=1.0, base=0,
                                    pattern=[[-1, P]], channel_multiplier=1).then_inc(consts_made, 1)
            nc.gpsimd.memset(p_all[:, :, 0:1], 0.0).then_inc(zeros_made, 1)
            pool.wait_ge(rows_landed, 32)
            for i in range(NT):
                pool.wait_ge(hT_read, i + 2)
                order.put(nc.gpsimd.tensor_tensor(h_tok[:, i, :], h_tok[:, i, :], g_row[:, :], ALU.mult))
            order.settle()
            for i in range(NT):
                order.put(nc.gpsimd.tensor_tensor(h_tok[:, i, :], h_tok[:, i, :], b_row[:, :], ALU.add))
            order.settle()

        @block.vector
        def _(dve):
            order = Order(dve, dve_order)
            order.put(nc.vector.memset(pair_ones[:, :], 0.0))
            order.settle()
            for h in range(2):
                order.put(nc.vector.memset(pair_ones[HD * h:HD * (h + 1), HD * h:HD * (h + 1)], 1.0))
            for i, (_, n) in enumerate(TILES):
                dve.wait_ge(x_landed[i], 16)
                for c in range(2):
                    order.put(nc.vector.bn_stats(stats[0:n, i, c, :], tok(i)[:, 512 * c:512 * (c + 1)]))
            order.settle()
            for i, (_, n) in enumerate(TILES):
                nc.vector.bn_aggr(mv[0:n, i, :], stats[0:n, i, :, :]).then_inc(var_ready, 1)
            for i, (_, n) in enumerate(TILES):
                dve.wait_ge(std_ready, i + 1)
                order.put(nc.vector.reciprocal(rstd[0:n, i:i + 1], std[0:n, i:i + 1]))
            order.settle()
            for i, (_, n) in enumerate(TILES):
                nc.vector.tensor_scalar(tok(i), tok(i), mv[0:n, i, 0:1], rstd[0:n, i:i + 1],
                                        ALU.subtract, ALU.mult).then_inc(ln_done, 1)
            dve.wait_ge(params_landed, 16)
            for i, (t0, n) in enumerate(TILES):
                dve.wait_ge(hT_bank, 2 * i + 1)
                for k in range(4):
                    last = nc.vector.tensor_scalar(hT[:, k, t0:t0 + n], ps[:, 2 * (i % 2), P * k:P * k + n],
                                                   par("ln_in_g", k), par("ln_in_b", k), ALU.mult, ALU.add)
                last.then_inc(hT_copied_v, 1)
            dve.wait_ge(wi_done, 1)
            nc.vector.tensor_scalar(wi_tok[:, :, :], ps[:, 4, 0:NT * HEADS].rearrange("p (i h) -> p i h", i=NT),
                                    ISCALE, None, ALU.mult).then_inc(wi_copied, 1)

        @block.scalar
        def _(act):
            act.wait_ge(eps_made, len(EPSILONS))
            for i, (_, n) in enumerate(TILES):
                act.wait_ge(var_ready, i + 1)
                nc.scalar.activation(std[0:n, i:i + 1], mv[0:n, i, 1:2], ACT.Sqrt, bias=eps[0:n, 0:1]
                                     ).then_inc(std_ready, 1)
            act.wait_ge(params_landed, 16)
            for i, (t0, n) in enumerate(TILES):
                act.wait_ge(hT_bank, 2 * i + 2)
                for k in range(4, KD):
                    last = nc.scalar.activation(hT[:, k, t0:t0 + n], ps[:, 2 * (i % 2) + 1, P * (k - 4):P * (k - 4) + n],
                                                ACT.Identity, bias=par("ln_in_b", k), scale=par("ln_in_g", k))
                last.then_inc(hT_copied_s, 1)
            with act.Fori(0, NCT // 2) as i:
                for j in range(2):
                    act.wait_ge(proj_done, i * 2 + (j + 1))
                    nc.scalar.activation(p_all[:, i * 2 + j, 1:PW].rearrange("p (h t) -> p h t", h=2),
                                         ps[:, 4 + 2 * j:6 + 2 * j, 0:HALF], ACT.Copy).then_inc(proj_copied, 1)

        @block.tensor
        def _(pe):
            pe.wait_ge(consts_made, 2)
            for i, (t0, n) in enumerate(TILES):
                pe.wait_ge(ln_done, i + 1)
                if i >= 2:
                    pe.wait_ge(hT_copied_v, i - 1)
                    pe.wait_ge(hT_copied_s, i - 1)
                for k in range(KD):
                    last = nc.tensor.transpose(ps[:, 2 * (i % 2) + k // 4, P * (k % 4):P * (k % 4) + n],
                                               tok(i)[:, P * k:P * (k + 1)], ident[0:n, 0:n])
                    if k == 3:
                        last.then_inc(hT_bank, 1)
                last.then_inc(hT_bank, 1)
                pe.wait_ge(hT_bank, 2 * i + 2)
                pe.sem_inc(hT_read, 1)
            pe.wait_ge(hT_copied_v, len(TILES))
            pe.wait_ge(hT_copied_s, len(TILES))

            def index_weights():
                pe.wait_ge(wiw_landed, 16)
                for i in range(NT):
                    for k in range(KD):
                        last = nc.tensor.matmul(ps[:, 4, HEADS * i:HEADS * (i + 1)],
                                                hT[:, k, META + P * i:META + P * (i + 1)], wi_w[:, k, :],
                                                start=(k == 0), stop=(k == KD - 1))
                last.then_inc(wi_done, 1)
                pe.wait_ge(wi_copied, 1)

            def columns(i, j, first):
                ct = i * RING + j
                pe.wait_ge(w_landed[j], 16 if first else (i + 1) * 16)
                if not first or j >= 2:
                    pe.wait_ge(proj_copied, ct - 1)
                for half in range(2):
                    for k in range(KD):
                        last = nc.tensor.matmul(ps[:, 4 + 2 * (j % 2) + half, 0:HALF], w_ring[:, j, P * k:P * (k + 1)],
                                                hT[:, k, HALF * half:HALF * (half + 1)],
                                                start=(k == 0), stop=(k == KD - 1))
                last.then_inc(proj_done, 1)

            index_weights()
            for j in range(RING):
                columns(0, j, True)
            with pe.Fori(1, NCT // RING) as i:
                for j in range(RING):
                    columns(i, j, False)


def attend(nc, a, g):
    ps, ident, ones, pair_ones = g["ps"], g["ident"], g["ones"], g["pair_ones"]
    p_all, par, eps, wi_tok, attended = g["p_all"], g["par"], g["eps"], g["wi_tok"], g["attended"]
    with ExitStack() as ctx:
        sb = lambda name, shape: ctx.enter_context(nc.sbuf_tensor(name, shape, F32))
        sem = semaphores(nc, ctx, "attend")
        w_uk = sb("w_uk", [P, PAIRS, KV])
        w_uv = sb("w_uv", [P, HEADS * HD])
        cT, c_tok = sb("cT", [P, T]), sb("c_tok", [P, 1 + NT, KV])
        kiT = sb("kiT", [P, T])
        q_abs = sb("q_abs", [P, HEADS, SEQ])
        score = sb("score", [P, T])
        relu = sb("relu", [P, 2, T])
        barred = sb("barred", [P, T])
        best = sb("best", [P, 8])
        prob = sb("prob", [P, HEADS, T])
        peak, low_peak, total, share = (sb(n, [P, HEADS]) for n in ("peak", "low_peak", "total", "share"))
        probT = sb("probT", [P, 1 + NT, 4 * P])
        lat = sb("lat", [P, HEADS, P])
        landed, squares, summed, roots, centred, c_ready, ki_ready = (
            sem(n) for n in ("uk_landed", "c_squares", "c_summed", "c_roots", "centred", "c_ready", "ki_ready"))
        c_turned, c_copied, abs_done, abs_copied = sem("c_turned"), sem("c_copied"), sem("abs_done"), sem("abs_copied")
        logit_done, relu_done, relu_used = sem("logit_done"), sem("relu_done"), sem("relu_used")
        att_done, att_read, exped, shared, scaled = (
            sem(n) for n in ("att_done", "att_read", "exped", "shared", "scaled"))
        turned, turn_copied, lat_done, lat_copied, out_done, out_copied = (
            sem(n) for n in ("p_turned", "p_copied", "lat_done", "lat_copied", "oa_done", "oa_copied"))
        order_sem = sem("dve_order2")
        q, qi = p_all[:, CT_Q:CT_Q + 4, 1 + META:PW], p_all[:, CT_QI:CT_QI + 4, 1 + META:PW]
        ckv, ki = p_all[:, CT_CKV, 1:PW], p_all[:, CT_KI, 1:PW]
        sq, root = prob[:, 0:2, :], prob[:, 2:4, :]
        halves = lambda x: x.rearrange("p (h t) -> p h t", h=2)
        blocks = lambda i: list(enumerate(TILES[:i + 2]))
        turns_before = lambda i: sum(2 * (x + 2) for x in range(i))
        block = ctx.enter_context(nc.Block())

        @block.sync
        def _(sp):
            sp.dma_start(w_uk[:, :, :], a["w_uk"]).then_inc(landed, 16)
            sp.dma_start(w_uv[:, :], a["w_uv"]).then_inc(landed, 16)
            sp.wait_ge(landed, 32)

        @block.scalar
        def _(act):
            act.wait_ge(summed, 1)
            nc.scalar.activation(halves(root[:, 0, :]), ps[:, 0:2, 0:HALF], ACT.Sqrt, bias=eps[:, 1:2],
                                 scale=1.0 / KV).then_inc(roots, 1)
            act.wait_ge(summed, 3)
            nc.scalar.activation(halves(root[:, 1, :]), ps[:, 4:6, 0:HALF], ACT.Sqrt, bias=eps[:, 0:1],
                                 scale=1.0 / HD).then_inc(roots, 1)
            act.wait_ge(c_turned, 1)
            nc.scalar.activation(c_tok[:, 1:1 + NT, :], ps[:, 6, :].rearrange("p (b r) -> p b r", b=NT), ACT.Copy
                                 ).then_inc(c_copied, 1)
            nc.scalar.activation(c_tok[0:META, 0, :], ps[0:META, 7, 0:KV], ACT.Copy).then_inc(c_copied, 1)
            for h in range(HEADS):
                act.wait_ge(abs_done, h + 1)
                nc.scalar.activation(q_abs[:, h, :], ps[:, h % 4, :], ACT.Copy).then_inc(abs_copied, 1)

            def relus(i):
                w = WIDTH[i]
                for h in range(HEADS):
                    n = HEADS * i + h
                    act.wait_ge(logit_done, n + 1)
                    if n >= 2:
                        act.wait_ge(relu_used, n - 1)
                    src = ps[:, 2 * (h % 2):2 * (h % 2) + 2, :].rearrange("p b t -> p (b t)")[:, 0:w]
                    nc.scalar.activation(relu[:, h % 2, 0:w], src, ACT.Relu).then_inc(relu_done, 1)

            relus(0)
            for i in range(NT):
                w = WIDTH[i]
                for h in range(HEADS):
                    act.wait_ge(att_read, HEADS * i + h + 1)
                    nc.scalar.activation(prob[:, h, 0:w], prob[:, h, 0:w], ACT.Exp, bias=low_peak[:, h:h + 1],
                                         accum_out=total[:, h:h + 1]).then_inc(exped, 1)
                    if h:
                        act.wait_ge(shared, HEADS * i + h)
                        nc.scalar.activation(prob[:, h - 1, 0:w], prob[:, h - 1, 0:w], ACT.Copy,
                                             scale=share[:, h - 1:h]).then_inc(scaled, 1)
                act.wait_ge(shared, HEADS * (i + 1))
                nc.scalar.activation(prob[:, HEADS - 1, 0:w], prob[:, HEADS - 1, 0:w], ACT.Copy,
                                     scale=share[:, HEADS - 1:HEADS]).then_inc(scaled, 1)
                if i + 1 < NT:
                    relus(i + 1)
                n = turns_before(i)
                for half in range(2):
                    for b, (_, m) in blocks(i):
                        act.wait_ge(turned, n + 1)
                        if n:
                            act.wait_ge(lat_done, 2 * i + half)
                        nc.scalar.activation(probT[0:m, b, :], ps[0:m, 4 + n % 2, :], ACT.Copy).then_inc(turn_copied, 1)
                        n += 1
                    act.wait_ge(lat_done, 2 * i + half + 1)
                    if i:
                        act.wait_ge(out_done, i)
                    nc.scalar.activation(lat[:, 4 * half:4 * half + 4, :], ps[:, 6, :].rearrange("p (h q) -> p h q", h=4),
                                         ACT.Copy).then_inc(lat_copied, 1)
                act.wait_ge(out_done, i + 1)
                nc.scalar.activation(attended[:, :, P * i:P * (i + 1)], ps[:, 7, :].rearrange("p (j q) -> p j q", j=4),
                                     ACT.Copy).then_inc(out_copied, 1)

        @block.tensor
        def _(pe):
            def sums(weights, src, bank):
                for half in range(2):
                    last = nc.tensor.matmul(ps[:, bank + half, 0:HALF], weights[:, :],
                                            src[:, HALF * half:HALF * (half + 1)], start=True, stop=True)
                last.then_inc(summed, 1)

            pe.wait_ge(squares, 1)
            sums(ones, sq[:, 0, :], 0)
            sums(pair_ones, ki, 2)
            pe.wait_ge(squares, 2)
            sums(pair_ones, sq[:, 1, :], 4)
            pe.wait_ge(c_ready, 1)
            for b, (t0, n) in enumerate(TILES):
                dst = ps[0:n, 7, 0:KV] if b == 0 else ps[0:n, 6, KV * (b - 1):KV * b]
                last = nc.tensor.transpose(dst, cT[:, t0:t0 + n], ident[:, :])
            last.then_inc(c_turned, 1)
            pe.wait_ge(landed, 32)
            pe.wait_ge(roots, 2)
            pe.wait_ge(centred, 1)
            for h in range(HEADS):
                e, j = h % 2, h // 2
                if h >= 4:
                    pe.wait_ge(abs_copied, h - 3)
                rows = slice(HD * e, HD * (e + 1))
                nc.tensor.matmul(ps[:, h % 4, :], w_uk[rows, j, :], q[rows, j, :], start=True, stop=True
                                 ).then_inc(abs_done, 1)

            def pieces(bank, w):
                return [(ps[:, bank, 0:min(w, 512)], 0, min(w, 512))] + ([(ps[:, bank + 1, 0:w - 512], 512, w)] if w > 512 else [])

            def logits(i):
                for h in range(HEADS):
                    n = HEADS * i + h
                    rows = slice(HD * (h % 2), HD * (h % 2 + 1))
                    if n >= 2:
                        pe.wait_ge(relu_done, n - 1)
                    for dst, lo, hi in pieces(2 * (h % 2), WIDTH[i]):
                        last = nc.tensor.matmul(dst, qi[rows, h // 2, P * i:P * (i + 1)], kiT[rows, lo:hi],
                                                start=True, stop=True)
                    last.then_inc(logit_done, 1)

            pe.wait_ge(ki_ready, 1)
            pe.wait_ge(abs_copied, HEADS)
            pe.wait_ge(c_copied, 2)
            logits(0)
            for i in range(NT):
                if i:
                    pe.wait_ge(out_copied, i)
                    pe.wait_ge(lat_copied, 2 * i)
                for h in range(HEADS):
                    n = HEADS * i + h
                    if n >= 2:
                        pe.wait_ge(att_read, n - 1)
                    for dst, lo, hi in pieces(4 + 2 * (h % 2), WIDTH[i]):
                        last = nc.tensor.matmul(dst, q_abs[:, h, P * i:P * (i + 1)], cT[:, lo:hi], start=True, stop=True)
                    last.then_inc(att_done, 1)
                if i + 1 < NT:
                    logits(i + 1)
                pe.wait_ge(att_read, HEADS * (i + 1))
                n = turns_before(i)
                for half in range(2):
                    pe.wait_ge(scaled, HEADS * i + 4 * half + 4)
                    for b, (k0, m) in blocks(i):
                        if n >= 2:
                            pe.wait_ge(turn_copied, n - 1)
                        for h in range(4):
                            last = nc.tensor.transpose(ps[0:m, 4 + n % 2, P * h:P * (h + 1)],
                                                       prob[:, 4 * half + h, k0:k0 + m], ident[:, :])
                        last.then_inc(turned, 1)
                        n += 1
                    pe.wait_ge(turn_copied, n)
                    if half:
                        pe.wait_ge(lat_copied, 2 * i + 1)
                    for b, (k0, m) in blocks(i):
                        last = nc.tensor.matmul(ps[:, 6, :], c_tok[0:m, b, :], probT[0:m, b, :],
                                                start=(b == 0), stop=(b == i + 1))
                    last.then_inc(lat_done, 1)
                pe.wait_ge(lat_copied, 2 * i + 2)
                for h in range(HEADS):
                    e, j = h % 2, h // 2
                    last = nc.tensor.matmul(ps[HD * e:HD * (e + 1), 7, P * j:P * (j + 1)], w_uv[:, HD * h:HD * (h + 1)],
                                            lat[:, h, :], start=True, stop=True)
                last.then_inc(out_done, 1)

        @block.vector
        def _(dve):
            order = Order(dve, order_sem)
            put, settle = order.put, order.settle
            v_ = nc.vector
            v_.tensor_tensor(sq[:, 0, :], ckv, ckv, ALU.mult).then_inc(squares, 1)
            dve.wait_ge(summed, 2)
            put(v_.scalar_tensor_tensor(halves(ki), ps[:, 2:4, 0:HALF], -1.0 / HD, halves(ki), ALU.mult, ALU.add))
            settle()
            v_.tensor_tensor(sq[:, 1, :], ki, ki, ALU.mult).then_inc(squares, 1)
            dve.wait_ge(roots, 1)
            put(v_.reciprocal(root[:, 0, :], root[:, 0, :]))
            settle()
            v_.scalar_tensor_tensor(cT[:, :], ckv, par("kv_g"), root[:, 0, :], ALU.mult, ALU.mult).then_inc(c_ready, 1)
            dve.wait_ge(roots, 2)
            put(v_.reciprocal(root[:, 1, :], root[:, 1, :]))
            settle()
            put(v_.scalar_tensor_tensor(kiT[:, :], ki, par("ki_g"), root[:, 1, :], ALU.mult, ALU.mult))
            settle()
            v_.tensor_scalar(kiT[:, :], kiT[:, :], par("ki_b"), None, ALU.add).then_inc(ki_ready, 1)
            dve.sem_inc(centred, 1)
            for i in range(NT):
                w = WIDTH[i]
                s = score[:, 0:w]
                hidden = slice(w - CHUNK, w)
                for h in range(HEADS):
                    dve.wait_ge(relu_done, HEADS * i + h + 1)
                    weight, src = wi_tok[:, i, h:h + 1], relu[:, h % 2, 0:w]
                    if h == 0:
                        ins = v_.tensor_scalar(s, src, weight, None, ALU.mult)
                    else:
                        dve.wait_ge(relu_used, HEADS * i + h)
                        ins = v_.scalar_tensor_tensor(s, src, weight, s, ALU.mult, ALU.add)
                    ins.then_inc(relu_used, 1)
                dve.wait_ge(relu_used, HEADS * (i + 1))
                put(v_.memset(score[0:HD, hidden], FILL))
                settle()
                for _ in range(TOPK // 8):
                    put(v_.max(best[:, :], s))
                    settle()
                    put(v_.match_replace(s, best[:, :], s, MARK))
                    settle()
                if i:
                    dve.wait_ge(att_read, HEADS * i)
                put(v_.tensor_scalar(barred[:, 0:w], s, MARK, LOW, ALU.not_equal, ALU.mult))
                settle()
                put(v_.memset(barred[0:HD, hidden], LOW))
                settle()
                if i:
                    dve.wait_ge(turned, turns_before(i))
                for h in range(HEADS):
                    dve.wait_ge(att_done, HEADS * i + h + 1)
                    src = ps[:, 4 + 2 * (h % 2):6 + 2 * (h % 2), :].rearrange("p b t -> p (b t)")[:, 0:w]
                    put(v_.tensor_tensor_reduce(prob[:, h, 0:w], src, barred[:, 0:w], ASCALE, FILL, ALU.add, ALU.max,
                                                peak[:, h:h + 1]))
                    settle()
                    v_.tensor_scalar(low_peak[:, h:h + 1], peak[:, h:h + 1], -1.0, None, ALU.mult).then_inc(att_read, 1)
                    if h:
                        dve.wait_ge(exped, HEADS * i + h)
                        v_.reciprocal(share[:, h - 1:h], total[:, h - 1:h]).then_inc(shared, 1)
                dve.wait_ge(exped, HEADS * (i + 1))
                v_.reciprocal(share[:, HEADS - 1:HEADS], total[:, HEADS - 1:HEADS]).then_inc(shared, 1)


def prepare(nc, a, g):
    ps, pair_ones, p_all, par, eps = g["ps"], g["pair_ones"], g["p_all"], g["par"], g["eps"]
    out_gate, bonus, chunk_decay = g["out_gate"], g["bonus"], g["chunk_decay"]
    with ExitStack() as ctx:
        sb = lambda name, shape: ctx.enter_context(nc.sbuf_tensor(name, shape, F32))
        sem = semaphores(nc, ctx, "prepare")
        lora = sb("lora", [P, 512])
        lora_g = sb("lora_g", [P, 512])
        step = sb("step", [P, CT_G + 1, T])
        decay = sb("decay", [P, PAIRS, T])
        rate = sb("rate", [P, PAIRS, T])
        kk = sb("kk", [P, PAIRS, T])
        keep = sb("keep", [P, PAIRS])
        at_start = step[:, 0:4, :]
        norm = step[:, 4:8, :]
        work = step[:, 8:12, :]
        r, k, v = (p_all[:, c:c + 4, 1:PW] for c in (CT_R, CT_K, CT_V))
        wa, gl = p_all[:, CT_WA, 1:PW], p_all[:, CT_G, 1:PW]
        aT, bT = p_all[:, CT_Q:CT_Q + 4, 1:PW], p_all[:, CT_Q + 4:CT_Q + 8, 1:PW]
        landed, shifted, squashed, low_done = sem("lora_landed"), sem("shifted"), sem("squashed"), sem("low_done")
        low_read_s, low_read_v = sem("low_read_s"), sem("low_read_v")
        squares, norms_summed, norms_read = sem("squares"), sem("norms_summed"), sem("norms_read")
        decay_ready, rk_ready, rk_summed, order_sem = sem("decay_ready"), sem("rk_ready"), sem("rk_summed"), sem("dve_order3")
        sig_done = sem("sig_done")
        block = ctx.enter_context(nc.Block())

        @block.sync
        def _(sp):
            sp.dma_start(lora[0:HD, :], a["w2"][0]).then_inc(landed, 16)
            sp.dma_start(lora[HD:P, :], a["a2"][0]).then_inc(landed, 16)
            sp.dma_start(lora_g[:, :], a["g2"][0]).then_inc(landed, 16)
            sp.wait_ge(landed, 48)

        @block.scalar
        def _(act):
            act.wait_ge(shifted, 1)
            nc.scalar.activation(wa[0:HD, :], wa[0:HD, :], ACT.Tanh).then_inc(squashed, 1)
            nc.scalar.activation(gl, gl, ACT.Sigmoid).then_inc(squashed, 1)
            for n in range(8):
                dst, bias = (decay, "w0") if n < 4 else (rate, "a0")
                act.wait_ge(low_done, n + 1)
                b = 2 * (n % 4)
                ins = nc.scalar.activation(dst[:, n % 4, :].rearrange("p (h t) -> p h t", h=2),
                                           ps[:, b:b + 2, 0:HALF], ACT.Sigmoid, bias=par(bias, n % 4))
                ins.then_inc(low_read_s, 1)
            act.wait_ge(low_read_s, 4)
            nc.scalar.activation(decay[:, :, :], decay[:, :, :], ACT.Exp, scale=-float(np.exp(-0.5))).then_inc(decay_ready, 1)
            for c in range(PAIRS):
                act.wait_ge(norms_summed, c + 1)
                nc.scalar.activation(norm[:, c, :].rearrange("p (h t) -> p h t", h=2), ps[:, 2 * c:2 * c + 2, 0:HALF],
                                     ACT.Sqrt, bias=eps[:, 2:3]).then_inc(norms_read, 1)

        @block.tensor
        def _(pe):
            pe.wait_ge(landed, 48)
            pe.wait_ge(squashed, 2)
            for n in range(12):
                b, c = 2 * (n % 4), n % 4
                if 4 <= n < 12:
                    pe.wait_ge(low_read_s, n - 3)
                w, x = ((lora[0:HD, :], wa[0:HD, :]), (lora[HD:P, :], wa[HD:P, :]), (lora_g[:, :], gl))[n // 4]
                for half in range(2):
                    last = nc.tensor.matmul(ps[:, b + half, 0:HALF], w[:, P * c:P * (c + 1)],
                                            x[:, HALF * half:HALF * (half + 1)], start=True, stop=True)
                last.then_inc(low_done, 1)

            def per_head_sums(src, done):
                for c in range(PAIRS):
                    for half in range(2):
                        last = nc.tensor.matmul(ps[:, 2 * c + half, 0:HALF], pair_ones[:, :],
                                                src[:, c, HALF * half:HALF * (half + 1)], start=True, stop=True)
                    last.then_inc(done, 1)

            pe.wait_ge(squares, 1)
            pe.wait_ge(low_read_v, 4)
            per_head_sums(work, norms_summed)
            pe.wait_ge(rk_ready, 1)
            pe.wait_ge(norms_read, PAIRS)
            per_head_sums(work, rk_summed)

        @block.vector
        def _(dve):
            order = Order(dve, order_sem)
            put, settle = order.put, order.settle
            v_ = nc.vector
            put(v_.tensor_tensor(step[:, :, :], p_all[:, 0:CT_G + 1, 0:T], p_all[:, 0:CT_G + 1, 1:PW], ALU.subtract))
            put(v_.tensor_scalar(keep[:, :], g["params"][:, PCOL["k_a"]:PCOL["k_a"] + 4], -1.0, 1.0, ALU.mult, ALU.add))
            settle()
            for c in [CT_WA, CT_G] + list(range(CT_WA)):
                ins = v_.scalar_tensor_tensor(p_all[:, c, 1:PW], step[:, c, :], par("mu", c), p_all[:, c, 1:PW],
                                              ALU.mult, ALU.add)
                put(ins)
                if c == CT_G:
                    settle()
                    dve.sem_inc(shifted, 1)
            settle()
            for c in range(PAIRS):
                put(v_.tensor_scalar(kk[:, c, :], k[:, c, :], par("k_k", c), None, ALU.mult))
            settle()
            v_.tensor_tensor(work, kk[:, :, :], kk[:, :, :], ALU.mult).then_inc(squares, 1)
            for c in range(PAIRS):
                dve.wait_ge(low_done, 9 + c)
                v_.tensor_copy(out_gate[:, c, :].rearrange("p (h t) -> p h t", h=2),
                               ps[:, 2 * c:2 * c + 2, 0:HALF]).then_inc(low_read_v, 1)
            dve.wait_ge(low_read_s, 8)
            dve.wait_ge(norms_summed, PAIRS)
            for c in range(PAIRS):
                put(v_.tensor_scalar(work[:, c, :], rate[:, c, :], par("k_a", c), keep[:, c:c + 1], ALU.mult, ALU.add))
            settle()
            put(v_.tensor_tensor(k, k, work, ALU.mult))
            settle()
            put(v_.tensor_tensor(work, r, k, ALU.mult))
            settle()
            for c in range(PAIRS):
                put(v_.tensor_scalar(work[:, c, :], work[:, c, :], par("r_k", c), None, ALU.mult))
            settle()
            dve.sem_inc(rk_ready, 1)
            put(v_.memset(at_start, 0.0))
            dve.wait_ge(decay_ready, 1)
            settle()
            starts = slice(META, T, CHUNK)
            put(v_.tensor_copy(at_start[:, :, 0:1], decay[:, :, 0:1]))
            put(v_.tensor_copy(at_start[:, :, starts], decay[:, :, starts]))
            settle()
            put(v_.memset(decay[:, :, 0:1], 0.0))
            put(v_.memset(decay[:, :, starts], 0.0))
            settle()
            flat = lambda x: x.rearrange("p c t -> p (c t)")
            put(v_.tensor_tensor_scan(flat(decay[:, :, :]), flat(decay[:, :, :]), flat(at_start), 0.0, ALU.mult, ALU.add))
            dve.wait_ge(norms_read, PAIRS)
            put(v_.reciprocal(norm, norm))
            settle()
            put(v_.tensor_tensor(kk[:, :, :], kk[:, :, :], norm, ALU.mult))
            put(v_.tensor_copy(chunk_decay[:, :, :], decay[:, :, META - 1:T:CHUNK]))
            settle()
            inverse = at_start
            put(v_.reciprocal(inverse, decay[:, :, :]))
            put(v_.tensor_tensor(aT[:, :, 1:T], kk[:, :, 1:T], decay[:, :, 0:T - 1], ALU.mult))
            put(v_.tensor_tensor(norm, kk[:, :, :], rate[:, :, :], ALU.mult))
            put(v_.tensor_tensor(r, r, decay[:, :, :], ALU.mult))
            settle()
            put(v_.tensor_copy(aT[:, :, 0:1], kk[:, :, 0:1]))
            put(v_.tensor_copy(aT[:, :, starts], kk[:, :, starts]))
            put(v_.tensor_tensor(bT, norm, inverse, ALU.mult))
            put(v_.tensor_tensor(k, k, inverse, ALU.mult))
            for c in range(PAIRS):
                dve.wait_ge(rk_summed, c + 1)
                put(v_.tensor_tensor(bonus[:, c, :].rearrange("p (h t) -> p h t", h=2), ps[:, 2 * c:2 * c + 2, 0:HALF],
                                     v[:, c, :].rearrange("p (h t) -> p h t", h=2), ALU.mult))
            settle()


def scan_chunks(nc, a, g):
    ps, ident, ones, pair_ones = g["ps"], g["ident"], g["ones"], g["pair_ones"]
    p_all, par, eps, chunk_decay = g["p_all"], g["par"], g["eps"], g["chunk_decay"]
    with ExitStack() as ctx:
        sb = lambda name, shape: ctx.enter_context(nc.sbuf_tensor(name, shape, F32))
        sem = semaphores(nc, ctx, "scan_chunks")
        below16, above16 = sb("below16", [P, P]), sb("above16", [P, P])
        below32, below64 = sb("below32", [P, P]), sb("below64", [P, P])
        above64, upto64 = sb("above64", [P, P]), sb("upto64", [P, P])
        k_hat, b_hat = sb("k_hat", [P, PAIRS, P]), sb("b_hat", [P, PAIRS, P])
        k_tok, b_tok = sb("k_tok", [P, 2, 512]), sb("b_tok", [P, 2, 512])
        v_tok = sb("v_tok", [P, 512])
        grams = {n: sb(n, [P, 2, 4, P]) for n in ("low16", "low32", "low64", "up16", "inv", "rb", "ak", "rk")}
        pw = [sb(f"pw{i}", [P, 2, 4, P]) for i in range(4)]
        x_sb, u_sb = sb("x_sb", [P, 512]), sb("u_sb", [P, 512])
        state = sb("state", [P, 3, PAIRS, P])
        faded = sb("faded", [P, PAIRS, P])
        masks_made, tok_zero = sem("masks_made"), sem("tok_zero")
        hats, turned, tok_copied = sem("hats"), sem("turned"), sem("tok_copied")
        gram_done, gram_read = sem("gram_done"), sem("gram_read")
        step_done, step_s, step_v = sem("step_done"), sem("step_s"), sem("step_v")
        x_done, x_read, u_done, u_read, s_done, s_read, y_done, y_read = (
            sem(n) for n in ("x_done", "x_read", "u_done", "u_read", "s_done", "s_read", "y_done", "y_read"))
        order_sem, pool_order, u16_made = sem("dve_order4"), sem("pool_order4"), sem("u16_made")
        kT, rT, vT = (p_all[:, c:c + 4, 1:PW] for c in (CT_K, CT_R, CT_V))
        aT, bT = p_all[:, CT_Q:CT_Q + 4, 1:PW], p_all[:, CT_Q + 4:CT_Q + 8, 1:PW]
        block = ctx.enter_context(nc.Block())

        low16, low32, low64, up16, inv = (grams[n] for n in ("low16", "low32", "low64", "up16", "inv"))
        GRAMS = [(aT, bT, [(low16, below16), (low32, below32), (low64, below64)]),
                 (bT, aT, [(up16, above16)]),
                 (kT, aT, [(grams["ak"], above64)]),
                 (bT, rT, [(grams["rb"], upto64)]),
                 (kT, rT, [(grams["rk"], upto64)])]
        STEPS = [(up16, low16, pw[0], "s", "copy", 0, 0),
                 (low16, up16, pw[1], "s", "copy", 0, 0),
                 (pw[0], inv, inv, "v", "add", 1, 0),
                 (pw[1], pw[0], pw[2], "s", "copy", 2, 0),
                 (pw[0], pw[1], pw[3], "s", "copy", 2, 0),
                 (pw[2], inv, inv, "v", "add", 3, 1),
                 (pw[3], pw[2], pw[0], "s", "copy", 4, 1),
                 (pw[0], inv, inv, "v", "add", 5, 2),
                 (low32, inv, pw[1], "s", "copy", 5, 3),
                 (inv, None, pw[2], "v", "copy", 5, 3),
                 (pw[2], pw[1], inv, "v", "subtract", 6, 4),
                 (low64, inv, pw[3], "s", "copy", 6, 5),
                 (inv, None, pw[0], "v", "copy", 6, 5),
                 (pw[0], pw[3], inv, "v", "subtract", 7, 6)]
        S16 = 8

        def steps_of(tt):
            return STEPS[:S16] if TILES[tt][1] == META else STEPS

        def before(tt, engine):
            return sum(2 * sum(s[3] == engine for s in steps_of(i)) for i in range(tt))

        def chunks_of(tt):
            return [(0, 0, META)] if tt == 0 else [(2 * tt - 1, 0, CHUNK), (2 * tt, CHUNK, CHUNK)]

        @block.gpsimd
        def _(pool):
            order = Order(pool, pool_order)

            def within(dst, w):
                view = dst[:, :].rearrange("p (b w) -> p b w", w=w)
                order.put(nc.gpsimd.affine_select(out=view, in_=ones[:, :].rearrange("p (b w) -> p b w", w=w),
                                                  compare_op=ALU.is_ge, fill=0.0, base=0,
                                                  pattern=[[-w, P // w], [0, w]], channel_multiplier=1))
                order.settle()
                order.put(nc.gpsimd.affine_select(out=view, in_=view, compare_op=ALU.is_ge, fill=0.0, base=w - 1,
                                                  pattern=[[w, P // w], [0, w]], channel_multiplier=-1))

            def side(dst, src, mult, strict):
                return nc.gpsimd.affine_select(out=dst[:, :], in_=src[:, :], compare_op=ALU.is_ge, fill=0.0,
                                               base=-strict, pattern=[[mult, P]], channel_multiplier=-mult)

            within(above16, 16)
            within(above64, 64)
            within(below32, 32)
            order.settle()
            order.put(nc.gpsimd.tensor_tensor(below64[:, :], above64[:, :], below32[:, :], ALU.subtract))
            order.settle()
            order.put(nc.gpsimd.tensor_tensor(below32[:, :], below32[:, :], above16[:, :], ALU.subtract))
            order.put(side(below16, above16, -1, 1))
            order.put(side(upto64, above64, 1, 0))
            order.settle()
            order.put(side(above16, above16, 1, 1))
            order.put(side(above64, above64, 1, 1))
            order.put(side(below32, below32, -1, 1))
            order.put(side(below64, below64, -1, 1))
            order.settle()
            pool.sem_inc(masks_made, 1)

        @block.vector
        def _(dve):
            order = Order(dve, order_sem)
            put, settle = order.put, order.settle
            v_ = nc.vector
            for x in (k_tok, b_tok, state):
                put(v_.memset(x[:, :, :], 0.0))
            put(v_.memset(x_sb[:, :], 0.0))
            put(v_.memset(u_sb[:, :], 0.0))
            put(v_.memset(v_tok[:, :], 0.0))
            settle()
            dve.sem_inc(tok_zero, 1)
            dve.wait_ge(masks_made, 1)
            for tt, (t0, n) in enumerate(TILES):
                if tt:
                    dve.wait_ge(turned, 3 * tt)
                for src, dst in ((kT, k_hat), (bT, b_hat)):
                    for c, p0, m in chunks_of(tt):
                        put(v_.tensor_tensor(dst[:, :, p0:p0 + m], src[:, :, t0 + p0:t0 + p0 + m],
                                             chunk_decay[:, :, c:c + 1].broadcast_to([P, PAIRS, m]), ALU.mult))
                settle()
                dve.sem_inc(hats, 1)
                if tt:
                    dve.wait_ge(y_done, tt)
                for i, (_, _, copies) in enumerate(GRAMS):
                    for e in range(2):
                        dve.wait_ge(gram_done, 10 * tt + 2 * i + e + 1)
                        bank = ps[0:n, (2 * i + e) % 4, :].rearrange("p (j t) -> p j t", j=4)[:, :, 0:n]
                        for dst, mask in copies:
                            put(v_.tensor_tensor(dst[0:n, e, :, 0:n], bank,
                                                 mask[0:n, 0:n].unsqueeze(1).broadcast_to([n, 4, n]), ALU.mult))
                        settle()
                        if i == 1:
                            put(v_.tensor_tensor(inv[0:n, e, :, 0:n], ident[0:n, 0:n].unsqueeze(1).broadcast_to([n, 4, n]),
                                                 up16[0:n, e, :, 0:n], ALU.subtract))
                            settle()
                        dve.sem_inc(gram_read, 1)
                steps = steps_of(tt)
                for i, (_, _, dst, engine, how, _, _) in enumerate(steps):
                    for e in range(2):
                        if engine != "v":
                            continue
                        dve.wait_ge(step_done, 2 * sum(len(steps_of(x)) for x in range(tt)) + 2 * i + e + 1)
                        bank = ps[0:n, 4 + 2 * e + i % 2, :].rearrange("p (j t) -> p j t", j=4)[:, :, 0:n]
                        d = dst[0:n, e, :, 0:n]
                        if how == "copy":
                            v_.tensor_copy(d, bank).then_inc(step_v, 1)
                        else:
                            v_.tensor_tensor(d, d, bank, ALU.add if how == "add" else ALU.subtract).then_inc(step_v, 1)
                for c, p0, m in chunks_of(tt):
                    now, after = state[:, c % 3], state[:, (c + 1) % 3]
                    dve.wait_ge(x_done, c + 1)
                    v_.tensor_copy(x_sb[p0:p0 + m, :], ps[p0:p0 + m, 0, :]).then_inc(x_read, 1)
                    put(v_.tensor_tensor(faded[:, :, :], now[:, :, :],
                                         chunk_decay[:, :, c:c + 1].broadcast_to([P, PAIRS, P]), ALU.mult))
                    settle()
                    dve.wait_ge(s_done, c + 1)
                    for e in range(2):
                        rows = slice(HD * e, HD * (e + 1))
                        put(v_.tensor_tensor(after[rows, :, rows], faded[rows, :, rows],
                                             ps[rows, 2, :].rearrange("p (j v) -> p j v", j=4)[:, :, rows], ALU.add))
                    settle()
                    dve.sem_inc(s_read, 1)

        @block.scalar
        def _(act):
            act.wait_ge(tok_zero, 1)
            for tt, (t0, n) in enumerate(TILES):
                for i, dst in enumerate((k_tok, b_tok, None)):
                    act.wait_ge(turned, 3 * tt + i + 1)
                    if dst is None:
                        nc.scalar.activation(v_tok[0:n, :], ps[0:n, 6, :], ACT.Copy).then_inc(tok_copied, 1)
                        continue
                    for x, (_, p0, m) in enumerate(chunks_of(tt)):
                        last = nc.scalar.activation(dst[p0:p0 + m, x, :], ps[p0:p0 + m, 4 + i, :], ACT.Copy)
                    last.then_inc(tok_copied, 1)
                steps = steps_of(tt)
                for i, (_, _, dst, engine, _, _, _) in enumerate(steps):
                    for e in range(2):
                        if engine != "s":
                            continue
                        act.wait_ge(step_done, 2 * sum(len(steps_of(x)) for x in range(tt)) + 2 * i + e + 1)
                        bank = ps[0:n, 4 + 2 * e + i % 2, :].rearrange("p (j t) -> p j t", j=4)[:, :, 0:n]
                        nc.scalar.activation(dst[0:n, e, :, 0:n], bank, ACT.Copy).then_inc(step_s, 1)
                for c, p0, m in chunks_of(tt):
                    act.wait_ge(u_done, c + 1)
                    nc.scalar.activation(u_sb[p0:p0 + m, :], ps[p0:p0 + m, 1, :], ACT.Copy, scale=-1.0).then_inc(u_read, 1)
                act.wait_ge(y_done, tt + 1)
                nc.scalar.activation(aT[:, :, t0:t0 + n], ps[:, 3, :].rearrange("p (j t) -> p j t", j=4)[:, :, 0:n],
                                     ACT.Copy).then_inc(y_read, 1)

        @block.tensor
        def _(pe):
            for tt, (t0, n) in enumerate(TILES):
                span = slice(t0, t0 + n)
                chunks = chunks_of(tt)
                pe.wait_ge(hats, tt + 1)
                if tt:
                    pe.wait_ge(step_v, before(tt, "v"))
                    pe.wait_ge(step_s, before(tt, "s"))
                for i in range(3):
                    for j in range(PAIRS):
                        src = (k_hat[:, j, 0:n], b_hat[:, j, 0:n], vT[:, j, span])[i]
                        last = nc.tensor.transpose(ps[0:n, 4 + i, P * j:P * (j + 1)], src, ident[:, :])
                    last.then_inc(turned, 1)
                if tt:
                    pe.wait_ge(y_read, tt)
                for i, (lhs, rhs, _) in enumerate(GRAMS):
                    for e in range(2):
                        at = 2 * i + e
                        if at >= 4:
                            pe.wait_ge(gram_read, 10 * tt + at - 3)
                        for j in range(PAIRS):
                            last = nc.tensor.matmul(ps[0:n, at % 4, P * j:P * j + n], lhs[HD * e:HD * (e + 1), j, span],
                                                    rhs[HD * e:HD * (e + 1), j, span], start=True, stop=True)
                        last.then_inc(gram_done, 1)
                pe.wait_ge(tok_copied, 3 * (tt + 1))
                s0, v0 = before(tt, "s"), before(tt, "v")
                for i, (lhs, rhs, _, _, _, need_s, need_v) in enumerate(steps_of(tt)):
                    for e in range(2):
                        if i == 0:
                            pe.wait_ge(gram_read, 10 * tt + 3 + e)
                        if need_s:
                            pe.wait_ge(step_s, s0 + 2 * need_s - 1 + e)
                        if need_v:
                            pe.wait_ge(step_v, v0 + 2 * need_v - 1 + e)
                        if i >= 2:
                            who = steps_of(tt)[i - 2][3]
                            taken = sum(s[3] == who for s in STEPS[:i - 1])
                            pe.wait_ge(step_s if who == "s" else step_v, (s0 if who == "s" else v0) + 2 * taken - 1 + e)
                        for j in range(4):
                            dst = ps[0:n, 4 + 2 * e + i % 2, P * j:P * j + n]
                            if rhs is None:
                                last = nc.tensor.transpose(dst, lhs[0:n, e, j, 0:n], ident[0:n, 0:n])
                            else:
                                last = nc.tensor.matmul(dst, lhs[0:n, e, j, 0:n], rhs[0:n, e, j, 0:n], start=True, stop=True)
                        last.then_inc(step_done, 1)
                pe.wait_ge(gram_read, 10 * (tt + 1))
                pe.wait_ge(step_v, before(tt + 1, "v"))
                for x, (c, p0, m) in enumerate(chunks):
                    rows = slice(p0, p0 + m)
                    now = state[:, c % 3]
                    for e in range(2):
                        for j in range(PAIRS):
                            h = 2 * j + e
                            nc.tensor.matmul(ps[rows, 0, HD * h:HD * (h + 1)], grams["ak"][0:n, e, j, rows],
                                             v_tok[0:n, HD * h:HD * (h + 1)], start=(h == 0), stop=False,
                                             skip_group_check=True)
                    if c:
                        pe.wait_ge(s_read, c)
                    for j in range(PAIRS):
                        last = nc.tensor.matmul(ps[rows, 0, P * j:P * (j + 1)], aT[:, j, t0 + p0:t0 + p0 + m],
                                                now[:, j, :], start=False, stop=(j == PAIRS - 1), skip_group_check=True)
                    last.then_inc(x_done, 1)
                    pe.wait_ge(x_read, c + 1)
                    for e in range(2):
                        for j in range(PAIRS):
                            h = 2 * j + e
                            last = nc.tensor.matmul(ps[rows, 1, HD * h:HD * (h + 1)], inv[0:n, e, j, rows],
                                                    x_sb[0:n, HD * h:HD * (h + 1)], start=True, stop=True)
                    last.then_inc(u_done, 1)
                    for j in range(PAIRS):
                        nc.tensor.matmul(ps[:, 2, P * j:P * (j + 1)], k_tok[0:n, x, P * j:P * (j + 1)],
                                         v_tok[0:n, P * j:P * (j + 1)], start=(j == 0), stop=False, skip_group_check=True)
                    pe.wait_ge(u_read, c + 1)
                    for j in range(PAIRS):
                        last = nc.tensor.matmul(ps[:, 2, P * j:P * (j + 1)], b_tok[0:n, x, P * j:P * (j + 1)],
                                                u_sb[0:n, P * j:P * (j + 1)], start=False, stop=(j == PAIRS - 1),
                                                skip_group_check=True)
                    last.then_inc(s_done, 1)
                for j in range(PAIRS):
                    for name, src in (("rk", v_tok), ("rb", u_sb)):
                        for e in range(2):
                            h = 2 * j + e
                            nc.tensor.matmul(ps[HD * e:HD * (e + 1), 3, P * j:P * j + n], src[0:n, HD * h:HD * (h + 1)],
                                             grams[name][0:n, e, j, 0:n], start=(name == "rk"), stop=False,
                                             skip_group_check=True)
                    for x, (c, p0, m) in enumerate(chunks):
                        last = nc.tensor.matmul(ps[:, 3, P * j + p0:P * j + p0 + m], state[:, c % 3, j, :],
                                                rT[:, j, t0 + p0:t0 + p0 + m], start=False, stop=(x == len(chunks) - 1),
                                                skip_group_check=True)
                last.then_inc(y_done, 1)


def join(nc, a, g):
    ps, ident, pair_ones, h_tok, h1T = g["ps"], g["ident"], g["pair_ones"], g["h_tok"], g["h1T"]
    p_all, par, eps, attended = g["p_all"], g["par"], g["eps"], g["attended"]
    out_gate, bonus = g["out_gate"], g["bonus"]
    with ExitStack() as ctx:
        sb = lambda name, shape: ctx.enter_context(nc.sbuf_tensor(name, shape, F32))
        sem = semaphores(nc, ctx, "join")
        w_pa, w_pb, w_o = sb("w_pa", [P, PAIRS, D]), sb("w_pb", [P, PAIRS, D]), sb("w_o", [P, KD, D])
        stats, mv, std, rstd = sb("stats1", [P, NT, 2, 6]), sb("mv1", [P, NT, 2]), sb("std1", [P, NT]), sb("rstd1", [P, NT])
        flat = g["arena"]
        g_row, b_row = flat[:, KD * SEQ:KD * SEQ + D], flat[:, KD * SEQ + D:KD * SEQ + 2 * D]
        real = slice(1 + META, PW)
        y = p_all[:, CT_Q:CT_Q + 4, real]
        root = p_all[:, CT_Q + 4:CT_Q + 8, real]
        gate = lambda c: p_all[:, CT_GATE + c, real]
        gates_a, gates_b = p_all[:, CT_GATE:CT_GATE + KD, real], p_all[:, CT_GATE + KD:CT_GATE + 2 * KD, real]
        landed = [sem(f"{n}_landed") for n in ("w_pa", "w_pb", "w_o", "row1")]
        sums_done, squares, roots, gated, ob_ready = (
            sem(n) for n in ("y_sums", "y_squares", "y_roots", "gated", "ob_ready"))
        branch_done, branch_read, mixed_ready = sem("branch_done"), sem("branch_read"), sem("mixed_ready")
        wo_done, var_ready, std_ready, ln_done = sem("wo_done"), sem("var1"), sem("std1_ready"), sem("ln1_done")
        wo_read = sem("wo_read")
        turned, copied_v, copied_s, order_sem, pool_order = (
            sem(n) for n in ("h1_turned", "h1_copied_v", "h1_copied_s", "dve_order5", "pool_order5"))
        block = ctx.enter_context(nc.Block())

        @block.sync
        def _(sp):
            for dst, name, s in ((w_pa, "w_pa", landed[0]), (w_pb, "w_pb", landed[1]), (w_o, "w_o", landed[2])):
                sp.dma_start(dst[:, :, :], a[name][0].rearrange("(k p) n -> p k n", p=P)).then_inc(s, 16)
            sp.dma_start(g_row, a["ln1_g"].partition_broadcast(P)).then_inc(landed[3], 16)
            sp.dma_start(b_row, a["ln1_b"].partition_broadcast(P)).then_inc(landed[3], 16)

        @block.scalar
        def _(act):
            for c in range(2 * KD):
                nc.scalar.activation(gate(c), gate(c), ACT.Sigmoid, bias=par("b_gate", c)).then_inc(gated, 1)
            for c in range(PAIRS):
                act.wait_ge(sums_done, PAIRS + c + 1)
                nc.scalar.activation(root[:, c, :], ps[:, c, :], ACT.Sqrt, bias=eps[:, 3:4], scale=1.0 / HD).then_inc(roots, 1)

            def root_of(i):
                act.wait_ge(var_ready, i + 1)
                nc.scalar.activation(std[:, i:i + 1], mv[:, i, 1:2], ACT.Sqrt, bias=eps[:, 0:1]).then_inc(std_ready, 1)

            root_of(0)
            for i in range(NT):
                if i + 1 < NT:
                    root_of(i + 1)
                act.wait_ge(turned, 2 * i + 2)
                for k in range(4, KD):
                    last = nc.scalar.activation(h1T[:, k, P * i:P * (i + 1)], ps[:, 4 + 2 * (i % 2) + 1, P * (k - 4):P * (k - 3)],
                                                ACT.Identity, bias=par("ln1_b", k), scale=par("ln1_g", k))
                last.then_inc(copied_s, 1)

        @block.tensor
        def _(pe):
            def head_sums(src):
                for c in range(PAIRS):
                    nc.tensor.matmul(ps[:, c, :], pair_ones[:, :], src[:, c, :], start=True, stop=True).then_inc(sums_done, 1)

            def branch(w, x, base):
                for c in range(KD):
                    n = base + c
                    if n >= 4:
                        pe.wait_ge(branch_read, n - 3)
                    for k in range(PAIRS):
                        last = nc.tensor.matmul(ps[:, 4 + n % 4, :], w[:, k, P * c:P * (c + 1)], x[:, k, :],
                                                start=(k == 0), stop=(k == PAIRS - 1))
                    last.then_inc(branch_done, 1)

            head_sums(y)
            pe.wait_ge(squares, 1)
            head_sums(root)
            pe.wait_ge(landed[0], 16)
            branch(w_pa, attended, 0)
            pe.wait_ge(landed[1], 16)
            pe.wait_ge(ob_ready, 1)
            branch(w_pb, y, KD)
            pe.wait_ge(landed[2], 16)
            pe.wait_ge(mixed_ready, 1)
            pe.wait_ge(roots, PAIRS)
            for i in range(NT):
                for half in range(2):
                    n = 2 * i + half
                    if n >= 4:
                        pe.wait_ge(wo_read, n - 3)
                    for k in range(KD):
                        last = nc.tensor.matmul(ps[:, n % 4, :], gates_a[:, k, P * i:P * (i + 1)],
                                                w_o[:, k, 512 * half:512 * (half + 1)], start=(k == 0), stop=(k == KD - 1))
                    last.then_inc(wo_done, 1)
            pe.wait_ge(branch_read, 2 * KD)
            for i in range(NT):
                pe.wait_ge(ln_done, i + 1)
                if i >= 2:
                    pe.wait_ge(copied_v, i - 1)
                    pe.wait_ge(copied_s, i - 1)
                for k in range(KD):
                    last = nc.tensor.transpose(ps[:, 4 + 2 * (i % 2) + k // 4, P * (k % 4):P * (k % 4 + 1)],
                                               h_tok[:, i, P * k:P * (k + 1)], ident[:, :])
                    if k % 4 == 3:
                        last.then_inc(turned, 1)

        @block.vector
        def _(dve):
            order = Order(dve, order_sem)
            put, settle = order.put, order.settle
            v_ = nc.vector
            for c in range(PAIRS):
                dve.wait_ge(sums_done, c + 1)
                put(v_.scalar_tensor_tensor(y[:, c, :], ps[:, c, :], -1.0 / HD, y[:, c, :], ALU.mult, ALU.add))
            settle()
            v_.tensor_tensor(root, y, y, ALU.mult).then_inc(squares, 1)
            dve.wait_ge(roots, PAIRS)
            put(v_.reciprocal(root, root))
            settle()
            put(v_.tensor_tensor(y, y, root, ALU.mult))
            settle()
            for c in range(PAIRS):
                put(v_.tensor_scalar(y[:, c, :], y[:, c, :], par("lnx_g", c), par("lnx_b", c), ALU.mult, ALU.add))
            settle()
            put(v_.tensor_tensor(y, y, bonus[:, :, META:T], ALU.add))
            settle()
            v_.tensor_tensor(y, y, out_gate[:, :, META:T], ALU.mult).then_inc(ob_ready, 1)
            for n in range(2 * KD):
                dve.wait_ge(gated, n + 1)
                dve.wait_ge(branch_done, n + 1)
                v_.tensor_tensor(gate(n), ps[:, 4 + n % 4, :], gate(n), ALU.mult).then_inc(branch_read, 1)
            dve.wait_ge(branch_read, 2 * KD)
            v_.tensor_tensor(gates_a, gates_a, gates_b, ALU.add).then_inc(mixed_ready, 1)

            def take_turned(i):
                dve.wait_ge(turned, 2 * i + 1)
                for k in range(4):
                    last = v_.tensor_scalar(h1T[:, k, P * i:P * (i + 1)], ps[:, 4 + 2 * (i % 2), P * k:P * (k + 1)],
                                            par("ln1_g", k), par("ln1_b", k), ALU.mult, ALU.add)
                last.then_inc(copied_v, 1)

            for i in range(NT):
                for half in range(2):
                    dve.wait_ge(wo_done, 2 * i + half + 1)
                    part = h_tok[:, i, 512 * half:512 * (half + 1)]
                    v_.scalar_tensor_tensor(part, part, ALPHA, ps[:, (2 * i + half) % 4, :], ALU.mult, ALU.add
                                            ).then_inc(wo_read, 1)
                dve.wait_ge(wo_read, 2 * i + 2)
                for half in range(2):
                    put(v_.bn_stats(stats[:, i, half, :], h_tok[:, i, 512 * half:512 * (half + 1)]))
                settle()
                v_.bn_aggr(mv[:, i, :], stats[:, i, :, :]).then_inc(var_ready, 1)
                dve.wait_ge(std_ready, i + 1)
                put(v_.reciprocal(rstd[:, i:i + 1], std[:, i:i + 1]))
                settle()
                v_.tensor_scalar(h_tok[:, i, :], h_tok[:, i, :], mv[:, i, 0:1], rstd[:, i:i + 1],
                                 ALU.subtract, ALU.mult).then_inc(ln_done, 1)
                if i:
                    take_turned(i - 1)
            take_turned(NT - 1)

        @block.gpsimd
        def _(pool):
            order = Order(pool, pool_order)
            pool.wait_ge(landed[3], 32)
            for i in range(NT):
                pool.wait_ge(turned, 2 * i + 2)
                order.put(nc.gpsimd.tensor_tensor(h_tok[:, i, :], h_tok[:, i, :], g_row, ALU.mult))
            order.settle()
            for i in range(NT):
                order.put(nc.gpsimd.tensor_tensor(h_tok[:, i, :], h_tok[:, i, :], b_row, ALU.add))
            order.settle()


def route(nc, a, g):
    ps, ident, h1T, dense = g["ps"], g["ident"], g["h1T"], g["dense"]
    NP = PEER_HEADS * PEER_TOPK
    K = PEER_TOPK
    LOTS = SEQ // LOT
    with ExitStack() as ctx:
        sb = lambda name, shape, dt=F32: ctx.enter_context(nc.sbuf_tensor(name, shape, dt))
        sem = semaphores(nc, ctx, "route")
        wq = sb("wq", [P, 4, KD * P])
        sub_keys = sb("sub_keys", [P, 2 * PEER_HEADS, P])
        qT = sb("qT", [P, 2, SEQ])
        s_head = sb("s_head", [P, 2, 2, NT, P])
        top = sb("top", [P, 2, NT, K])
        top_at = sb("top_at", [P, 2, NT, K], U32)
        keys = sb("keys", [P, 2, 2, NT, K])
        cand = sb("cand", [P, NT, K * K])
        best = sb("best6", [P, NT, K])
        best_at = sb("best_at", [P, NT, K], U32)
        split_at = sb("split_at", [P, 2, NT, K], U32)
        place = sb("place", [P, 2, NT, K])
        is_place = sb("is_place", [P, 2, 2, NT, K, K])
        picks = sb("picks", [P, 3, NT, NP])
        picksT = sb("picksT", [P, 3, SEQ])
        small = sb("small", [P, NT * PEER_HEADS])
        count16, count128 = sb("count16", [P, K]), sb("count128", [P, P])
        now = sb("now", [P, 3, 2 * LOT])
        spare = g["arena"][:, KD * SEQ:]
        hot2, hot1 = (spare[:, 16 * P * x:16 * P * (x + 1)].rearrange("p (s k) -> p s k", s=16) for x in range(2))
        lot = spare[:, 32 * P:32 * P + 2 * P * LOT].rearrange("p (r k n) -> p r k n", r=2, k=P)
        wq_landed = [sem(f"wq_landed{j}") for j in range(4)]
        keys_landed, counted = sem("sub_keys_landed"), sem("counted")
        q_done, q_copied, s_done, s_copied, topped = (sem(n) for n in ("q_done", "q_copied", "s_done", "s_copied", "topped"))
        placed, found, summed = sem("placed"), sem("found"), sem("found_summed")
        order_sem, softmax_sem, now_ready = sem("dve_order6"), sem("softmax_order"), sem("now_ready")
        lowered, raised, gates_ready, picks_turned, picks_copied = (
            sem(n) for n in ("lowered", "raised", "gates_ready", "picks_turned", "picks_copied"))
        hot_ready, four_done, four_copied = sem("hot_ready"), sem("four_done"), sem("four_copied")
        lot_stored = [sem(f"lot_stored{j}") for j in range(2)]
        block = ctx.enter_context(nc.Block())

        @block.sync
        def _(sp):
            for j in range(4):
                sp.dma_start(wq[:, j, :], a["wq_t"][j]).then_inc(wq_landed[j], 16)
            sp.dma_start(sub_keys[:, :, :], a["sub_keys"]).then_inc(keys_landed, 16)
            with sp.Fori(1, PEER_HEADS // 2) as i:
                for j in range(4):
                    sp.wait_ge(q_done, i * 4 + (j - 3))
                    sp.dma_start(wq[:, j, :], a["wq_t"][i * 4 + j]).then_inc(wq_landed[j], 16)
            with sp.Fori(0, LOTS // 2) as i:
                for j in range(2):
                    sp.wait_ge(four_copied, i * 8 + (4 * j + 4 + 8))
                    sp.dma_start(dense[i * 2 + j], lot[:, j, :, :].rearrange("p k n -> p (k n)")).then_inc(lot_stored[j], 16)
            for j in range(2):
                sp.wait_ge(lot_stored[j], 16 * (LOTS // 2))

        @block.gpsimd
        def _(pool):
            nc.gpsimd.iota(count16[:, :], [[1, K]], 0, 0, allow_small_or_imprecise_dtypes=True).then_inc(counted, 1)
            nc.gpsimd.iota(count128[:, :], [[1, P]], 0, 0, allow_small_or_imprecise_dtypes=True).then_inc(counted, 1)
            pool.wait_ge(counted, 2)
            with pool.Fori(0, PEER_HEADS // 2) as i:
                for r in range(2):
                    pool.wait_ge(placed, i * 2 + (r + 1))
                    for x in range(2):
                        nc.gpsimd.tensor_tensor(is_place[:, r, x], is_place[:, r, x],
                                                keys[:, r, x].unsqueeze(2).broadcast_to([P, NT, K, K]), ALU.mult
                                                ).then_inc(found, 1)

        @block.scalar
        def _(act):
            act.sem_inc(s_copied, 4)
            act.sem_inc(four_copied, 8)
            with act.Fori(0, PEER_HEADS // 2) as i:
                for r in range(2):
                    for x in range(2):
                        act.wait_ge(q_done, i * 4 + (2 * r + x + 1))
                        act.wait_ge(s_done, i * 4 + (2 * r + x + 1))
                        nc.scalar.activation(qT[:, x, :], ps[:, 2 * r + x, :], ACT.Copy).then_inc(q_copied, 1)
                    act.wait_ge(topped, i * 2 + (r + 1))
                    for x in range(2):
                        act.wait_ge(s_done, i * 4 + (2 * r + x + 3))
                        nc.scalar.activation(s_head[:, r, x], ps[:, 4 + 2 * r + x, :].rearrange("p (t k) -> p t k", t=NT),
                                             ACT.Copy).then_inc(s_copied, 1)
            act.wait_ge(lowered, 1)
            nc.scalar.activation(picks[:, 2], picks[:, 2], ACT.Exp).then_inc(raised, 1)
            with act.Fori(0, LOTS // 2) as i:
                for q in range(8):
                    if q % 4 == 0:
                        act.wait_ge(lot_stored[q // 4], i * 16)
                    act.wait_ge(four_done, i * 8 + (q + 1 + 4))
                    nc.scalar.activation(lot[:, q // 4, :, 4 * (q % 4):4 * (q % 4) + 4].rearrange("p k n -> p n k"),
                                         ps[:, q, :].rearrange("p (n k) -> p n k", n=4), ACT.Copy).then_inc(four_copied, 1)

        @block.tensor
        def _(pe):
            pe.sem_inc(s_done, 2)
            pe.sem_inc(four_done, 4)
            pe.wait_ge(keys_landed, 16)
            with pe.Fori(0, PEER_HEADS // 2) as i:
                for r in range(2):
                    for x in range(2):
                        pe.wait_ge(wq_landed[2 * r + x], (i + 1) * 16)
                        for k in range(KD):
                            last = nc.tensor.matmul(ps[:, 2 * r + x, :], wq[:, 2 * r + x, P * k:P * (k + 1)], h1T[:, k, :],
                                                    start=(k == 0), stop=(k == KD - 1))
                        last.then_inc(q_done, 1)
                    for x in range(2):
                        pe.wait_ge(q_copied, i * 4 + (2 * r + x + 1))
                        pe.wait_ge(s_copied, i * 4 + (2 * r + x + 1))
                        for t in range(NT):
                            last = nc.tensor.matmul(ps[:, 4 + 2 * r + x, P * t:P * (t + 1)], qT[:, x, P * t:P * (t + 1)],
                                                    sub_keys[:, i * 4 + (2 * r + x), :], start=True, stop=True)
                        last.then_inc(s_done, 1)
            pe.wait_ge(s_copied, 2 * PEER_HEADS + 4)
            pe.wait_ge(gates_ready, 1)
            for x in range(3):
                for t in range(NT):
                    last = nc.tensor.transpose(ps[:, x, P * t:P * (t + 1)], picks[:, x, t, :], ident[:, :])
                last.then_inc(picks_turned, 1)
            pe.wait_ge(picks_copied, 3)
            with pe.Fori(0, LOTS // 2) as i:
                for q in range(8):
                    pe.wait_ge(four_copied, i * 8 + (q + 1))
                    pe.wait_ge(hot_ready, i * 8 + (q + 1))
                    for n in range(4):
                        s = (4 * q + n) % 16
                        last = nc.tensor.matmul(ps[:, q, P * n:P * (n + 1)], hot2[:, s, :], hot1[:, s, :],
                                                start=True, stop=True)
                    last.then_inc(four_done, 1)

        @block.vector
        def _(dve):
            v_ = nc.vector
            dve.sem_inc(topped, 2)
            dve.wait_ge(counted, 2)

            def rank(i, r):
                done = [0]

                def put(ins):
                    ins.then_inc(order_sem, 1)
                    done[0] += 1

                def settle():
                    dve.wait_ge(order_sem, done[0])

                def best_two_rounds(values, out, at, streams):
                    lo, hi = slice(0, 8), slice(8, 16)
                    for x in streams:
                        put(v_.max(out(x)[:, lo], values(x)))
                    settle()
                    for x in streams:
                        put(v_.max_index(at(x)[:, lo], out(x)[:, lo], values(x)))
                    settle()
                    for x in streams:
                        put(v_.match_replace(values(x), out(x)[:, lo], values(x), MARK))
                    settle()
                    for x in streams:
                        put(v_.max(out(x)[:, hi], values(x)))
                    settle()
                    for x in streams:
                        put(v_.max_index(at(x)[:, hi], out(x)[:, hi], values(x)))

                dve.sem_clear(order_sem)
                dve.wait_ge(s_copied, i * 4 + (2 * r + 2 + 4))
                dve.sem_inc(order_sem, 1)
                done[0] += 1
                best_two_rounds(lambda x: s_head[:, r, x // NT, x % NT, :], lambda x: top[:, x // NT, x % NT, :],
                                lambda x: top_at[:, x // NT, x % NT, :], range(2 * NT))
                settle()
                dve.sem_inc(topped, 1)
                put(v_.tensor_copy(keys[:, r], top_at[:, :]))
                put(v_.tensor_tensor(cand[:, :, :].rearrange("p t (x y) -> p t x y", x=K),
                                     top[:, 0].unsqueeze(3).broadcast_to([P, NT, K, K]),
                                     top[:, 1].unsqueeze(2).broadcast_to([P, NT, K, K]), ALU.add))
                settle()
                best_two_rounds(lambda t: cand[:, t, :], lambda t: best[:, t, :], lambda t: best_at[:, t, :], range(NT))
                settle()
                put(v_.tensor_scalar(split_at[:, 0], best_at[:, :], 4, None, ALU.logical_shift_right))
                put(v_.tensor_scalar(split_at[:, 1], best_at[:, :], K - 1, None, ALU.bitwise_and))
                put(v_.tensor_copy(picks[:, 2, :, bass.ds(i * (2 * K) + r * K, K)], best[:, :]))
                settle()
                put(v_.tensor_copy(place[:, :], split_at[:, :]))
                settle()
                for x in range(2):
                    put(v_.tensor_tensor(is_place[:, r, x].rearrange("p t k j -> p (t k) j"),
                                         place[:, x].rearrange("p t k -> p (t k)").unsqueeze(2).broadcast_to([P, NT * K, K]),
                                         count16[:, :].unsqueeze(1).broadcast_to([P, NT * K, K]), ALU.is_equal))
                settle()
                dve.sem_inc(placed, 1)

            def number(i, r):
                dve.wait_ge(found, i * 4 + (2 * r + 2))
                v_.tensor_reduce(picks[:, 0:2, :, bass.ds(i * (2 * K) + r * K, K)], is_place[:, r], AX.X,
                                 ALU.add).then_inc(summed, 1)

            rank(0, 0)
            rank(0, 1)
            number(0, 0)
            with dve.Fori(1, PEER_HEADS // 2) as i:
                rank(i, 0)
                number(i - 1, 1)
                rank(i, 1)
                number(i, 0)
            number(PEER_HEADS // 2 - 1, 1)
            gate = picks[:, 2].rearrange("p t (h k) -> p (t h) k", h=PEER_HEADS)
            dve.wait_ge(summed, PEER_HEADS)
            v_.tensor_copy(small[:, :], gate[:, :, 0]).then_inc(softmax_sem, 1)
            dve.wait_ge(softmax_sem, 1)
            wide = small[:, :].unsqueeze(2).broadcast_to([P, NT * PEER_HEADS, K])
            v_.tensor_tensor(gate, gate, wide, ALU.subtract).then_inc(lowered, 1)
            dve.wait_ge(raised, 1)
            v_.tensor_reduce(small[:, :], gate, AX.X, ALU.add).then_inc(softmax_sem, 1)
            dve.wait_ge(softmax_sem, 2)
            v_.reciprocal(small[:, :], small[:, :]).then_inc(softmax_sem, 1)
            dve.wait_ge(softmax_sem, 3)
            v_.tensor_tensor(gate, gate, wide, ALU.mult).then_inc(gates_ready, 1)
            for x in range(3):
                dve.wait_ge(picks_turned, x + 1)
                v_.tensor_copy(picksT[:, x, :], ps[:, x, :]).then_inc(picks_copied, 1)
            dve.wait_ge(picks_copied, 3)
            with dve.Fori(0, LOTS // 2) as i:
                dve.wait_ge(hot_ready, i * 8)
                v_.tensor_copy(now[:, :, :], picksT[:, :, bass.ds(i * (2 * LOT), 2 * LOT)]).then_inc(now_ready, 1)
                dve.wait_ge(now_ready, i + 1)
                for q in range(8):
                    dve.wait_ge(four_done, i * 8 + (q + 1))
                    for n in range(4):
                        t = 4 * q + n
                        v_.tensor_scalar(hot2[:, t % 16, :], count128[:, :], now[:, 1, t:t + 1], None, ALU.is_equal)
                        last = v_.tensor_scalar(hot1[:, t % 16, :], count128[:, :], now[:, 0, t:t + 1],
                                                now[:, 2, t:t + 1], ALU.is_equal, ALU.mult)
                    last.then_inc(hot_ready, 1)


def experts(nc, a, g, out):
    ps, h_tok, h1T, dense, eps = g["ps"], g["h_tok"], g["h1T"], g["dense"], g["eps"]
    GT = 8
    GROUPS = EXPERT_KEYS // GT
    LOTS = SEQ // LOT
    with ExitStack() as ctx:
        sb = lambda name, shape, dt=F32: ctx.enter_context(nc.sbuf_tensor(name, shape, dt))
        sem = semaphores(nc, ctx, "experts")
        u_ring = sb("u_ring", [P, 4, KD * P])
        v_ring = g["arena"][:, KD * SEQ:KD * SEQ + 2 * GT * D].rearrange("p (r j d) -> p r j d", r=2, j=GT)
        gates = sb("gates", [P, 2, LOTS, GT * LOT])
        coef = sb("coef", [P, 2, GT, SEQ])
        act_out = sb("act_out", [P, 2, SEQ])
        g_row, b_row = sb("g_row2", [P, D]), sb("b_row2", [P, D])
        stats, mv, std, rstd = sb("stats2", [P, NT, 2, 6]), sb("mv2", [P, NT, 2]), sb("std2", [P, NT]), sb("rstd2", [P, NT])
        u_landed = [sem(f"u_landed{j}") for j in range(4)]
        v_landed, gates_landed = [sem(f"v_landed{j}") for j in range(2)], [sem(f"gates_landed{j}") for j in range(2)]
        hid_done, hid_read, coef_made, sum_done, sum_read = (
            sem(n) for n in ("hid_done", "hid_read", "coef_made", "sum_done", "sum_read"))
        scaled, order_sem, var_ready, std_ready, row_landed, ready = (
            sem(n) for n in ("h_scaled", "dve_order7", "var2", "std2_ready", "row2_landed", "out_ready"))
        stored = sem("out_stored")
        block = ctx.enter_context(nc.Block())

        @block.sync
        def _(sp):
            def load(i, r):
                sp.wait_ge(coef_made, i * (2 * GT) + GT * r)
                sp.dma_start(gates[:, r], dense[:, :, bass.ds(i * (2 * GT * LOT) + r * (GT * LOT), GT * LOT)]
                             .rearrange("l p k -> p l k")).then_inc(gates_landed[r], 16)
                for j in range(GT):
                    sp.wait_ge(hid_done, i * (2 * GT) + (GT * r + j + 1))
                    sp.dma_start(u_ring[:, j % 4, :], a["u_t"][i * (2 * GT) + (GT * r + j)]).then_inc(u_landed[j % 4], 16)
                sp.wait_ge(sum_done, i * (2 * GT) + (GT * r + GT))
                sp.dma_start(v_ring[:, r], a["v_t"][i * 2 + r].rearrange("j p d -> p j d")).then_inc(v_landed[r], 16)

            with sp.Fori(0, GROUPS // 2) as i:
                load(i, 0)
                load(i, 1)
            sp.dma_start(g_row[:, :], a["ln2_g"].partition_broadcast(P)).then_inc(row_landed, 16)
            sp.dma_start(b_row[:, :], a["ln2_b"].partition_broadcast(P)).then_inc(row_landed, 16)
            for t in range(NT):
                sp.wait_ge(ready, t + 1)
                sp.dma_start(out[0, P * t:P * (t + 1), :], h_tok[:, t, :]).then_inc(stored, 16)
            sp.wait_ge(stored, 16 * NT)

        @block.scalar
        def _(act):
            act.sem_inc(hid_read, 4)
            with act.Fori(0, GROUPS) as i:
                for j in range(GT):
                    act.wait_ge(hid_done, i * GT + (j + 1 + 4))
                    act.wait_ge(coef_made, i * GT + (j - 1 + GT))
                    nc.scalar.activation(act_out[:, j % 2, :], ps[:, j % 4, :], ACT.Gelu).then_inc(hid_read, 1)
            for t in range(NT):
                act.wait_ge(var_ready, t + 1)
                nc.scalar.activation(std[:, t:t + 1], mv[:, t, 1:2], ACT.Sqrt, bias=eps[:, 0:1]).then_inc(std_ready, 1)

        @block.tensor
        def _(pe):
            pe.sem_inc(hid_done, 4)
            pe.sem_inc(sum_done, 2 * GT)

            def hidden(i, r):
                for j in range(GT):
                    pe.wait_ge(u_landed[j % 4], i * 64 + (16 * (2 * r + j // 4) + 16))
                    pe.wait_ge(hid_read, i * (2 * GT) + (GT * r + j + 1))
                    for k in range(KD):
                        last = nc.tensor.matmul(ps[:, j % 4, :], u_ring[:, j % 4, P * k:P * (k + 1)], h1T[:, k, :],
                                                start=(k == 0), stop=(k == KD - 1))
                    last.then_inc(hid_done, 1)

            def sums(i, r):
                pe.wait_ge(coef_made, i * (2 * GT) + (GT * r + GT + GT))
                pe.wait_ge(v_landed[r], i * 16 + 16)
                for b in range(2 * NT):
                    pe.wait_ge(sum_read, i * (4 * NT) + (2 * NT * r + b + 1))
                    for j in range(GT):
                        last = nc.tensor.matmul(ps[:, 4 + b % 4, :], coef[:, r, j, P * (b // 2):P * (b // 2 + 1)],
                                                v_ring[:, r, j, 512 * (b % 2):512 * (b % 2 + 1)],
                                                start=(j == 0), stop=(j == GT - 1))
                    last.then_inc(sum_done, 1)

            hidden(0, 0)
            with pe.Fori(0, GROUPS // 2 - 1) as i:
                hidden(i, 1)
                sums(i, 0)
                hidden(i + 1, 0)
                sums(i, 1)
            hidden(GROUPS // 2 - 1, 1)
            sums(GROUPS // 2 - 1, 0)
            sums(GROUPS // 2 - 1, 1)

        @block.vector
        def _(dve):
            v_ = nc.vector
            order = Order(dve, order_sem)
            put, settle = order.put, order.settle
            dve.sem_inc(coef_made, GT)
            dve.sem_inc(sum_read, 4)
            for t in range(NT):
                v_.tensor_scalar(h_tok[:, t, :], h_tok[:, t, :], ALPHA, None, ALU.mult).then_inc(scaled, 1)

            def weigh(i, r):
                dve.wait_ge(gates_landed[r], i * 16 + 16)
                for j in range(GT):
                    dve.wait_ge(hid_read, i * (2 * GT) + (GT * r + j + 1 + 4))
                    split = lambda x: x.rearrange("p (l n) -> p l n", l=LOTS)
                    v_.tensor_tensor(split(coef[:, r, j, :]), split(act_out[:, j % 2, :]),
                                     gates[:, r, :, LOT * j:LOT * (j + 1)], ALU.mult).then_inc(coef_made, 1)

            def gather(i, r):
                for b in range(2 * NT):
                    dve.wait_ge(sum_done, i * (4 * NT) + (2 * NT * r + b + 1 + 2 * GT))
                    part = h_tok[:, b // 2, 512 * (b % 2):512 * (b % 2 + 1)]
                    v_.tensor_tensor(part, part, ps[:, 4 + b % 4, :], ALU.add).then_inc(sum_read, 1)

            dve.wait_ge(scaled, NT)
            weigh(0, 0)
            with dve.Fori(0, GROUPS // 2 - 1) as i:
                weigh(i, 1)
                gather(i, 0)
                weigh(i + 1, 0)
                gather(i, 1)
            weigh(GROUPS // 2 - 1, 1)
            gather(GROUPS // 2 - 1, 0)
            gather(GROUPS // 2 - 1, 1)
            dve.wait_ge(sum_read, 2 * NT * GROUPS + 4)
            dve.wait_ge(row_landed, 32)
            for t in range(NT):
                for half in range(2):
                    put(v_.bn_stats(stats[:, t, half, :], h_tok[:, t, 512 * half:512 * (half + 1)]))
            settle()
            for t in range(NT):
                v_.bn_aggr(mv[:, t, :], stats[:, t, :, :]).then_inc(var_ready, 1)
            for t in range(NT):
                dve.wait_ge(std_ready, t + 1)
                put(v_.reciprocal(rstd[:, t:t + 1], std[:, t:t + 1]))
                settle()
                put(v_.tensor_scalar(h_tok[:, t, :], h_tok[:, t, :], mv[:, t, 0:1], rstd[:, t:t + 1],
                                     ALU.subtract, ALU.mult))
                settle()
                put(v_.tensor_tensor(h_tok[:, t, :], h_tok[:, t, :], g_row[:, :], ALU.mult))
                settle()
                v_.tensor_tensor(h_tok[:, t, :], h_tok[:, t, :], b_row[:, :], ALU.add).then_inc(ready, 1)


_OUT_SHAPE = (1, SEQ, D)


def lay_out(v):
    w = v["w_in"][0]
    A = HEADS * HD
    at = [0, A, A + KV, 2 * A + KV, 2 * A + KV + HD, 2 * A + KV + HD + HEADS]
    q, ckv, qi, ki, wi = (w[:, at[n]:at[n + 1]] for n in range(5))
    b = w[:, at[5]:at[5] + 3 * A + 256]
    gates = w[:, at[5] + 3 * A + 256:]
    cols = np.concatenate([b, q, ckv, qi, ki, ki, gates], axis=1)

    def by_columns(w):
        return np.ascontiguousarray(w.reshape(KD, P, -1, P).transpose(2, 1, 0, 3).reshape(-1, P, KD * P))

    wi_w = np.ascontiguousarray(wi.reshape(KD, P, HEADS).transpose(1, 0, 2))

    def columns(x):
        return x.reshape(-1, P).T

    twice = lambda x: np.concatenate([x, x])
    named = {"ln_in_g": v["ln_in_g"], "ln_in_b": v["ln_in_b"], "mu": v["b_mu"][0], "b_gate": v["b_gate"][0],
             "kv_g": v["a_kv_norm_g"][0], "ki_g": twice(v["a_kidx_g"][0]), "ki_b": twice(v["a_kidx_b"][0]),
             "w0": v["b_w0"][0], "a0": v["b_a0"][0], "k_k": v["b_k_k"][0], "k_a": v["b_k_a"][0],
             "r_k": v["b_r_k"][0], "lnx_g": v["b_lnx_g"][0], "lnx_b": v["b_lnx_b"][0],
             "ln1_g": v["ln1_g"][0], "ln1_b": v["ln1_b"][0]}
    params = np.ascontiguousarray(np.concatenate([columns(named[n]) for n, _ in PARAMS], axis=1))
    return {"x": v["x"], "meta": v["meta"], "w_in_t": by_columns(cols), "wi_w": wi_w, "params": params,
            "ln_in_g": v["ln_in_g"], "ln_in_b": v["ln_in_b"],
            "w2": v["b_w2"], "a2": v["b_a2"], "g2": v["b_g2"],
            "w_uk": np.ascontiguousarray(v["a_w_uk"][0].reshape(KV, PAIRS, P).transpose(2, 1, 0)),
            "w_pa": v["w_pa"], "w_pb": v["w_pb"], "w_o": v["w_o"], "ln1_g": v["ln1_g"][0], "ln1_b": v["ln1_b"][0],
            "ln2_g": v["ln2_g"][0], "ln2_b": v["ln2_b"][0],
            "wq_t": by_columns(v["peer_wq"][0]), "u_t": by_columns(v["peer_u"][0].T),
            "v_t": v["peer_v"].reshape(EXPERT_KEYS // 8, 8, P, D),
            "sub_keys": np.ascontiguousarray(v["peer_subkeys"][0].reshape(2 * PEER_HEADS, EXPERT_KEYS, P).transpose(2, 0, 1)),
            "w_uv": v["a_w_uv"][0].reshape(KV, HEADS * HD)}


def kernel(**inputs):
    import concourse.bacc as bacc
    from concourse.bass_utils import run_bass_kernel_spmd

    nc = bacc.Bacc("TRN2", target_bir_lowering=False, num_devices=1)
    arrays, args = {}, {}
    for name, x in lay_out({k: np.asarray(x) for k, x in inputs.items()}).items():
        arrays[f"in_{name}"] = np.ascontiguousarray(x)
        args[name] = nc.dram_tensor(f"in_{name}", x.shape, mybir.dt.from_np(x.dtype), kind="ExternalInput").ap()
    out = nc.dram_tensor("out_0", _OUT_SHAPE, F32, kind="ExternalOutput").ap()
    build(nc, args, out)
    return run_bass_kernel_spmd(nc, [arrays], core_ids=[0]).results[0]["out_0"]
```

```python
from contextlib import ExitStack

import numpy as np

import concourse.bass as bass
from concourse import mybir

F32 = mybir.dt.float32
BF16 = mybir.dt.bfloat16
F32R = mybir.dt.float32r
U32 = mybir.dt.uint32
ALU = mybir.AluOpType
ACT = mybir.ActivationFunctionType
AX = mybir.AxisListType

P = 128
D = 1024
KD = D // P
META, SEQ, CHUNK = 16, 512, 64
T = META + SEQ
NT = SEQ // P
HALF = T // 2
LN_EPS, RMS_EPS, KK_EPS, LNX_EPS = EPSILONS = 1e-5, 1e-6, 1e-12, 64e-5
ALPHA = 2.0 ** 0.25
HEADS, HD = 8, 64
PAIRS = HEADS * HD // P
KV = 128
TOPK = min(256, SEQ // 4)
ISCALE = HEADS ** -0.5 * HD ** -0.5
ASCALE = HD ** -0.5
EXPERT_KEYS, PEER_HEADS, PEER_TOPK = 128, 8, 16
LOT = 16
PARKED = 56
MARK, FILL, LOW = -3.4e38, -3.3e38, -1.0e30

CT_R, CT_K, CT_V, CT_WA, CT_G = 0, 4, 8, 12, 13
CT_Q, CT_CKV, CT_QI, CT_KI, CT_GATE = 14, 18, 19, 23, 24
NCT = 40
PW = T + 1

PARAMS = [("ln_in_g", 8), ("ln_in_b", 8), ("mu", 14), ("b_gate", 16), ("kv_g", 1), ("ki_g", 1), ("ki_b", 1),
          ("w0", 4), ("a0", 4), ("k_k", 4), ("k_a", 4), ("r_k", 4), ("lnx_g", 4), ("lnx_b", 4),
          ("ln1_g", 8), ("ln1_b", 8)]
PCOL, _n = {}, 0
for _name, _w in PARAMS:
    PCOL[_name] = _n
    _n += _w
NPARAM = _n

TILES = [(0, META)] + [(META + P * i, P) for i in range(NT)]
WIDTH = [META + P * (i + 1) for i in range(NT)]


class Order:

    def __init__(self, eng, sem):
        self.eng, self.sem, self.n = eng, sem, 0

    def put(self, ins):
        ins.then_inc(self.sem, 1)
        self.n += 1
        return self.n

    def settle(self):
        if self.n:
            self.eng.wait_ge(self.sem, self.n)


def semaphores(nc, ctx, stage):
    made = []

    def sem(name):
        made.append(nc.alloc_semaphore(f"{stage}.{name}"))
        return made[-1]

    def retire():
        nc.clear_and_free_semaphores(made)
        nc.all_engine_barrier()

    ctx.callback(retire)
    return sem


def build(nc, a, out):
    with ExitStack() as ctx:
        def sb(name, shape, dt=F32, at=None):
            return (at or ctx).enter_context(nc.sbuf_tensor(name, shape, dt))

        def semaphore(name, at=None):
            return (at or ctx).enter_context(nc.semaphore(name))

        ps = ctx.enter_context(nc.psum_tensor("ps", [P, 8, 512], F32))
        params = sb("params", [P, NPARAM])
        ident = sb("ident", [P, P])
        ones = sb("ones", [P, P])
        pair_ones = sb("pair_ones", [P, P])
        h_tok = sb("h_tok", [P, NT, D])
        wi_tok = sb("wi_tok", [P, NT, HEADS])
        h1T = sb("h1T", [P, KD, SEQ])[:, :, :]
        eps = sb("eps", [P, 4])

        dense = nc.dram_tensor("dense_gates", [SEQ // LOT, P, P * LOT], F32, kind="Internal").ap()
        parked = nc.dram_tensor("parked_gelu", [PARKED, P, SEQ], F32, kind="Internal").ap()

        def par(name, i=0, rows=P):
            c = PCOL[name] + i
            return params[0:rows, c:c + 1]

        with ExitStack() as layer:
            arena = sb("arena", [P, NCT * PW], at=layer)
            p_all = arena[:, :].rearrange("p (c t) -> p c t", c=NCT)
            out_gate = sb("out_gate", [P, PAIRS, T], at=layer)
            bonus = sb("bonus", [P, PAIRS, T], at=layer)
            chunk_decay = sb("chunk_decay", [P, PAIRS, 1 + SEQ // CHUNK], at=layer)
            attended = sb("attended", [P, PAIRS, SEQ], at=layer)
            project(nc, a, locals())
            attend(nc, a, locals())
            prepare(nc, a, locals())
            scan_chunks(nc, a, locals())
            join(nc, a, locals())
        h_hl = sb("h_hl", [P, 2, KD, SEQ], F32R)
        route(nc, a, locals())
        experts(nc, a, locals(), out)


def project(nc, a, g):
    ps, params, ident, ones, pair_ones = g["ps"], g["params"], g["ident"], g["ones"], g["pair_ones"]
    h_tok, p_all, wi_tok, par, eps = g["h_tok"], g["p_all"], g["wi_tok"], g["par"], g["eps"]
    RING = 4
    with ExitStack() as ctx:
        sb = lambda name, shape: ctx.enter_context(nc.sbuf_tensor(name, shape, F32))
        sem = semaphores(nc, ctx, "project")
        meta_tok = sb("meta_tok", [META, D])
        hT = sb("hT", [P, KD, T])
        w_ring = sb("w_ring", [P, RING, KD * P])
        wi_w = sb("wi_w", [P, KD, HEADS])
        g_row = sb("g_row", [P, D])
        b_row = sb("b_row", [P, D])
        stats = sb("stats", [P, 5, 2, 6])
        mv = sb("mv", [P, 5, 2])
        std = sb("std", [P, 5])
        rstd = sb("rstd", [P, 5])
        x_landed = [sem(f"x_landed{i}") for i in range(5)]
        params_landed, rows_landed, wiw_landed = sem("params_landed"), sem("rows_landed"), sem("wiw_landed")
        w_landed = [sem(f"w_landed{j}") for j in range(RING)]
        consts_made, zeros_made, var_ready, std_ready = sem("consts_made"), sem("zeros_made"), sem("var_ready"), sem("std_ready")
        ln_done, hT_bank, hT_copied_v, hT_copied_s = sem("ln_done"), sem("hT_bank"), sem("hT_copied_v"), sem("hT_copied_s")
        proj_done, proj_copied, wi_done, wi_copied = sem("proj_done"), sem("proj_copied"), sem("wi_done"), sem("wi_copied")
        pool_order, dve_order, hT_read = sem("pool_order"), sem("dve_order"), sem("hT_read")

        eps_made = sem("eps_made")

        def tok(i):
            return meta_tok[:, :] if i == 0 else h_tok[:, i - 1, :]

        block = ctx.enter_context(nc.Block())

        @block.sync
        def _(sp):
            sp.dma_start(meta_tok[:, :], a["meta"]).then_inc(x_landed[0], 16)
            for i in range(NT):
                sp.dma_start(h_tok[:, i, :], a["x"][0, P * i:P * (i + 1), :]).then_inc(x_landed[i + 1], 16)
            sp.dma_start(params[:, :], a["params"]).then_inc(params_landed, 16)
            for j in range(RING):
                sp.dma_start(w_ring[:, j, :], a["w_in_t"][j]).then_inc(w_landed[j], 16)
            sp.dma_start(wi_w[:, :, :], a["wi_w"]).then_inc(wiw_landed, 16)
            sp.dma_start(g_row[:, :], a["ln_in_g"].partition_broadcast(P)).then_inc(rows_landed, 16)
            sp.dma_start(b_row[:, :], a["ln_in_b"].partition_broadcast(P)).then_inc(rows_landed, 16)
            with sp.Fori(1, NCT // RING) as i:
                for j in range(RING):
                    sp.wait_ge(proj_done, i * RING + (j - RING + 1))
                    sp.dma_start(w_ring[:, j, :], a["w_in_t"][i * RING + j]).then_inc(w_landed[j], 16)

        @block.gpsimd
        def _(pool):
            order = Order(pool, pool_order)
            for n, e in enumerate(EPSILONS):
                nc.gpsimd.memset(eps[:, n:n + 1], e).then_inc(eps_made, 1)
            order.put(nc.gpsimd.memset(ident[:, :], 0.0))
            nc.gpsimd.memset(ones[:, :], 1.0).then_inc(consts_made, 1)
            order.settle()
            nc.gpsimd.affine_select(out=ident[:, :], in_=ident[:, :], compare_op=ALU.not_equal, fill=1.0, base=0,
                                    pattern=[[-1, P]], channel_multiplier=1).then_inc(consts_made, 1)
            nc.gpsimd.memset(p_all[:, :, 0:1], 0.0).then_inc(zeros_made, 1)
            pool.wait_ge(rows_landed, 32)
            for i in range(NT):
                pool.wait_ge(hT_read, i + 2)
                order.put(nc.gpsimd.tensor_tensor(h_tok[:, i, :], h_tok[:, i, :], g_row[:, :], ALU.mult))
            order.settle()
            for i in range(NT):
                order.put(nc.gpsimd.tensor_tensor(h_tok[:, i, :], h_tok[:, i, :], b_row[:, :], ALU.add))
            order.settle()

        @block.vector
        def _(dve):
            order = Order(dve, dve_order)
            order.put(nc.vector.memset(pair_ones[:, :], 0.0))
            order.settle()
            for h in range(2):
                order.put(nc.vector.memset(pair_ones[HD * h:HD * (h + 1), HD * h:HD * (h + 1)], 1.0))
            for i, (_, n) in enumerate(TILES):
                dve.wait_ge(x_landed[i], 16)
                for c in range(2):
                    order.put(nc.vector.bn_stats(stats[0:n, i, c, :], tok(i)[:, 512 * c:512 * (c + 1)]))
            order.settle()
            for i, (_, n) in enumerate(TILES):
                nc.vector.bn_aggr(mv[0:n, i, :], stats[0:n, i, :, :]).then_inc(var_ready, 1)
            for i, (_, n) in enumerate(TILES):
                dve.wait_ge(std_ready, i + 1)
                order.put(nc.vector.reciprocal(rstd[0:n, i:i + 1], std[0:n, i:i + 1]))
            order.settle()
            for i, (_, n) in enumerate(TILES):
                nc.vector.tensor_scalar(tok(i), tok(i), mv[0:n, i, 0:1], rstd[0:n, i:i + 1],
                                        ALU.subtract, ALU.mult).then_inc(ln_done, 1)
            dve.wait_ge(params_landed, 16)
            for i, (t0, n) in enumerate(TILES):
                dve.wait_ge(hT_bank, 2 * i + 1)
                for k in range(4):
                    last = nc.vector.tensor_scalar(hT[:, k, t0:t0 + n], ps[:, 2 * (i % 2), P * k:P * k + n],
                                                   par("ln_in_g", k), par("ln_in_b", k), ALU.mult, ALU.add)
                last.then_inc(hT_copied_v, 1)
            dve.wait_ge(wi_done, 1)
            nc.vector.tensor_scalar(wi_tok[:, :, :], ps[:, 4, 0:NT * HEADS].rearrange("p (i h) -> p i h", i=NT),
                                    ISCALE, None, ALU.mult).then_inc(wi_copied, 1)

        @block.scalar
        def _(act):
            act.wait_ge(eps_made, len(EPSILONS))
            for i, (_, n) in enumerate(TILES):
                act.wait_ge(var_ready, i + 1)
                nc.scalar.activation(std[0:n, i:i + 1], mv[0:n, i, 1:2], ACT.Sqrt, bias=eps[0:n, 0:1]
                                     ).then_inc(std_ready, 1)
            act.wait_ge(params_landed, 16)
            for i, (t0, n) in enumerate(TILES):
                act.wait_ge(hT_bank, 2 * i + 2)
                for k in range(4, KD):
                    last = nc.scalar.activation(hT[:, k, t0:t0 + n], ps[:, 2 * (i % 2) + 1, P * (k - 4):P * (k - 4) + n],
                                                ACT.Identity, bias=par("ln_in_b", k), scale=par("ln_in_g", k))
                last.then_inc(hT_copied_s, 1)
            with act.Fori(0, NCT // 2) as i:
                for j in range(2):
                    act.wait_ge(proj_done, i * 2 + (j + 1))
                    nc.scalar.activation(p_all[:, i * 2 + j, 1:PW].rearrange("p (h t) -> p h t", h=2),
                                         ps[:, 4 + 2 * j:6 + 2 * j, 0:HALF], ACT.Copy).then_inc(proj_copied, 1)

        @block.tensor
        def _(pe):
            pe.wait_ge(consts_made, 2)
            for i, (t0, n) in enumerate(TILES):
                pe.wait_ge(ln_done, i + 1)
                if i >= 2:
                    pe.wait_ge(hT_copied_v, i - 1)
                    pe.wait_ge(hT_copied_s, i - 1)
                for k in range(KD):
                    last = nc.tensor.transpose(ps[:, 2 * (i % 2) + k // 4, P * (k % 4):P * (k % 4) + n],
                                               tok(i)[:, P * k:P * (k + 1)], ident[0:n, 0:n])
                    if k == 3:
                        last.then_inc(hT_bank, 1)
                last.then_inc(hT_bank, 1)
                pe.wait_ge(hT_bank, 2 * i + 2)
                pe.sem_inc(hT_read, 1)
            pe.wait_ge(hT_copied_v, len(TILES))
            pe.wait_ge(hT_copied_s, len(TILES))

            def index_weights():
                pe.wait_ge(wiw_landed, 16)
                for i in range(NT):
                    for k in range(KD):
                        last = nc.tensor.matmul(ps[:, 4, HEADS * i:HEADS * (i + 1)],
                                                hT[:, k, META + P * i:META + P * (i + 1)], wi_w[:, k, :],
                                                start=(k == 0), stop=(k == KD - 1))
                last.then_inc(wi_done, 1)
                pe.wait_ge(wi_copied, 1)

            def columns(i, j, first):
                ct = i * RING + j
                pe.wait_ge(w_landed[j], 16 if first else (i + 1) * 16)
                if not first or j >= 2:
                    pe.wait_ge(proj_copied, ct - 1)
                for half in range(2):
                    for k in range(KD):
                        last = nc.tensor.matmul(ps[:, 4 + 2 * (j % 2) + half, 0:HALF], w_ring[:, j, P * k:P * (k + 1)],
                                                hT[:, k, HALF * half:HALF * (half + 1)],
                                                start=(k == 0), stop=(k == KD - 1))
                last.then_inc(proj_done, 1)

            index_weights()
            for j in range(RING):
                columns(0, j, True)
            with pe.Fori(1, NCT // RING) as i:
                for j in range(RING):
                    columns(i, j, False)


def attend(nc, a, g):
    ps, ident, ones, pair_ones = g["ps"], g["ident"], g["ones"], g["pair_ones"]
    p_all, par, eps, wi_tok, attended = g["p_all"], g["par"], g["eps"], g["wi_tok"], g["attended"]
    with ExitStack() as ctx:
        sb = lambda name, shape: ctx.enter_context(nc.sbuf_tensor(name, shape, F32))
        sem = semaphores(nc, ctx, "attend")
        w_uk = sb("w_uk", [P, PAIRS, KV])
        w_uv = sb("w_uv", [P, HEADS * HD])
        cT, c_tok = sb("cT", [P, T]), sb("c_tok", [P, 1 + NT, KV])
        kiT = sb("kiT", [P, T])
        q_abs = sb("q_abs", [P, HEADS, SEQ])
        score = sb("score", [P, T])
        relu = sb("relu", [P, 2, T])
        barred = sb("barred", [P, T])
        best = sb("best", [P, 8])
        prob = sb("prob", [P, HEADS, T])
        peak, low_peak, total, share = (sb(n, [P, HEADS]) for n in ("peak", "low_peak", "total", "share"))
        probT = sb("probT", [P, 1 + NT, 4 * P])
        lat = sb("lat", [P, HEADS, P])
        landed, squares, summed, roots, centred, c_ready, ki_ready = (
            sem(n) for n in ("uk_landed", "c_squares", "c_summed", "c_roots", "centred", "c_ready", "ki_ready"))
        c_turned, c_copied, abs_done, abs_copied = sem("c_turned"), sem("c_copied"), sem("abs_done"), sem("abs_copied")
        logit_done, relu_done, relu_used = sem("logit_done"), sem("relu_done"), sem("relu_used")
        att_done, att_read, exped, shared, scaled = (
            sem(n) for n in ("att_done", "att_read", "exped", "shared", "scaled"))
        turned, turn_copied, lat_done, lat_copied, out_done, out_copied = (
            sem(n) for n in ("p_turned", "p_copied", "lat_done", "lat_copied", "oa_done", "oa_copied"))
        order_sem = sem("dve_order2")
        q, qi = p_all[:, CT_Q:CT_Q + 4, 1 + META:PW], p_all[:, CT_QI:CT_QI + 4, 1 + META:PW]
        ckv, ki = p_all[:, CT_CKV, 1:PW], p_all[:, CT_KI, 1:PW]
        sq, root = prob[:, 0:2, :], prob[:, 2:4, :]
        halves = lambda x: x.rearrange("p (h t) -> p h t", h=2)
        blocks = lambda i: list(enumerate(TILES[:i + 2]))
        turns_before = lambda i: sum(2 * (x + 2) for x in range(i))
        block = ctx.enter_context(nc.Block())

        @block.sync
        def _(sp):
            sp.dma_start(w_uk[:, :, :], a["w_uk"]).then_inc(landed, 16)
            sp.dma_start(w_uv[:, :], a["w_uv"]).then_inc(landed, 16)
            sp.wait_ge(landed, 32)

        @block.scalar
        def _(act):
            act.wait_ge(summed, 1)
            nc.scalar.activation(halves(root[:, 0, :]), ps[:, 0:2, 0:HALF], ACT.Sqrt, bias=eps[:, 1:2],
                                 scale=1.0 / KV).then_inc(roots, 1)
            act.wait_ge(summed, 3)
            nc.scalar.activation(halves(root[:, 1, :]), ps[:, 4:6, 0:HALF], ACT.Sqrt, bias=eps[:, 0:1],
                                 scale=1.0 / HD).then_inc(roots, 1)
            act.wait_ge(c_turned, 1)
            nc.scalar.activation(c_tok[:, 1:1 + NT, :], ps[:, 6, :].rearrange("p (b r) -> p b r", b=NT), ACT.Copy
                                 ).then_inc(c_copied, 1)
            nc.scalar.activation(c_tok[0:META, 0, :], ps[0:META, 7, 0:KV], ACT.Copy).then_inc(c_copied, 1)
            for h in range(HEADS):
                act.wait_ge(abs_done, h + 1)
                nc.scalar.activation(q_abs[:, h, :], ps[:, h % 4, :], ACT.Copy).then_inc(abs_copied, 1)

            def relus(i):
                w = WIDTH[i]
                for h in range(HEADS):
                    n = HEADS * i + h
                    act.wait_ge(logit_done, n + 1)
                    if n >= 2:
                        act.wait_ge(relu_used, n - 1)
                    src = ps[:, 2 * (h % 2):2 * (h % 2) + 2, :].rearrange("p b t -> p (b t)")[:, 0:w]
                    nc.scalar.activation(relu[:, h % 2, 0:w], src, ACT.Relu).then_inc(relu_done, 1)

            relus(0)
            for i in range(NT):
                w = WIDTH[i]
                for h in range(HEADS):
                    act.wait_ge(att_read, HEADS * i + h + 1)
                    nc.scalar.activation(prob[:, h, 0:w], prob[:, h, 0:w], ACT.Exp, bias=low_peak[:, h:h + 1],
                                         accum_out=total[:, h:h + 1]).then_inc(exped, 1)
                    if h:
                        act.wait_ge(shared, HEADS * i + h)
                        nc.scalar.activation(prob[:, h - 1, 0:w], prob[:, h - 1, 0:w], ACT.Copy,
                                             scale=share[:, h - 1:h]).then_inc(scaled, 1)
                act.wait_ge(shared, HEADS * (i + 1))
                nc.scalar.activation(prob[:, HEADS - 1, 0:w], prob[:, HEADS - 1, 0:w], ACT.Copy,
                                     scale=share[:, HEADS - 1:HEADS]).then_inc(scaled, 1)
                if i + 1 < NT:
                    relus(i + 1)
                n = turns_before(i)
                for half in range(2):
                    for b, (_, m) in blocks(i):
                        act.wait_ge(turned, n + 1)
                        if n:
                            act.wait_ge(lat_done, 2 * i + half)
                        nc.scalar.activation(probT[0:m, b, :], ps[0:m, 4 + n % 2, :], ACT.Copy).then_inc(turn_copied, 1)
                        n += 1
                    act.wait_ge(lat_done, 2 * i + half + 1)
                    if i:
                        act.wait_ge(out_done, i)
                    nc.scalar.activation(lat[:, 4 * half:4 * half + 4, :], ps[:, 6, :].rearrange("p (h q) -> p h q", h=4),
                                         ACT.Copy).then_inc(lat_copied, 1)
                act.wait_ge(out_done, i + 1)
                nc.scalar.activation(attended[:, :, P * i:P * (i + 1)], ps[:, 7, :].rearrange("p (j q) -> p j q", j=4),
                                     ACT.Copy).then_inc(out_copied, 1)

        @block.tensor
        def _(pe):
            def sums(weights, src, bank):
                for half in range(2):
                    last = nc.tensor.matmul(ps[:, bank + half, 0:HALF], weights[:, :],
                                            src[:, HALF * half:HALF * (half + 1)], start=True, stop=True)
                last.then_inc(summed, 1)

            pe.wait_ge(squares, 1)
            sums(ones, sq[:, 0, :], 0)
            sums(pair_ones, ki, 2)
            pe.wait_ge(squares, 2)
            sums(pair_ones, sq[:, 1, :], 4)
            pe.wait_ge(c_ready, 1)
            for b, (t0, n) in enumerate(TILES):
                dst = ps[0:n, 7, 0:KV] if b == 0 else ps[0:n, 6, KV * (b - 1):KV * b]
                last = nc.tensor.transpose(dst, cT[:, t0:t0 + n], ident[:, :])
            last.then_inc(c_turned, 1)
            pe.wait_ge(landed, 32)
            pe.wait_ge(roots, 2)
            pe.wait_ge(centred, 1)
            for h in range(HEADS):
                e, j = h % 2, h // 2
                if h >= 4:
                    pe.wait_ge(abs_copied, h - 3)
                rows = slice(HD * e, HD * (e + 1))
                nc.tensor.matmul(ps[:, h % 4, :], w_uk[rows, j, :], q[rows, j, :], start=True, stop=True
                                 ).then_inc(abs_done, 1)

            def pieces(bank, w):
                return [(ps[:, bank, 0:min(w, 512)], 0, min(w, 512))] + ([(ps[:, bank + 1, 0:w - 512], 512, w)] if w > 512 else [])

            def logits(i):
                for h in range(HEADS):
                    n = HEADS * i + h
                    rows = slice(HD * (h % 2), HD * (h % 2 + 1))
                    if n >= 2:
                        pe.wait_ge(relu_done, n - 1)
                    for dst, lo, hi in pieces(2 * (h % 2), WIDTH[i]):
                        last = nc.tensor.matmul(dst, qi[rows, h // 2, P * i:P * (i + 1)], kiT[rows, lo:hi],
                                                start=True, stop=True)
                    last.then_inc(logit_done, 1)

            pe.wait_ge(ki_ready, 1)
            pe.wait_ge(abs_copied, HEADS)
            pe.wait_ge(c_copied, 2)
            logits(0)
            for i in range(NT):
                if i:
                    pe.wait_ge(out_copied, i)
                    pe.wait_ge(lat_copied, 2 * i)
                for h in range(HEADS):
                    n = HEADS * i + h
                    if n >= 2:
                        pe.wait_ge(att_read, n - 1)
                    for dst, lo, hi in pieces(4 + 2 * (h % 2), WIDTH[i]):
                        last = nc.tensor.matmul(dst, q_abs[:, h, P * i:P * (i + 1)], cT[:, lo:hi], start=True, stop=True)
                    last.then_inc(att_done, 1)
                if i + 1 < NT:
                    logits(i + 1)
                pe.wait_ge(att_read, HEADS * (i + 1))
                n = turns_before(i)
                for half in range(2):
                    pe.wait_ge(scaled, HEADS * i + 4 * half + 4)
                    for b, (k0, m) in blocks(i):
                        if n >= 2:
                            pe.wait_ge(turn_copied, n - 1)
                        for h in range(4):
                            last = nc.tensor.transpose(ps[0:m, 4 + n % 2, P * h:P * (h + 1)],
                                                       prob[:, 4 * half + h, k0:k0 + m], ident[:, :])
                        last.then_inc(turned, 1)
                        n += 1
                    pe.wait_ge(turn_copied, n)
                    if half:
                        pe.wait_ge(lat_copied, 2 * i + 1)
                    for b, (k0, m) in blocks(i):
                        last = nc.tensor.matmul(ps[:, 6, :], c_tok[0:m, b, :], probT[0:m, b, :],
                                                start=(b == 0), stop=(b == i + 1))
                    last.then_inc(lat_done, 1)
                pe.wait_ge(lat_copied, 2 * i + 2)
                for h in range(HEADS):
                    e, j = h % 2, h // 2
                    last = nc.tensor.matmul(ps[HD * e:HD * (e + 1), 7, P * j:P * (j + 1)], w_uv[:, HD * h:HD * (h + 1)],
                                            lat[:, h, :], start=True, stop=True)
                last.then_inc(out_done, 1)

        @block.vector
        def _(dve):
            order = Order(dve, order_sem)
            put, settle = order.put, order.settle
            v_ = nc.vector
            v_.tensor_tensor(sq[:, 0, :], ckv, ckv, ALU.mult).then_inc(squares, 1)
            dve.wait_ge(summed, 2)
            put(v_.scalar_tensor_tensor(halves(ki), ps[:, 2:4, 0:HALF], -1.0 / HD, halves(ki), ALU.mult, ALU.add))
            settle()
            v_.tensor_tensor(sq[:, 1, :], ki, ki, ALU.mult).then_inc(squares, 1)
            dve.wait_ge(roots, 1)
            put(v_.reciprocal(root[:, 0, :], root[:, 0, :]))
            settle()
            v_.scalar_tensor_tensor(cT[:, :], ckv, par("kv_g"), root[:, 0, :], ALU.mult, ALU.mult).then_inc(c_ready, 1)
            dve.wait_ge(roots, 2)
            put(v_.reciprocal(root[:, 1, :], root[:, 1, :]))
            settle()
            put(v_.scalar_tensor_tensor(kiT[:, :], ki, par("ki_g"), root[:, 1, :], ALU.mult, ALU.mult))
            settle()
            v_.tensor_scalar(kiT[:, :], kiT[:, :], par("ki_b"), None, ALU.add).then_inc(ki_ready, 1)
            dve.sem_inc(centred, 1)
            for i in range(NT):
                w = WIDTH[i]
                s = score[:, 0:w]
                hidden = slice(w - CHUNK, w)
                for h in range(HEADS):
                    dve.wait_ge(relu_done, HEADS * i + h + 1)
                    weight, src = wi_tok[:, i, h:h + 1], relu[:, h % 2, 0:w]
                    if h == 0:
                        ins = v_.tensor_scalar(s, src, weight, None, ALU.mult)
                    else:
                        dve.wait_ge(relu_used, HEADS * i + h)
                        ins = v_.scalar_tensor_tensor(s, src, weight, s, ALU.mult, ALU.add)
                    ins.then_inc(relu_used, 1)
                dve.wait_ge(relu_used, HEADS * (i + 1))
                put(v_.memset(score[0:HD, hidden], FILL))
                settle()
                for _ in range(TOPK // 8):
                    put(v_.max(best[:, :], s))
                    settle()
                    put(v_.match_replace(s, best[:, :], s, MARK))
                    settle()
                if i:
                    dve.wait_ge(att_read, HEADS * i)
                put(v_.tensor_scalar(barred[:, 0:w], s, MARK, LOW, ALU.not_equal, ALU.mult))
                settle()
                put(v_.memset(barred[0:HD, hidden], LOW))
                settle()
                if i:
                    dve.wait_ge(turned, turns_before(i))
                for h in range(HEADS):
                    dve.wait_ge(att_done, HEADS * i + h + 1)
                    src = ps[:, 4 + 2 * (h % 2):6 + 2 * (h % 2), :].rearrange("p b t -> p (b t)")[:, 0:w]
                    put(v_.tensor_tensor_reduce(prob[:, h, 0:w], src, barred[:, 0:w], ASCALE, FILL, ALU.add, ALU.max,
                                                peak[:, h:h + 1]))
                    settle()
                    v_.tensor_scalar(low_peak[:, h:h + 1], peak[:, h:h + 1], -1.0, None, ALU.mult).then_inc(att_read, 1)
                    if h:
                        dve.wait_ge(exped, HEADS * i + h)
                        v_.reciprocal(share[:, h - 1:h], total[:, h - 1:h]).then_inc(shared, 1)
                dve.wait_ge(exped, HEADS * (i + 1))
                v_.reciprocal(share[:, HEADS - 1:HEADS], total[:, HEADS - 1:HEADS]).then_inc(shared, 1)


def prepare(nc, a, g):
    ps, pair_ones, p_all, par, eps = g["ps"], g["pair_ones"], g["p_all"], g["par"], g["eps"]
    out_gate, bonus, chunk_decay = g["out_gate"], g["bonus"], g["chunk_decay"]
    with ExitStack() as ctx:
        sb = lambda name, shape: ctx.enter_context(nc.sbuf_tensor(name, shape, F32))
        sem = semaphores(nc, ctx, "prepare")
        lora = sb("lora", [P, 512])
        lora_g = sb("lora_g", [P, 512])
        step = sb("step", [P, CT_G + 1, T])
        decay = sb("decay", [P, PAIRS, T])
        rate = sb("rate", [P, PAIRS, T])
        kk = sb("kk", [P, PAIRS, T])
        keep = sb("keep", [P, PAIRS])
        at_start = step[:, 0:4, :]
        norm = step[:, 4:8, :]
        work = step[:, 8:12, :]
        r, k, v = (p_all[:, c:c + 4, 1:PW] for c in (CT_R, CT_K, CT_V))
        wa, gl = p_all[:, CT_WA, 1:PW], p_all[:, CT_G, 1:PW]
        aT, bT = p_all[:, CT_Q:CT_Q + 4, 1:PW], p_all[:, CT_Q + 4:CT_Q + 8, 1:PW]
        landed, shifted, squashed, low_done = sem("lora_landed"), sem("shifted"), sem("squashed"), sem("low_done")
        low_read_s, low_read_v = sem("low_read_s"), sem("low_read_v")
        squares, norms_summed, norms_read = sem("squares"), sem("norms_summed"), sem("norms_read")
        decay_ready, rk_ready, rk_summed, order_sem = sem("decay_ready"), sem("rk_ready"), sem("rk_summed"), sem("dve_order3")
        sig_done = sem("sig_done")
        block = ctx.enter_context(nc.Block())

        @block.sync
        def _(sp):
            sp.dma_start(lora[0:HD, :], a["w2"][0]).then_inc(landed, 16)
            sp.dma_start(lora[HD:P, :], a["a2"][0]).then_inc(landed, 16)
            sp.dma_start(lora_g[:, :], a["g2"][0]).then_inc(landed, 16)
            sp.wait_ge(landed, 48)

        @block.scalar
        def _(act):
            act.wait_ge(shifted, 1)
            nc.scalar.activation(wa[0:HD, :], wa[0:HD, :], ACT.Tanh).then_inc(squashed, 1)
            nc.scalar.activation(gl, gl, ACT.Sigmoid).then_inc(squashed, 1)
            for n in range(8):
                dst, bias = (decay, "w0") if n < 4 else (rate, "a0")
                act.wait_ge(low_done, n + 1)
                b = 2 * (n % 4)
                ins = nc.scalar.activation(dst[:, n % 4, :].rearrange("p (h t) -> p h t", h=2),
                                           ps[:, b:b + 2, 0:HALF], ACT.Sigmoid, bias=par(bias, n % 4))
                ins.then_inc(low_read_s, 1)
            act.wait_ge(low_read_s, 4)
            nc.scalar.activation(decay[:, :, :], decay[:, :, :], ACT.Exp, scale=-float(np.exp(-0.5))).then_inc(decay_ready, 1)
            for c in range(PAIRS):
                act.wait_ge(norms_summed, c + 1)
                nc.scalar.activation(norm[:, c, :].rearrange("p (h t) -> p h t", h=2), ps[:, 2 * c:2 * c + 2, 0:HALF],
                                     ACT.Sqrt, bias=eps[:, 2:3]).then_inc(norms_read, 1)

        @block.tensor
        def _(pe):
            pe.wait_ge(landed, 48)
            pe.wait_ge(squashed, 2)
            for n in range(12):
                b, c = 2 * (n % 4), n % 4
                if 4 <= n < 12:
                    pe.wait_ge(low_read_s, n - 3)
                w, x = ((lora[0:HD, :], wa[0:HD, :]), (lora[HD:P, :], wa[HD:P, :]), (lora_g[:, :], gl))[n // 4]
                for half in range(2):
                    last = nc.tensor.matmul(ps[:, b + half, 0:HALF], w[:, P * c:P * (c + 1)],
                                            x[:, HALF * half:HALF * (half + 1)], start=True, stop=True)
                last.then_inc(low_done, 1)

            def per_head_sums(src, done):
                for c in range(PAIRS):
                    for half in range(2):
                        last = nc.tensor.matmul(ps[:, 2 * c + half, 0:HALF], pair_ones[:, :],
                                                src[:, c, HALF * half:HALF * (half + 1)], start=True, stop=True)
                    last.then_inc(done, 1)

            pe.wait_ge(squares, 1)
            pe.wait_ge(low_read_v, 4)
            per_head_sums(work, norms_summed)
            pe.wait_ge(rk_ready, 1)
            pe.wait_ge(norms_read, PAIRS)
            per_head_sums(work, rk_summed)

        @block.vector
        def _(dve):
            order = Order(dve, order_sem)
            put, settle = order.put, order.settle
            v_ = nc.vector
            put(v_.tensor_tensor(step[:, :, :], p_all[:, 0:CT_G + 1, 0:T], p_all[:, 0:CT_G + 1, 1:PW], ALU.subtract))
            put(v_.tensor_scalar(keep[:, :], g["params"][:, PCOL["k_a"]:PCOL["k_a"] + 4], -1.0, 1.0, ALU.mult, ALU.add))
            settle()
            for c in [CT_WA, CT_G] + list(range(CT_WA)):
                ins = v_.scalar_tensor_tensor(p_all[:, c, 1:PW], step[:, c, :], par("mu", c), p_all[:, c, 1:PW],
                                              ALU.mult, ALU.add)
                put(ins)
                if c == CT_G:
                    settle()
                    dve.sem_inc(shifted, 1)
            settle()
            for c in range(PAIRS):
                put(v_.tensor_scalar(kk[:, c, :], k[:, c, :], par("k_k", c), None, ALU.mult))
            settle()
            v_.tensor_tensor(work, kk[:, :, :], kk[:, :, :], ALU.mult).then_inc(squares, 1)
            for c in range(PAIRS):
                dve.wait_ge(low_done, 9 + c)
                v_.tensor_copy(out_gate[:, c, :].rearrange("p (h t) -> p h t", h=2),
                               ps[:, 2 * c:2 * c + 2, 0:HALF]).then_inc(low_read_v, 1)
            dve.wait_ge(low_read_s, 8)
            dve.wait_ge(norms_summed, PAIRS)
            for c in range(PAIRS):
                put(v_.tensor_scalar(work[:, c, :], rate[:, c, :], par("k_a", c), keep[:, c:c + 1], ALU.mult, ALU.add))
            settle()
            put(v_.tensor_tensor(k, k, work, ALU.mult))
            settle()
            put(v_.tensor_tensor(work, r, k, ALU.mult))
            settle()
            for c in range(PAIRS):
                put(v_.tensor_scalar(work[:, c, :], work[:, c, :], par("r_k", c), None, ALU.mult))
            settle()
            dve.sem_inc(rk_ready, 1)
            put(v_.memset(at_start, 0.0))
            dve.wait_ge(decay_ready, 1)
            settle()
            starts = slice(META, T, CHUNK)
            put(v_.tensor_copy(at_start[:, :, 0:1], decay[:, :, 0:1]))
            put(v_.tensor_copy(at_start[:, :, starts], decay[:, :, starts]))
            settle()
            put(v_.memset(decay[:, :, 0:1], 0.0))
            put(v_.memset(decay[:, :, starts], 0.0))
            settle()
            flat = lambda x: x.rearrange("p c t -> p (c t)")
            put(v_.tensor_tensor_scan(flat(decay[:, :, :]), flat(decay[:, :, :]), flat(at_start), 0.0, ALU.mult, ALU.add))
            dve.wait_ge(norms_read, PAIRS)
            put(v_.reciprocal(norm, norm))
            settle()
            put(v_.tensor_tensor(kk[:, :, :], kk[:, :, :], norm, ALU.mult))
            put(v_.tensor_copy(chunk_decay[:, :, :], decay[:, :, META - 1:T:CHUNK]))
            settle()
            inverse = at_start
            put(v_.reciprocal(inverse, decay[:, :, :]))
            put(v_.tensor_tensor(aT[:, :, 1:T], kk[:, :, 1:T], decay[:, :, 0:T - 1], ALU.mult))
            put(v_.tensor_tensor(norm, kk[:, :, :], rate[:, :, :], ALU.mult))
            put(v_.tensor_tensor(r, r, decay[:, :, :], ALU.mult))
            settle()
            put(v_.tensor_copy(aT[:, :, 0:1], kk[:, :, 0:1]))
            put(v_.tensor_copy(aT[:, :, starts], kk[:, :, starts]))
            put(v_.tensor_tensor(bT, norm, inverse, ALU.mult))
            put(v_.tensor_tensor(k, k, inverse, ALU.mult))
            for c in range(PAIRS):
                dve.wait_ge(rk_summed, c + 1)
                put(v_.tensor_tensor(bonus[:, c, :].rearrange("p (h t) -> p h t", h=2), ps[:, 2 * c:2 * c + 2, 0:HALF],
                                     v[:, c, :].rearrange("p (h t) -> p h t", h=2), ALU.mult))
            settle()


def scan_chunks(nc, a, g):
    ps, ident, ones, pair_ones = g["ps"], g["ident"], g["ones"], g["pair_ones"]
    p_all, par, eps, chunk_decay = g["p_all"], g["par"], g["eps"], g["chunk_decay"]
    with ExitStack() as ctx:
        sb = lambda name, shape: ctx.enter_context(nc.sbuf_tensor(name, shape, F32))
        sem = semaphores(nc, ctx, "scan_chunks")
        below16, above16 = sb("below16", [P, P]), sb("above16", [P, P])
        below32, below64 = sb("below32", [P, P]), sb("below64", [P, P])
        above64, upto64 = sb("above64", [P, P]), sb("upto64", [P, P])
        scratch = g["h1T"].rearrange("p k t -> p (k t)")
        k_hat, b_hat = (scratch[:, 512 * x:512 * (x + 1)].rearrange("p (c t) -> p c t", c=PAIRS) for x in range(2))
        k_tok, b_tok = sb("k_tok", [P, 2, 512]), sb("b_tok", [P, 2, 512])
        v_tok = sb("v_tok", [P, 512])
        grams = {n: sb(n, [P, 2, 4, P]) for n in ("low16", "low32", "low64", "up16", "inv", "rb", "ak", "rk")}
        pw = [sb(f"pw{i}", [P, 2, 4, P]) for i in range(4)]
        x_sb, u_sb = scratch[:, 1024:1536], scratch[:, 1536:2048]
        state = scratch[:, 2048:2048 + 3 * 512].rearrange("p (s c t) -> p s c t", s=3, c=PAIRS)
        faded = scratch[:, 3584:].rearrange("p (c t) -> p c t", c=PAIRS)
        masks_made, tok_zero = sem("masks_made"), sem("tok_zero")
        hats, turned, tok_copied = sem("hats"), sem("turned"), sem("tok_copied")
        gram_done, gram_read = sem("gram_done"), sem("gram_read")
        step_done, step_s, step_v = sem("step_done"), sem("step_s"), sem("step_v")
        x_done, x_read, u_done, u_read, s_done, s_read, y_done, y_read = (
            sem(n) for n in ("x_done", "x_read", "u_done", "u_read", "s_done", "s_read", "y_done", "y_read"))
        order_sem, pool_order, u16_made = sem("dve_order4"), sem("pool_order4"), sem("u16_made")
        kT, rT, vT = (p_all[:, c:c + 4, 1:PW] for c in (CT_K, CT_R, CT_V))
        aT, bT = p_all[:, CT_Q:CT_Q + 4, 1:PW], p_all[:, CT_Q + 4:CT_Q + 8, 1:PW]
        block = ctx.enter_context(nc.Block())

        low16, low32, low64, up16, inv = (grams[n] for n in ("low16", "low32", "low64", "up16", "inv"))
        GRAMS = [(aT, bT, [(low16, below16), (low32, below32), (low64, below64)]),
                 (bT, aT, [(up16, above16)]),
                 (kT, aT, [(grams["ak"], above64)]),
                 (bT, rT, [(grams["rb"], upto64)]),
                 (kT, rT, [(grams["rk"], upto64)])]
        STEPS = [(up16, low16, pw[0], "s", "copy", 0, 0),
                 (low16, up16, pw[1], "s", "copy", 0, 0),
                 (pw[0], inv, inv, "v", "add", 1, 0),
                 (pw[1], pw[0], pw[2], "s", "copy", 2, 0),
                 (pw[0], pw[1], pw[3], "s", "copy", 2, 0),
                 (pw[2], inv, inv, "v", "add", 3, 1),
                 (pw[3], pw[2], pw[0], "s", "copy", 4, 1),
                 (pw[0], inv, inv, "v", "add", 5, 2),
                 (low32, inv, pw[1], "s", "copy", 5, 3),
                 (inv, None, pw[2], "v", "copy", 5, 3),
                 (pw[2], pw[1], inv, "v", "subtract", 6, 4),
                 (low64, inv, pw[3], "s", "copy", 6, 5),
                 (inv, None, pw[0], "v", "copy", 6, 5),
                 (pw[0], pw[3], inv, "v", "subtract", 7, 6)]
        S16 = 8

        def steps_of(tt):
            return STEPS[:S16] if TILES[tt][1] == META else STEPS

        def before(tt, engine):
            return sum(2 * sum(s[3] == engine for s in steps_of(i)) for i in range(tt))

        def chunks_of(tt):
            return [(0, 0, META)] if tt == 0 else [(2 * tt - 1, 0, CHUNK), (2 * tt, CHUNK, CHUNK)]

        @block.gpsimd
        def _(pool):
            order = Order(pool, pool_order)

            def within(dst, w):
                view = dst[:, :].rearrange("p (b w) -> p b w", w=w)
                order.put(nc.gpsimd.affine_select(out=view, in_=ones[:, :].rearrange("p (b w) -> p b w", w=w),
                                                  compare_op=ALU.is_ge, fill=0.0, base=0,
                                                  pattern=[[-w, P // w], [0, w]], channel_multiplier=1))
                order.settle()
                order.put(nc.gpsimd.affine_select(out=view, in_=view, compare_op=ALU.is_ge, fill=0.0, base=w - 1,
                                                  pattern=[[w, P // w], [0, w]], channel_multiplier=-1))

            def side(dst, src, mult, strict):
                return nc.gpsimd.affine_select(out=dst[:, :], in_=src[:, :], compare_op=ALU.is_ge, fill=0.0,
                                               base=-strict, pattern=[[mult, P]], channel_multiplier=-mult)

            within(above16, 16)
            within(above64, 64)
            within(below32, 32)
            order.settle()
            order.put(nc.gpsimd.tensor_tensor(below64[:, :], above64[:, :], below32[:, :], ALU.subtract))
            order.settle()
            order.put(nc.gpsimd.tensor_tensor(below32[:, :], below32[:, :], above16[:, :], ALU.subtract))
            order.put(side(below16, above16, -1, 1))
            order.put(side(upto64, above64, 1, 0))
            order.settle()
            order.put(side(above16, above16, 1, 1))
            order.put(side(above64, above64, 1, 1))
            order.put(side(below32, below32, -1, 1))
            order.put(side(below64, below64, -1, 1))
            order.settle()
            pool.sem_inc(masks_made, 1)

        @block.vector
        def _(dve):
            order = Order(dve, order_sem)
            put, settle = order.put, order.settle
            v_ = nc.vector
            for x in (k_tok, b_tok, state):
                put(v_.memset(x[:, :, :], 0.0))
            put(v_.memset(x_sb[:, :], 0.0))
            put(v_.memset(u_sb[:, :], 0.0))
            put(v_.memset(v_tok[:, :], 0.0))
            settle()
            dve.sem_inc(tok_zero, 1)
            dve.wait_ge(masks_made, 1)
            for tt, (t0, n) in enumerate(TILES):
                if tt:
                    dve.wait_ge(turned, 3 * tt)
                for src, dst in ((kT, k_hat), (bT, b_hat)):
                    for c, p0, m in chunks_of(tt):
                        put(v_.tensor_tensor(dst[:, :, p0:p0 + m], src[:, :, t0 + p0:t0 + p0 + m],
                                             chunk_decay[:, :, c:c + 1].broadcast_to([P, PAIRS, m]), ALU.mult))
                settle()
                dve.sem_inc(hats, 1)
                if tt:
                    dve.wait_ge(y_done, tt)
                for i, (_, _, copies) in enumerate(GRAMS):
                    for e in range(2):
                        dve.wait_ge(gram_done, 10 * tt + 2 * i + e + 1)
                        bank = ps[0:n, (2 * i + e) % 4, :].rearrange("p (j t) -> p j t", j=4)[:, :, 0:n]
                        for dst, mask in copies:
                            put(v_.tensor_tensor(dst[0:n, e, :, 0:n], bank,
                                                 mask[0:n, 0:n].unsqueeze(1).broadcast_to([n, 4, n]), ALU.mult))
                        settle()
                        if i == 1:
                            put(v_.tensor_tensor(inv[0:n, e, :, 0:n], ident[0:n, 0:n].unsqueeze(1).broadcast_to([n, 4, n]),
                                                 up16[0:n, e, :, 0:n], ALU.subtract))
                            settle()
                        dve.sem_inc(gram_read, 1)
                steps = steps_of(tt)
                for i, (_, _, dst, engine, how, _, _) in enumerate(steps):
                    for e in range(2):
                        if engine != "v":
                            continue
                        dve.wait_ge(step_done, 2 * sum(len(steps_of(x)) for x in range(tt)) + 2 * i + e + 1)
                        bank = ps[0:n, 4 + 2 * e + i % 2, :].rearrange("p (j t) -> p j t", j=4)[:, :, 0:n]
                        d = dst[0:n, e, :, 0:n]
                        if how == "copy":
                            v_.tensor_copy(d, bank).then_inc(step_v, 1)
                        else:
                            v_.tensor_tensor(d, d, bank, ALU.add if how == "add" else ALU.subtract).then_inc(step_v, 1)
                for c, p0, m in chunks_of(tt):
                    now, after = state[:, c % 3], state[:, (c + 1) % 3]
                    dve.wait_ge(x_done, c + 1)
                    v_.tensor_copy(x_sb[p0:p0 + m, :], ps[p0:p0 + m, 0, :]).then_inc(x_read, 1)
                    put(v_.tensor_tensor(faded[:, :, :], now[:, :, :],
                                         chunk_decay[:, :, c:c + 1].broadcast_to([P, PAIRS, P]), ALU.mult))
                    settle()
                    dve.wait_ge(s_done, c + 1)
                    for e in range(2):
                        rows = slice(HD * e, HD * (e + 1))
                        put(v_.tensor_tensor(after[rows, :, rows], faded[rows, :, rows],
                                             ps[rows, 2, :].rearrange("p (j v) -> p j v", j=4)[:, :, rows], ALU.add))
                    settle()
                    dve.sem_inc(s_read, 1)

        @block.scalar
        def _(act):
            act.wait_ge(tok_zero, 1)
            for tt, (t0, n) in enumerate(TILES):
                for i, dst in enumerate((k_tok, b_tok, None)):
                    act.wait_ge(turned, 3 * tt + i + 1)
                    if dst is None:
                        nc.scalar.activation(v_tok[0:n, :], ps[0:n, 6, :], ACT.Copy).then_inc(tok_copied, 1)
                        continue
                    for x, (_, p0, m) in enumerate(chunks_of(tt)):
                        last = nc.scalar.activation(dst[p0:p0 + m, x, :], ps[p0:p0 + m, 4 + i, :], ACT.Copy)
                    last.then_inc(tok_copied, 1)
                steps = steps_of(tt)
                for i, (_, _, dst, engine, _, _, _) in enumerate(steps):
                    for e in range(2):
                        if engine != "s":
                            continue
                        act.wait_ge(step_done, 2 * sum(len(steps_of(x)) for x in range(tt)) + 2 * i + e + 1)
                        bank = ps[0:n, 4 + 2 * e + i % 2, :].rearrange("p (j t) -> p j t", j=4)[:, :, 0:n]
                        nc.scalar.activation(dst[0:n, e, :, 0:n], bank, ACT.Copy).then_inc(step_s, 1)
                for c, p0, m in chunks_of(tt):
                    act.wait_ge(u_done, c + 1)
                    nc.scalar.activation(u_sb[p0:p0 + m, :], ps[p0:p0 + m, 1, :], ACT.Copy, scale=-1.0).then_inc(u_read, 1)
                act.wait_ge(y_done, tt + 1)
                nc.scalar.activation(aT[:, :, t0:t0 + n], ps[:, 3, :].rearrange("p (j t) -> p j t", j=4)[:, :, 0:n],
                                     ACT.Copy).then_inc(y_read, 1)

        @block.tensor
        def _(pe):
            for tt, (t0, n) in enumerate(TILES):
                span = slice(t0, t0 + n)
                chunks = chunks_of(tt)
                pe.wait_ge(hats, tt + 1)
                if tt:
                    pe.wait_ge(step_v, before(tt, "v"))
                    pe.wait_ge(step_s, before(tt, "s"))
                for i in range(3):
                    for j in range(PAIRS):
                        src = (k_hat[:, j, 0:n], b_hat[:, j, 0:n], vT[:, j, span])[i]
                        last = nc.tensor.transpose(ps[0:n, 4 + i, P * j:P * (j + 1)], src, ident[:, :])
                    last.then_inc(turned, 1)
                if tt:
                    pe.wait_ge(y_read, tt)
                for i, (lhs, rhs, _) in enumerate(GRAMS):
                    for e in range(2):
                        at = 2 * i + e
                        if at >= 4:
                            pe.wait_ge(gram_read, 10 * tt + at - 3)
                        for j in range(PAIRS):
                            last = nc.tensor.matmul(ps[0:n, at % 4, P * j:P * j + n], lhs[HD * e:HD * (e + 1), j, span],
                                                    rhs[HD * e:HD * (e + 1), j, span], start=True, stop=True)
                        last.then_inc(gram_done, 1)
                pe.wait_ge(tok_copied, 3 * (tt + 1))
                s0, v0 = before(tt, "s"), before(tt, "v")
                for i, (lhs, rhs, _, _, _, need_s, need_v) in enumerate(steps_of(tt)):
                    for e in range(2):
                        if i == 0:
                            pe.wait_ge(gram_read, 10 * tt + 3 + e)
                        if need_s:
                            pe.wait_ge(step_s, s0 + 2 * need_s - 1 + e)
                        if need_v:
                            pe.wait_ge(step_v, v0 + 2 * need_v - 1 + e)
                        if i >= 2:
                            who = steps_of(tt)[i - 2][3]
                            taken = sum(s[3] == who for s in STEPS[:i - 1])
                            pe.wait_ge(step_s if who == "s" else step_v, (s0 if who == "s" else v0) + 2 * taken - 1 + e)
                        for j in range(4):
                            dst = ps[0:n, 4 + 2 * e + i % 2, P * j:P * j + n]
                            if rhs is None:
                                last = nc.tensor.transpose(dst, lhs[0:n, e, j, 0:n], ident[0:n, 0:n])
                            else:
                                last = nc.tensor.matmul(dst, lhs[0:n, e, j, 0:n], rhs[0:n, e, j, 0:n], start=True, stop=True)
                        last.then_inc(step_done, 1)
                pe.wait_ge(gram_read, 10 * (tt + 1))
                pe.wait_ge(step_v, before(tt + 1, "v"))
                for x, (c, p0, m) in enumerate(chunks):
                    rows = slice(p0, p0 + m)
                    now = state[:, c % 3]
                    for e in range(2):
                        for j in range(PAIRS):
                            h = 2 * j + e
                            nc.tensor.matmul(ps[rows, 0, HD * h:HD * (h + 1)], grams["ak"][0:n, e, j, rows],
                                             v_tok[0:n, HD * h:HD * (h + 1)], start=(h == 0), stop=False,
                                             skip_group_check=True)
                    if c:
                        pe.wait_ge(s_read, c)
                    for j in range(PAIRS):
                        last = nc.tensor.matmul(ps[rows, 0, P * j:P * (j + 1)], aT[:, j, t0 + p0:t0 + p0 + m],
                                                now[:, j, :], start=False, stop=(j == PAIRS - 1), skip_group_check=True)
                    last.then_inc(x_done, 1)
                    pe.wait_ge(x_read, c + 1)
                    for e in range(2):
                        for j in range(PAIRS):
                            h = 2 * j + e
                            last = nc.tensor.matmul(ps[rows, 1, HD * h:HD * (h + 1)], inv[0:n, e, j, rows],
                                                    x_sb[0:n, HD * h:HD * (h + 1)], start=True, stop=True)
                    last.then_inc(u_done, 1)
                    for j in range(PAIRS):
                        nc.tensor.matmul(ps[:, 2, P * j:P * (j + 1)], k_tok[0:n, x, P * j:P * (j + 1)],
                                         v_tok[0:n, P * j:P * (j + 1)], start=(j == 0), stop=False, skip_group_check=True)
                    pe.wait_ge(u_read, c + 1)
                    for j in range(PAIRS):
                        last = nc.tensor.matmul(ps[:, 2, P * j:P * (j + 1)], b_tok[0:n, x, P * j:P * (j + 1)],
                                                u_sb[0:n, P * j:P * (j + 1)], start=False, stop=(j == PAIRS - 1),
                                                skip_group_check=True)
                    last.then_inc(s_done, 1)
                for j in range(PAIRS):
                    for name, src in (("rk", v_tok), ("rb", u_sb)):
                        for e in range(2):
                            h = 2 * j + e
                            nc.tensor.matmul(ps[HD * e:HD * (e + 1), 3, P * j:P * j + n], src[0:n, HD * h:HD * (h + 1)],
                                             grams[name][0:n, e, j, 0:n], start=(name == "rk"), stop=False,
                                             skip_group_check=True)
                    for x, (c, p0, m) in enumerate(chunks):
                        last = nc.tensor.matmul(ps[:, 3, P * j + p0:P * j + p0 + m], state[:, c % 3, j, :],
                                                rT[:, j, t0 + p0:t0 + p0 + m], start=False, stop=(x == len(chunks) - 1),
                                                skip_group_check=True)
                last.then_inc(y_done, 1)


def join(nc, a, g):
    ps, ident, pair_ones, h_tok, h1T = g["ps"], g["ident"], g["pair_ones"], g["h_tok"], g["h1T"]
    p_all, par, eps, attended = g["p_all"], g["par"], g["eps"], g["attended"]
    out_gate, bonus = g["out_gate"], g["bonus"]
    with ExitStack() as ctx:
        sb = lambda name, shape: ctx.enter_context(nc.sbuf_tensor(name, shape, F32))
        sem = semaphores(nc, ctx, "join")
        w_pa, w_pb, w_o = sb("w_pa", [P, PAIRS, D]), sb("w_pb", [P, PAIRS, D]), sb("w_o", [P, KD, D])
        stats, mv, std, rstd = sb("stats1", [P, NT, 2, 6]), sb("mv1", [P, NT, 2]), sb("std1", [P, NT]), sb("rstd1", [P, NT])
        flat = g["arena"]
        g_row, b_row = flat[:, KD * SEQ:KD * SEQ + D], flat[:, KD * SEQ + D:KD * SEQ + 2 * D]
        real = slice(1 + META, PW)
        y = p_all[:, CT_Q:CT_Q + 4, real]
        root = p_all[:, CT_Q + 4:CT_Q + 8, real]
        gate = lambda c: p_all[:, CT_GATE + c, real]
        gates_a, gates_b = p_all[:, CT_GATE:CT_GATE + KD, real], p_all[:, CT_GATE + KD:CT_GATE + 2 * KD, real]
        landed = [sem(f"{n}_landed") for n in ("w_pa", "w_pb", "w_o", "row1")]
        sums_done, squares, roots, gated, ob_ready = (
            sem(n) for n in ("y_sums", "y_squares", "y_roots", "gated", "ob_ready"))
        branch_done, branch_read, mixed_ready = sem("branch_done"), sem("branch_read"), sem("mixed_ready")
        wo_done, var_ready, std_ready, ln_done = sem("wo_done"), sem("var1"), sem("std1_ready"), sem("ln1_done")
        wo_read = sem("wo_read")
        turned, copied_v, copied_s, order_sem, pool_order = (
            sem(n) for n in ("h1_turned", "h1_copied_v", "h1_copied_s", "dve_order5", "pool_order5"))
        block = ctx.enter_context(nc.Block())

        @block.sync
        def _(sp):
            for dst, name, s in ((w_pa, "w_pa", landed[0]), (w_pb, "w_pb", landed[1]), (w_o, "w_o", landed[2])):
                sp.dma_start(dst[:, :, :], a[name][0].rearrange("(k p) n -> p k n", p=P)).then_inc(s, 16)
            sp.dma_start(g_row, a["ln1_g"].partition_broadcast(P)).then_inc(landed[3], 16)
            sp.dma_start(b_row, a["ln1_b"].partition_broadcast(P)).then_inc(landed[3], 16)

        @block.scalar
        def _(act):
            for c in range(2 * KD):
                nc.scalar.activation(gate(c), gate(c), ACT.Sigmoid, bias=par("b_gate", c)).then_inc(gated, 1)
            for c in range(PAIRS):
                act.wait_ge(sums_done, PAIRS + c + 1)
                nc.scalar.activation(root[:, c, :], ps[:, c, :], ACT.Sqrt, bias=eps[:, 3:4], scale=1.0 / HD).then_inc(roots, 1)

            def root_of(i):
                act.wait_ge(var_ready, i + 1)
                nc.scalar.activation(std[:, i:i + 1], mv[:, i, 1:2], ACT.Sqrt, bias=eps[:, 0:1]).then_inc(std_ready, 1)

            root_of(0)
            for i in range(NT):
                if i + 1 < NT:
                    root_of(i + 1)
                act.wait_ge(turned, 2 * i + 2)
                for k in range(4, KD):
                    last = nc.scalar.activation(h1T[:, k, P * i:P * (i + 1)], ps[:, 4 + 2 * (i % 2) + 1, P * (k - 4):P * (k - 3)],
                                                ACT.Identity, bias=par("ln1_b", k), scale=par("ln1_g", k))
                last.then_inc(copied_s, 1)

        @block.tensor
        def _(pe):
            def head_sums(src):
                for c in range(PAIRS):
                    nc.tensor.matmul(ps[:, c, :], pair_ones[:, :], src[:, c, :], start=True, stop=True).then_inc(sums_done, 1)

            def branch(w, x, base):
                for c in range(KD):
                    n = base + c
                    if n >= 4:
                        pe.wait_ge(branch_read, n - 3)
                    for k in range(PAIRS):
                        last = nc.tensor.matmul(ps[:, 4 + n % 4, :], w[:, k, P * c:P * (c + 1)], x[:, k, :],
                                                start=(k == 0), stop=(k == PAIRS - 1))
                    last.then_inc(branch_done, 1)

            head_sums(y)
            pe.wait_ge(squares, 1)
            head_sums(root)
            pe.wait_ge(landed[0], 16)
            branch(w_pa, attended, 0)
            pe.wait_ge(landed[1], 16)
            pe.wait_ge(ob_ready, 1)
            branch(w_pb, y, KD)
            pe.wait_ge(landed[2], 16)
            pe.wait_ge(mixed_ready, 1)
            pe.wait_ge(roots, PAIRS)
            for i in range(NT):
                for half in range(2):
                    n = 2 * i + half
                    if n >= 4:
                        pe.wait_ge(wo_read, n - 3)
                    for k in range(KD):
                        last = nc.tensor.matmul(ps[:, n % 4, :], gates_a[:, k, P * i:P * (i + 1)],
                                                w_o[:, k, 512 * half:512 * (half + 1)], start=(k == 0), stop=(k == KD - 1))
                    last.then_inc(wo_done, 1)
            pe.wait_ge(branch_read, 2 * KD)
            for i in range(NT):
                pe.wait_ge(ln_done, i + 1)
                if i >= 2:
                    pe.wait_ge(copied_v, i - 1)
                    pe.wait_ge(copied_s, i - 1)
                for k in range(KD):
                    last = nc.tensor.transpose(ps[:, 4 + 2 * (i % 2) + k // 4, P * (k % 4):P * (k % 4 + 1)],
                                               h_tok[:, i, P * k:P * (k + 1)], ident[:, :])
                    if k % 4 == 3:
                        last.then_inc(turned, 1)

        @block.vector
        def _(dve):
            order = Order(dve, order_sem)
            put, settle = order.put, order.settle
            v_ = nc.vector
            for c in range(PAIRS):
                dve.wait_ge(sums_done, c + 1)
                put(v_.scalar_tensor_tensor(y[:, c, :], ps[:, c, :], -1.0 / HD, y[:, c, :], ALU.mult, ALU.add))
            settle()
            v_.tensor_tensor(root, y, y, ALU.mult).then_inc(squares, 1)
            dve.wait_ge(roots, PAIRS)
            put(v_.reciprocal(root, root))
            settle()
            put(v_.tensor_tensor(y, y, root, ALU.mult))
            settle()
            for c in range(PAIRS):
                put(v_.tensor_scalar(y[:, c, :], y[:, c, :], par("lnx_g", c), par("lnx_b", c), ALU.mult, ALU.add))
            settle()
            put(v_.tensor_tensor(y, y, bonus[:, :, META:T], ALU.add))
            settle()
            v_.tensor_tensor(y, y, out_gate[:, :, META:T], ALU.mult).then_inc(ob_ready, 1)
            for n in range(2 * KD):
                dve.wait_ge(gated, n + 1)
                dve.wait_ge(branch_done, n + 1)
                v_.tensor_tensor(gate(n), ps[:, 4 + n % 4, :], gate(n), ALU.mult).then_inc(branch_read, 1)
            dve.wait_ge(branch_read, 2 * KD)
            v_.tensor_tensor(gates_a, gates_a, gates_b, ALU.add).then_inc(mixed_ready, 1)

            def take_turned(i):
                dve.wait_ge(turned, 2 * i + 1)
                for k in range(4):
                    last = v_.tensor_scalar(h1T[:, k, P * i:P * (i + 1)], ps[:, 4 + 2 * (i % 2), P * k:P * (k + 1)],
                                            par("ln1_g", k), par("ln1_b", k), ALU.mult, ALU.add)
                last.then_inc(copied_v, 1)

            for i in range(NT):
                for half in range(2):
                    dve.wait_ge(wo_done, 2 * i + half + 1)
                    part = h_tok[:, i, 512 * half:512 * (half + 1)]
                    v_.scalar_tensor_tensor(part, part, ALPHA, ps[:, (2 * i + half) % 4, :], ALU.mult, ALU.add
                                            ).then_inc(wo_read, 1)
                dve.wait_ge(wo_read, 2 * i + 2)
                for half in range(2):
                    put(v_.bn_stats(stats[:, i, half, :], h_tok[:, i, 512 * half:512 * (half + 1)]))
                settle()
                v_.bn_aggr(mv[:, i, :], stats[:, i, :, :]).then_inc(var_ready, 1)
                dve.wait_ge(std_ready, i + 1)
                put(v_.reciprocal(rstd[:, i:i + 1], std[:, i:i + 1]))
                settle()
                v_.tensor_scalar(h_tok[:, i, :], h_tok[:, i, :], mv[:, i, 0:1], rstd[:, i:i + 1],
                                 ALU.subtract, ALU.mult).then_inc(ln_done, 1)
                if i:
                    take_turned(i - 1)
            take_turned(NT - 1)

        @block.gpsimd
        def _(pool):
            order = Order(pool, pool_order)
            pool.wait_ge(landed[3], 32)
            for i in range(NT):
                pool.wait_ge(turned, 2 * i + 2)
                order.put(nc.gpsimd.tensor_tensor(h_tok[:, i, :], h_tok[:, i, :], g_row, ALU.mult))
            order.settle()
            for i in range(NT):
                order.put(nc.gpsimd.tensor_tensor(h_tok[:, i, :], h_tok[:, i, :], b_row, ALU.add))
            order.settle()


def route(nc, a, g):
    ps, ident, h1T, h_hl, dense, parked = g["ps"], g["ident"], g["h1T"], g["h_hl"], g["dense"], g["parked"]
    NP = PEER_HEADS * PEER_TOPK
    K = PEER_TOPK
    LOTS = SEQ // LOT
    TILES_OF_HEAD = 4
    DURING_TOPK = PEER_HEADS * TILES_OF_HEAD
    BETWEEN = 8
    LOTS_IN_LOOP = 4
    FOUR = 4
    with ExitStack() as ctx:
        sb = lambda name, shape, dt=F32: ctx.enter_context(nc.sbuf_tensor(name, shape, dt))
        sem = semaphores(nc, ctx, "route")
        staged = sb("w_staged", [P, 4, KD * P])
        w_hl = sb("w_hl", [P, 4, 2, KD * P], F32R)
        free = h1T.rearrange("p k t -> p (k t)")
        hot1 = free[:, 0:4 * FOUR * P].rearrange("p (r n k) -> p r n k", r=4, n=FOUR)
        act_out, qT = (free[:, 2048 + 1024 * x:3072 + 1024 * x].rearrange("p (j t) -> p j t", j=2) for x in range(2))
        sub_keys = sb("sub_keys", [P, 2 * PEER_HEADS, P])
        s_head = sb("s_head", [P, 2, 2, NT, P])
        top = sb("top", [P, 2, NT, K])
        top_at = sb("top_at", [P, 2, NT, K], U32)
        keys = sb("keys", [P, 2, NT, K])
        cand = sb("cand", [P, NT, K * K])
        best = sb("best6", [P, NT, K])
        best_at = sb("best_at", [P, NT, K], U32)
        split_at = sb("split_at", [P, 2, NT, K], U32)
        place = sb("place", [P, 2, NT, K])
        is_place = sb("is_place", [P, 2, NT, K, K])
        picks = sb("picks", [P, 3, NT, NP])
        picksT = sb("picksT", [P, 3, SEQ])
        small = sb("small", [P, NT * PEER_HEADS])
        count16, count128 = sb("count16", [P, K]), sb("count128", [P, P])
        now = sb("now", [P, 3, LOTS_IN_LOOP * LOT])
        hot2 = sb("hot2", [P, 4, FOUR, P], F32R)
        hot1_hl = sb("hot1_hl", [P, 4, 2, FOUR, P], F32R)
        lot = sb("lot", [P, 2, P, LOT])
        landed = [sem(f"w_landed{j}") for j in range(4)]
        h_high, h_low = sem("h_high"), sem("h_low")
        w_high, w_low, tile_done, gelu_made = sem("w_high"), sem("w_low"), sem("tile_done"), sem("gelu_made")
        act_parked = [sem(f"act_parked{j}") for j in range(2)]
        keys_landed, counted = sem("sub_keys_landed"), sem("counted")
        q_copied, s_done, s_copied, topped = (sem(n) for n in ("q_copied", "s_done", "s_copied", "topped"))
        order_sem, softmax_sem, now_ready = sem("dve_order6"), sem("softmax_order"), sem("now_ready")
        lowered, raised, gates_ready, picks_turned, picks_copied = (
            sem(n) for n in ("lowered", "raised", "gates_ready", "picks_turned", "picks_copied"))
        hot_ready, hot_high, hot_low = sem("hot_ready"), sem("hot_high"), sem("hot_low")
        four_done, four_copied = sem("four_done"), sem("four_copied")
        lot_stored = [sem(f"lot_stored{j}") for j in range(2)]
        block = ctx.enter_context(nc.Block())
        LOOPS = LOTS // LOTS_IN_LOOP
        UNTIL_DENSE = DURING_TOPK + BETWEEN
        EXPERTS_BEFORE = UNTIL_DENSE - 2 * PEER_HEADS
        tile_bank = lambda j, is_query: j % 2 if is_query else 2 + j % 2

        @block.sync
        def _(sp):
            def load(s, j):
                sp.dma_start(staged[:, j, :], a["stream"][s]).then_inc(landed[j], 16)

            for j in range(4):
                load(j, j)
            sp.dma_start(sub_keys[:, :, :], a["sub_keys"]).then_inc(keys_landed, 16)
            with sp.Fori(0, UNTIL_DENSE // 8) as i:
                for j in range(8):
                    sp.wait_ge(w_low, i * 8 + (j + 1))
                    load(i * 8 + (j + 4), j % 4)

            def lots(i, last=False):
                for j in range(LOTS_IN_LOOP):
                    if not last:
                        sp.wait_ge(w_low, i * 4 + (UNTIL_DENSE + j + 1))
                        load(i * 4 + (UNTIL_DENSE + j + 4), j)
                    sp.wait_ge(four_copied, i * (4 * LOTS_IN_LOOP) + (4 * j + 4 + 4))
                    sp.dma_start(dense[i * LOTS_IN_LOOP + j], lot[:, j % 2, :, :].rearrange("p k n -> p (k n)")
                                 ).then_inc(lot_stored[j % 2], 16)

            with sp.Fori(0, LOOPS - 1) as i:
                lots(i)
            lots(LOOPS - 1, last=True)
            for j in range(2):
                sp.wait_ge(lot_stored[j], 16 * (LOTS // 2 + 1))
                sp.wait_ge(act_parked[j], 16 * (PARKED // 2 + 1))

        @block.gpsimd
        def _(pool):
            nc.gpsimd.iota(count16[:, :], [[1, K]], 0, 0, allow_small_or_imprecise_dtypes=True).then_inc(counted, 1)
            nc.gpsimd.iota(count128[:, :], [[1, P]], 0, 0, allow_small_or_imprecise_dtypes=True).then_inc(counted, 1)

            def low(s, j):
                pool.wait_ge(w_high, s + 1)
                nc.gpsimd.tensor_tensor(w_hl[:, j % 4, 1, :], staged[:, j % 4, :], w_hl[:, j % 4, 0, :].bitcast(F32),
                                        ALU.subtract).then_inc(w_low, 1)

            def hot_lows(u, q):
                r = q % 4
                pool.wait_ge(hot_high, u + 1)
                nc.gpsimd.tensor_tensor(hot1_hl[:, r, 1], hot1[:, r], hot1_hl[:, r, 0].bitcast(F32),
                                        ALU.subtract).then_inc(hot_low, 1)

            for j in range(3):
                low(j, j)
            with pool.Fori(0, UNTIL_DENSE // 8) as i:
                for j in range(8):
                    low(i * 8 + (j + 3), j + 3)
            for q in range(3):
                hot_lows(q, q)

            def lots(i, last=False):
                for j in range(LOTS_IN_LOOP):
                    for q in range(3, 7):
                        if not (last and j == LOTS_IN_LOOP - 1 and q > 3):
                            hot_lows(i * (4 * LOTS_IN_LOOP) + (4 * j + q), q)
                        if q == 3 and not (last and j >= 1):
                            low(i * 4 + (UNTIL_DENSE + j + 3), j + 3)

            with pool.Fori(0, LOOPS - 1) as i:
                lots(i)
            lots(LOOPS - 1, last=True)

        @block.scalar
        def _(act):
            act.sem_inc(s_copied, 4)
            act.sem_inc(four_copied, 4)
            act.sem_inc(gelu_made, 2)
            act.sem_inc(q_copied, 2)
            for j in range(2):
                act.sem_inc(act_parked[j], 16)
                act.sem_inc(lot_stored[j], 16)
            for k in range(KD):
                nc.scalar.activation(h_hl[:, 0, k, :], h1T[:, k, :], ACT.Copy).then_inc(h_high, 1)

            def high(s, j, landings, free=True):
                act.wait_ge(landed[j % 4], landings * 16)
                if free:
                    act.wait_ge(tile_done, s - 2)
                nc.scalar.activation(w_hl[:, j % 4, 0, :], staged[:, j % 4, :], ACT.Copy).then_inc(w_high, 1)

            def gelu(s, n, j, turn):
                act.wait_ge(tile_done, s + 2)
                act.wait_ge(act_parked[j % 2], turn * 16)
                nc.scalar.activation(act_out[:, j % 2, :], ps[:, tile_bank(j, False), :], ACT.Gelu).then_inc(gelu_made, 1)
                act.wait_ge(gelu_made, n + 3)
                nc.scalar.dma_start(parked[n], act_out[:, j % 2, :]).then_inc(act_parked[j % 2], 16)

            for j in range(3):
                high(j, j, 1, free=False)
            act.wait_ge(h_low, KD)
            with act.Fori(0, PEER_HEADS // 2) as i:
                for r in range(2):
                    for x in range(2):
                        j = 4 * r + x
                        high(i * 8 + (j + 3), j + 3, i * 2 + ((j + 3) // 4 + 1))
                        act.wait_ge(tile_done, i * 8 + (j + 2))
                        nc.scalar.activation(qT[:, x, :], ps[:, tile_bank(j, True), :], ACT.Copy).then_inc(q_copied, 1)
                    j = 4 * r + 2
                    high(i * 8 + (j + 3), j + 3, i * 2 + ((j + 3) // 4 + 1))
                    gelu(i * 8 + j, i * 4 + 2 * r, j, i * 2 + (r + 1))
                    act.wait_ge(topped, i * 2 + (r + 1))
                    for x in range(2):
                        act.wait_ge(s_done, i * 4 + (2 * r + x + 1))
                        nc.scalar.activation(s_head[:, r, x], ps[:, 4 + 2 * r + x, :].rearrange("p (t k) -> p t k", t=NT),
                                             ACT.Copy).then_inc(s_copied, 1)
                    j = 4 * r + 3
                    high(i * 8 + (j + 3), j + 3, i * 2 + ((j + 3) // 4 + 1))
                    gelu(i * 8 + j, i * 4 + (2 * r + 1), j, i * 2 + (r + 1))
            for j in range(BETWEEN):
                high(DURING_TOPK + j + 3, j + 3, (DURING_TOPK + j + 3) // 4 + 1)
                gelu(DURING_TOPK + j, 2 * PEER_HEADS + j, j, PEER_HEADS + j // 2 + 1)
                if j == BETWEEN - 3:
                    act.wait_ge(lowered, 1)
                    nc.scalar.activation(picks[:, 2], picks[:, 2], ACT.Exp).then_inc(raised, 1)

            def hot_highs(u, q):
                act.wait_ge(hot_ready, u + 1)
                nc.scalar.activation(hot1_hl[:, q % 4, 0], hot1[:, q % 4], ACT.Copy).then_inc(hot_high, 1)

            def copy(u, q, j):
                act.wait_ge(four_done, u + (1 + 4))
                nc.scalar.activation(lot[:, j % 2, :, FOUR * q:FOUR * (q + 1)].rearrange("p k n -> p n k"),
                                     ps[:, 4 + q, :].rearrange("p (n k) -> p n k", n=FOUR), ACT.Copy
                                     ).then_inc(four_copied, 1)

            for q in range(3):
                hot_highs(q, q)

            def lots(i, last=False):
                for j in range(LOTS_IN_LOOP):
                    for q in range(4):
                        u = i * (4 * LOTS_IN_LOOP) + (4 * j + q)
                        if not (last and j == LOTS_IN_LOOP - 1 and q):
                            hot_highs(u + 3, q + 3)
                        if q == 0:
                            if not (last and j >= 1):
                                high(i * 4 + (UNTIL_DENSE + j + 3), j + 3, i + ((UNTIL_DENSE + j + 3) // 4 + 1))
                            gelu(i * 4 + (UNTIL_DENSE + j), i * 4 + (EXPERTS_BEFORE + j), j,
                                 i * 2 + ((EXPERTS_BEFORE + j) // 2 + 1))
                            act.wait_ge(lot_stored[j % 2], i * 32 + 16 * (j // 2 + 1))
                        copy(u, q, j)

            with act.Fori(0, LOOPS - 1) as i:
                lots(i)
            lots(LOOPS - 1, last=True)

        @block.tensor
        def _(pe):
            pe.sem_inc(four_done, 4)
            pe.sem_inc(tile_done, 1)

            def tile(s, j, is_query, before):
                pe.wait_ge(w_high, s + 1)
                pe.wait_ge(*before)
                bank = ps[:, tile_bank(j, is_query), :]
                for k in range(KD):
                    for part in range(2):
                        nc.tensor.matmul(bank, w_hl[:, j % 4, 0, P * k:P * (k + 1)], h_hl[:, part, k, :],
                                         start=(k == 0 and part == 0), stop=False)
                pe.wait_ge(w_low, s + 1)
                for k in range(KD):
                    last = nc.tensor.matmul(bank, w_hl[:, j % 4, 1, P * k:P * (k + 1)], h_hl[:, 0, k, :],
                                            start=False, stop=(k == KD - 1))
                last.then_inc(tile_done, 1)

            def scores(i, r):
                for x in range(2):
                    pe.wait_ge(q_copied, i * 4 + (2 * r + x + 3))
                    pe.wait_ge(s_copied, i * 4 + (2 * r + x + 1))
                    for t in range(NT):
                        last = nc.tensor.matmul(ps[:, 4 + 2 * r + x, P * t:P * (t + 1)], qT[:, x, P * t:P * (t + 1)],
                                                sub_keys[:, i * 4 + (2 * r + x), :], start=True, stop=True)
                    last.then_inc(s_done, 1)

            pe.wait_ge(h_high, KD)
            pe.wait_ge(h_low, KD)
            pe.wait_ge(keys_landed, 16)

            with pe.Fori(0, PEER_HEADS // 2) as i:
                for r in range(2):
                    for x in range(2):
                        tile(i * 8 + (4 * r + x), 4 * r + x, True, (q_copied, i * 4 + (2 * r + x + 1)))
                    tile(i * 8 + (4 * r + 2), 2, False, (gelu_made, i * 4 + (2 * r + 1)))
                    scores(i, r)
                    tile(i * 8 + (4 * r + 3), 3, False, (gelu_made, i * 4 + (2 * r + 2)))
            for j in range(BETWEEN):
                tile(DURING_TOPK + j, j, False, (gelu_made, 2 * PEER_HEADS + j + 1))
            pe.wait_ge(s_copied, 2 * PEER_HEADS + 4)
            pe.wait_ge(gates_ready, 1)
            for x in range(3):
                for t in range(NT):
                    last = nc.tensor.transpose(ps[:, 4 + x, P * t:P * (t + 1)], picks[:, x, t, :], ident[:, :])
                last.then_inc(picks_turned, 1)
            pe.wait_ge(picks_copied, 3)

            def four(u, q):
                pe.wait_ge(four_copied, u + 1)
                pe.wait_ge(hot_low, u + 1)
                for n in range(FOUR):
                    for part in range(2):
                        last = nc.tensor.matmul(ps[:, 4 + q, P * n:P * (n + 1)], hot2[:, q, n, :],
                                                hot1_hl[:, q, part, n, :], start=(part == 0), stop=(part == 1))
                last.then_inc(four_done, 1)

            with pe.Fori(0, LOOPS) as i:
                for j in range(LOTS_IN_LOOP):
                    tile(i * 4 + (UNTIL_DENSE + j), j, False, (gelu_made, i * 4 + (EXPERTS_BEFORE + j + 1)))
                    for q in range(4):
                        four(i * (4 * LOTS_IN_LOOP) + (4 * j + q), q)

        @block.vector
        def _(dve):
            v_ = nc.vector
            for k in range(KD):
                dve.wait_ge(h_high, k + 1)
                v_.tensor_tensor(h_hl[:, 1, k, :], h1T[:, k, :], h_hl[:, 0, k, :].bitcast(F32), ALU.subtract).then_inc(h_low, 1)
            dve.sem_inc(topped, 2)
            dve.wait_ge(counted, 2)

            def rank(i, r):
                done = [0]

                def put(ins):
                    ins.then_inc(order_sem, 1)
                    done[0] += 1

                def settle():
                    dve.wait_ge(order_sem, done[0])

                def best_two_rounds(values, out, at, streams):
                    lo, hi = slice(0, 8), slice(8, 16)
                    for x in streams:
                        put(v_.max(out(x)[:, lo], values(x)))
                    settle()
                    for x in streams:
                        put(v_.max_index(at(x)[:, lo], out(x)[:, lo], values(x)))
                    settle()
                    for x in streams:
                        put(v_.match_replace(values(x), out(x)[:, lo], values(x), MARK))
                    settle()
                    for x in streams:
                        put(v_.max(out(x)[:, hi], values(x)))
                    settle()
                    for x in streams:
                        put(v_.max_index(at(x)[:, hi], out(x)[:, hi], values(x)))

                dve.sem_clear(order_sem)
                dve.wait_ge(s_copied, i * 4 + (2 * r + 2 + 4))
                dve.sem_inc(order_sem, 1)
                done[0] += 1
                best_two_rounds(lambda x: s_head[:, r, x // NT, x % NT, :], lambda x: top[:, x // NT, x % NT, :],
                                lambda x: top_at[:, x // NT, x % NT, :], range(2 * NT))
                settle()
                dve.sem_inc(topped, 1)
                put(v_.tensor_copy(keys[:, :], top_at[:, :]))
                put(v_.tensor_tensor(cand[:, :, :].rearrange("p t (x y) -> p t x y", x=K),
                                     top[:, 0].unsqueeze(3).broadcast_to([P, NT, K, K]),
                                     top[:, 1].unsqueeze(2).broadcast_to([P, NT, K, K]), ALU.add))
                settle()
                best_two_rounds(lambda t: cand[:, t, :], lambda t: best[:, t, :], lambda t: best_at[:, t, :], range(NT))
                settle()
                put(v_.tensor_scalar(split_at[:, 0], best_at[:, :], 4, None, ALU.logical_shift_right))
                put(v_.tensor_scalar(split_at[:, 1], best_at[:, :], K - 1, None, ALU.bitwise_and))
                put(v_.tensor_copy(picks[:, 2, :, bass.ds(i * (2 * K) + r * K, K)], best[:, :]))
                settle()
                put(v_.tensor_copy(place[:, :], split_at[:, :]))
                settle()
                for x in range(2):
                    put(v_.tensor_tensor(is_place[:, x].rearrange("p t k j -> p (t k) j"),
                                         place[:, x].rearrange("p t k -> p (t k)").unsqueeze(2).broadcast_to([P, NT * K, K]),
                                         count16[:, :].unsqueeze(1).broadcast_to([P, NT * K, K]), ALU.is_equal))
                settle()
                for x in range(2):
                    put(v_.tensor_tensor(is_place[:, x], is_place[:, x],
                                         keys[:, x].unsqueeze(2).broadcast_to([P, NT, K, K]), ALU.mult))
                settle()
                put(v_.tensor_reduce(picks[:, 0:2, :, bass.ds(i * (2 * K) + r * K, K)], is_place[:, :], AX.X, ALU.add))
                settle()

            with dve.Fori(0, PEER_HEADS // 2) as i:
                rank(i, 0)
                rank(i, 1)
            gate = picks[:, 2].rearrange("p t (h k) -> p (t h) k", h=PEER_HEADS)
            v_.tensor_copy(small[:, :], gate[:, :, 0]).then_inc(softmax_sem, 1)
            dve.wait_ge(softmax_sem, 1)
            wide = small[:, :].unsqueeze(2).broadcast_to([P, NT * PEER_HEADS, K])
            v_.tensor_tensor(gate, gate, wide, ALU.subtract).then_inc(lowered, 1)
            dve.wait_ge(raised, 1)
            v_.tensor_reduce(small[:, :], gate, AX.X, ALU.add).then_inc(softmax_sem, 1)
            dve.wait_ge(softmax_sem, 2)
            v_.reciprocal(small[:, :], small[:, :]).then_inc(softmax_sem, 1)
            dve.wait_ge(softmax_sem, 3)
            v_.tensor_tensor(gate, gate, wide, ALU.mult).then_inc(gates_ready, 1)
            for x in range(3):
                dve.wait_ge(picks_turned, x + 1)
                v_.tensor_copy(picksT[:, x, :], ps[:, 4 + x, :]).then_inc(picks_copied, 1)
            dve.wait_ge(picks_copied, 3)
            with dve.Fori(0, LOOPS) as i:
                v_.tensor_copy(now[:, :, :], picksT[:, :, bass.ds(i * (LOTS_IN_LOOP * LOT), LOTS_IN_LOOP * LOT)]
                               ).then_inc(now_ready, 1)
                dve.wait_ge(now_ready, i + 1)
                for u in range(4 * LOTS_IN_LOOP):
                    dve.wait_ge(four_done, i * (4 * LOTS_IN_LOOP) + (u + 1))
                    for n in range(FOUR):
                        t = FOUR * u + n
                        v_.tensor_scalar(hot1[:, u % 4, n, :], count128[:, :], now[:, 0, t:t + 1],
                                         now[:, 2, t:t + 1], ALU.is_equal, ALU.mult)
                    v_.tensor_tensor(hot2[:, u % 4], count128[:, :].unsqueeze(1).broadcast_to([P, FOUR, P]),
                                     now[:, 1, FOUR * u:FOUR * (u + 1)].unsqueeze(2).broadcast_to([P, FOUR, P]),
                                     ALU.is_equal).then_inc(hot_ready, 1)
                dve.wait_ge(hot_ready, i * (4 * LOTS_IN_LOOP) + 4 * LOTS_IN_LOOP)


def experts(nc, a, g, out):
    ps, h_tok, h_hl, dense, parked, eps = g["ps"], g["h_tok"], g["h_hl"], g["dense"], g["parked"], g["eps"]
    GT = 4
    LOOP = 2 * GT
    LOTS = SEQ // LOT
    FIRST, LOOPS = PARKED // LOOP, EXPERT_KEYS // LOOP
    BANKS = 2 * NT
    STREAM = 2 * PEER_HEADS
    with ExitStack() as ctx:
        sb = lambda name, shape, dt=F32: ctx.enter_context(nc.sbuf_tensor(name, shape, dt))
        sem = semaphores(nc, ctx, "experts")
        u_staged = g["h1T"].rearrange("p k t -> p (k t)").rearrange("p (j w) -> p j w", j=4)
        u_hl = sb("u_hl", [P, 2, 2, KD * P], F32R)
        v_staged = sb("v_staged", [P, 2, D])
        v_hl = sb("v_hl", [P, 2, GT, 2, D], F32R)
        gates = sb("gates", [P, LOTS, LOOP * LOT])
        coef = sb("coef", [P, 2, SEQ])
        coef_hl = sb("coef_hl", [P, 2, GT, 2, SEQ], F32R)
        stats, mv, std, rstd = sb("stats2", [P, NT, 2, 6]), sb("mv2", [P, NT, 2]), sb("std2", [P, NT]), sb("rstd2", [P, NT])
        g_row, b_row = v_staged[:, 0, :], v_staged[:, 1, :]
        u_landed = [sem(f"u_landed{j}") for j in range(4)]
        v_landed, act_landed = [sem(f"v_landed{j}") for j in range(2)], [sem(f"act_landed{j}") for j in range(2)]
        gates_landed = sem("gates_landed")
        u_high, u_low, v_high, v_low, coef_high, coef_low = (
            sem(n) for n in ("u_high", "u_low", "v_high", "v_low", "coef_high", "coef_low"))
        hid_done, gelu_made, weighed, sum_done, sum_read = (
            sem(n) for n in ("hid_done", "gelu_made", "weighed", "sum_done", "sum_read"))
        scaled, order_sem, var_ready, std_ready, row_landed, ready = (
            sem(n) for n in ("h_scaled", "dve_order7", "var2", "std2_ready", "row2_landed", "out_ready"))
        stored = sem("out_stored")
        block = ctx.enter_context(nc.Block())

        fresh = lambda i, j: i * LOOP + (j - PARKED)

        @block.sync
        def _(sp):
            def load_u(i, j, wait=True):
                if wait:
                    sp.wait_ge(u_low, fresh(i, j - 3))
                sp.dma_start(u_staged[:, j % 4, :], a["stream"][i * LOOP + (STREAM + j)]).then_inc(u_landed[j % 4], 16)

            def load_v(i, j):
                sp.wait_ge(v_low, i * LOOP + (j + 1))
                sp.dma_start(v_staged[:, j % 2, :], a["v"][i * LOOP + j]).then_inc(v_landed[j % 2], 16)

            def load_gates(i):
                sp.wait_ge(weighed, i * LOOP + LOOP)
                sp.dma_start(gates[:, :, :], dense[:, :, bass.ds(i * (LOOP * LOT), LOOP * LOT)]
                             .rearrange("l p k -> p l k")).then_inc(gates_landed, 16)

            def load_parked(i, j):
                sp.wait_ge(coef_low, i * LOOP + (j + 1))
                sp.dma_start(coef[:, j % 2, :], parked[i * LOOP + j]).then_inc(act_landed[j % 2], 16)

            load_u(FIRST, 0, wait=False)
            load_u(FIRST, 1, wait=False)
            load_gates(0)
            for j in range(LOOP):
                load_parked(0, j)
                load_v(0, j)
                if j == 1:
                    load_u(FIRST, 2, wait=False)
                    load_u(FIRST, 3, wait=False)
            with sp.Fori(1, FIRST) as i:
                load_gates(i)
                for j in range(LOOP):
                    load_parked(i, j)
                    load_v(i, j)
            load_gates(FIRST)

            def both(i, last=False):
                for j in range(GT):
                    load_u(i, GT + j)
                for j in range(GT):
                    load_v(i, j)
                if not last:
                    for j in range(GT):
                        load_u(i, LOOP + j)
                for j in range(GT):
                    load_v(i, GT + j)
                if not last:
                    load_gates(i + 1)

            with sp.Fori(FIRST, LOOPS - 1) as i:
                both(i)
            both(LOOPS - 1, last=True)
            sp.wait_ge(v_low, EXPERT_KEYS + 2)
            sp.dma_start(g_row, a["ln2_g"].partition_broadcast(P)).then_inc(row_landed, 16)
            sp.dma_start(b_row, a["ln2_b"].partition_broadcast(P)).then_inc(row_landed, 16)
            for t in range(NT):
                sp.wait_ge(ready, t + 1)
                sp.dma_start(out[0, P * t:P * (t + 1), :], h_tok[:, t, :]).then_inc(stored, 16)
            sp.wait_ge(stored, 16 * NT)

        @block.gpsimd
        def _(pool):
            def low(i, j):
                pool.wait_ge(u_high, fresh(i, j + 1))
                nc.gpsimd.tensor_tensor(u_hl[:, j % 2, 1, :], u_staged[:, j % 4, :], u_hl[:, j % 2, 0, :].bitcast(F32),
                                        ALU.subtract).then_inc(u_low, 1)

            low(FIRST, 0)
            low(FIRST, 1)
            with pool.Fori(FIRST, LOOPS - 1) as i:
                for j in range(LOOP):
                    low(i, j + 2)
            for j in range(LOOP - 2):
                low(LOOPS - 1, j + 2)

        @block.scalar
        def _(act):
            def high_u(i, j, free=True):
                act.wait_ge(u_landed[j % 4], i * 32 + (16 * (j // 4 + 1) - 32 * FIRST))
                if free:
                    act.wait_ge(hid_done, fresh(i, j - 1))
                nc.scalar.activation(u_hl[:, j % 2, 0, :], u_staged[:, j % 4, :], ACT.Copy).then_inc(u_high, 1)

            def high_v(i, j):
                act.wait_ge(v_landed[j % 2], i * 64 + (16 * (j // 2) + 16))
                if j % GT == 0:
                    act.wait_ge(sum_done, i * (2 * BANKS) + (BANKS * (j // GT) + BANKS))
                nc.scalar.activation(v_hl[:, j // GT, j % GT, 0, :], v_staged[:, j % 2, :], ACT.Copy).then_inc(v_high, 1)

            def high_coef(i, j):
                act.wait_ge(weighed, i * LOOP + (j + 1 + LOOP))
                nc.scalar.activation(coef_hl[:, j // GT, j % GT, 0, :], coef[:, j % 2, :], ACT.Copy).then_inc(coef_high, 1)

            high_u(FIRST, 0, free=False)
            high_u(FIRST, 1, free=False)
            high_u(FIRST, 2)
            for j in range(LOOP):
                high_v(0, j)
                high_coef(0, j)
                if j == 0:
                    high_u(FIRST, 3)
            with act.Fori(1, FIRST) as i:
                for j in range(LOOP):
                    high_v(i, j)
                    high_coef(i, j)

            def both(i, first=False, last=False):
                for r in range(2):
                    for j in range(GT * r, GT * (r + 1)):
                        if not (last and j >= LOOP - 2) and not (first and j < 2):
                            high_u(i, j + 2)
                        act.wait_ge(hid_done, fresh(i, j + 1))
                        act.wait_ge(coef_low, i * LOOP + (j + 1))
                        nc.scalar.activation(coef[:, j % 2, :], ps[:, j % 4, :], ACT.Gelu).then_inc(gelu_made, 1)
                        high_coef(i, j)
                    for j in range(GT * r, GT * (r + 1)):
                        high_v(i, j)

            both(FIRST, first=True)
            with act.Fori(FIRST + 1, LOOPS - 1) as i:
                both(i)
            both(LOOPS - 1, last=True)
            for t in range(NT):
                act.wait_ge(var_ready, t + 1)
                nc.scalar.activation(std[:, t:t + 1], mv[:, t, 1:2], ACT.Sqrt, bias=eps[:, 0:1]).then_inc(std_ready, 1)

        @block.tensor
        def _(pe):
            pe.sem_inc(sum_done, 2 * BANKS)

            def hidden(i, r, first=False):
                for j in range(GT * r, GT * (r + 1)):
                    pe.wait_ge(u_high, fresh(i, j + 1))
                    if not first:
                        pe.wait_ge(gelu_made, fresh(i, j - 3))
                    bank = ps[:, j % 4, :]
                    for k in range(KD):
                        for part in range(2):
                            nc.tensor.matmul(bank, u_hl[:, j % 2, 0, P * k:P * (k + 1)], h_hl[:, part, k, :],
                                             start=(k == 0 and part == 0), stop=False)
                    pe.wait_ge(u_low, fresh(i, j + 1))
                    for k in range(KD):
                        last = nc.tensor.matmul(bank, u_hl[:, j % 2, 1, P * k:P * (k + 1)], h_hl[:, 0, k, :],
                                                start=False, stop=(k == KD - 1))
                    last.then_inc(hid_done, 1)

            def sums(i, r):
                pe.wait_ge(coef_low, i * LOOP + (GT * r + GT + 2))
                pe.wait_ge(v_low, i * LOOP + (GT * r + GT + 2))
                for b in range(BANKS):
                    pe.wait_ge(sum_read, i * (2 * BANKS) + (BANKS * r + b + 1))
                    for j in range(GT):
                        for n, (c, v) in enumerate(((0, 0), (0, 1), (1, 0))):
                            last = nc.tensor.matmul(ps[:, 4 + b % 4, :], coef_hl[:, r, j, c, P * (b // 2):P * (b // 2 + 1)],
                                                    v_hl[:, r, j, v, 512 * (b % 2):512 * (b % 2 + 1)],
                                                    start=(j == 0 and n == 0), stop=(j == GT - 1 and n == 2))
                    last.then_inc(sum_done, 1)

            hidden(FIRST, 0, first=True)
            with pe.Fori(0, FIRST) as i:
                sums(i, 0)
                sums(i, 1)
            with pe.Fori(FIRST, LOOPS - 1) as i:
                hidden(i, 1)
                sums(i, 0)
                hidden(i + 1, 0)
                sums(i, 1)
            hidden(LOOPS - 1, 1)
            sums(LOOPS - 1, 0)
            sums(LOOPS - 1, 1)

        @block.vector
        def _(dve):
            v_ = nc.vector
            order = Order(dve, order_sem)
            put, settle = order.put, order.settle
            dve.sem_inc(weighed, LOOP)
            dve.sem_inc(coef_low, 2)
            dve.sem_inc(v_low, 2)
            dve.sem_inc(sum_read, 4)
            for t in range(NT):
                v_.tensor_scalar(h_tok[:, t, :], h_tok[:, t, :], ALPHA, None, ALU.mult).then_inc(scaled, 1)

            def weigh(i, j, is_parked):
                if j == 0:
                    dve.wait_ge(gates_landed, i * 16 + 16)
                if is_parked:
                    dve.wait_ge(act_landed[j % 2], i * 64 + (16 * (j // 2) + 16))
                else:
                    dve.wait_ge(gelu_made, fresh(i, j + 1))
                x = coef[:, j % 2, :].rearrange("p (l n) -> p l n", l=LOTS)
                v_.tensor_tensor(x, x, gates[:, :, LOT * j:LOT * (j + 1)], ALU.mult).then_inc(weighed, 1)

            def low_coef(i, j):
                dve.wait_ge(coef_high, i * LOOP + (j + 1))
                v_.tensor_tensor(coef_hl[:, j // GT, j % GT, 1, :], coef[:, j % 2, :],
                                 coef_hl[:, j // GT, j % GT, 0, :].bitcast(F32), ALU.subtract).then_inc(coef_low, 1)

            def low_v(i, j):
                dve.wait_ge(v_high, i * LOOP + (j + 1))
                v_.tensor_tensor(v_hl[:, j // GT, j % GT, 1, :], v_staged[:, j % 2, :],
                                 v_hl[:, j // GT, j % GT, 0, :].bitcast(F32), ALU.subtract).then_inc(v_low, 1)

            def gather(i, j):
                r = j // GT
                for b in range(2 * (j % GT), 2 * (j % GT) + 2):
                    dve.wait_ge(sum_done, i * (2 * BANKS) + (BANKS * r + b + 1 + 2 * BANKS))
                    part = h_tok[:, b // 2, 512 * (b % 2):512 * (b % 2 + 1)]
                    v_.tensor_tensor(part, part, ps[:, 4 + b % 4, :], ALU.add).then_inc(sum_read, 1)

            def parked_tile(i, j, gathered):
                weigh(i, j, True)
                low_v(i, j)
                low_coef(i, j)
                if gathered:
                    gather(*gathered)

            dve.wait_ge(scaled, NT)
            for j in range(LOOP):
                parked_tile(0, j, (0, j - GT) if j >= GT else None)
            with dve.Fori(1, FIRST) as i:
                for j in range(LOOP):
                    parked_tile(i, j, (i, j - GT) if j >= GT else (i - 1, j + GT))

            def both(i):
                for r in range(2):
                    for j in range(GT * r, GT * (r + 1)):
                        weigh(i, j, False)
                        low_coef(i, j)
                    for j in range(GT * r, GT * (r + 1)):
                        low_v(i, j)
                        gather(*((i, j - GT) if r else (i - 1, j + GT)))

            with dve.Fori(FIRST, LOOPS) as i:
                both(i)
            dve.wait_ge(row_landed, 32)

            def normed(t):
                dve.wait_ge(std_ready, t + 1)
                put(v_.reciprocal(rstd[:, t:t + 1], std[:, t:t + 1]))
                settle()
                put(v_.tensor_scalar(h_tok[:, t, :], h_tok[:, t, :], mv[:, t, 0:1], rstd[:, t:t + 1],
                                     ALU.subtract, ALU.mult))
                settle()
                put(v_.tensor_tensor(h_tok[:, t, :], h_tok[:, t, :], g_row, ALU.mult))
                settle()
                v_.tensor_tensor(h_tok[:, t, :], h_tok[:, t, :], b_row, ALU.add).then_inc(ready, 1)

            for t in range(NT):
                gather(LOOPS - 1, GT + t)
                dve.wait_ge(sum_read, BANKS * (EXPERT_KEYS // GT - 1) + 2 * t + 2 + 4)
                for half in range(2):
                    put(v_.bn_stats(stats[:, t, half, :], h_tok[:, t, 512 * half:512 * (half + 1)]))
                settle()
                v_.bn_aggr(mv[:, t, :], stats[:, t, :, :]).then_inc(var_ready, 1)
                if t:
                    normed(t - 1)
            normed(NT - 1)


_OUT_SHAPE = (1, SEQ, D)


def lay_out(v):
    w = v["w_in"][0]
    A = HEADS * HD
    at = [0, A, A + KV, 2 * A + KV, 2 * A + KV + HD, 2 * A + KV + HD + HEADS]
    q, ckv, qi, ki, wi = (w[:, at[n]:at[n + 1]] for n in range(5))
    b = w[:, at[5]:at[5] + 3 * A + 256]
    gates = w[:, at[5] + 3 * A + 256:]
    cols = np.concatenate([b, q, ckv, qi, ki, ki, gates], axis=1)

    def by_columns(w):
        return np.ascontiguousarray(w.reshape(KD, P, -1, P).transpose(2, 1, 0, 3).reshape(-1, P, KD * P))

    wi_w = np.ascontiguousarray(wi.reshape(KD, P, HEADS).transpose(1, 0, 2))

    def columns(x):
        return x.reshape(-1, P).T

    twice = lambda x: np.concatenate([x, x])
    wq, u = by_columns(v["peer_wq"][0]), by_columns(v["peer_u"][0].T)
    order = [t for h in range(PEER_HEADS) for t in (wq[2 * h], wq[2 * h + 1], u[2 * h], u[2 * h + 1])]
    stream = np.concatenate([np.stack(order), u[2 * PEER_HEADS:]])
    named = {"ln_in_g": v["ln_in_g"], "ln_in_b": v["ln_in_b"], "mu": v["b_mu"][0], "b_gate": v["b_gate"][0],
             "kv_g": v["a_kv_norm_g"][0], "ki_g": twice(v["a_kidx_g"][0]), "ki_b": twice(v["a_kidx_b"][0]),
             "w0": v["b_w0"][0], "a0": v["b_a0"][0], "k_k": v["b_k_k"][0], "k_a": v["b_k_a"][0],
             "r_k": v["b_r_k"][0], "lnx_g": v["b_lnx_g"][0], "lnx_b": v["b_lnx_b"][0],
             "ln1_g": v["ln1_g"][0], "ln1_b": v["ln1_b"][0]}
    params = np.ascontiguousarray(np.concatenate([columns(named[n]) for n, _ in PARAMS], axis=1))
    return {"x": v["x"], "meta": v["meta"], "w_in_t": by_columns(cols), "wi_w": wi_w, "params": params,
            "ln_in_g": v["ln_in_g"], "ln_in_b": v["ln_in_b"],
            "w2": v["b_w2"], "a2": v["b_a2"], "g2": v["b_g2"],
            "w_uk": np.ascontiguousarray(v["a_w_uk"][0].reshape(KV, PAIRS, P).transpose(2, 1, 0)),
            "w_pa": v["w_pa"], "w_pb": v["w_pb"], "w_o": v["w_o"], "ln1_g": v["ln1_g"][0], "ln1_b": v["ln1_b"][0],
            "ln2_g": v["ln2_g"][0], "ln2_b": v["ln2_b"][0],
            "stream": stream, "v": v["peer_v"].reshape(EXPERT_KEYS, P, D),
            "sub_keys": np.ascontiguousarray(v["peer_subkeys"][0].reshape(2 * PEER_HEADS, EXPERT_KEYS, P).transpose(2, 0, 1)),
            "w_uv": v["a_w_uv"][0].reshape(KV, HEADS * HD)}


def kernel(**inputs):
    import concourse.bacc as bacc
    from concourse.bass_utils import run_bass_kernel_spmd

    nc = bacc.Bacc("TRN2", target_bir_lowering=False, num_devices=1)
    arrays, args = {}, {}
    for name, x in lay_out({k: np.asarray(x) for k, x in inputs.items()}).items():
        arrays[f"in_{name}"] = np.ascontiguousarray(x)
        args[name] = nc.dram_tensor(f"in_{name}", x.shape, mybir.dt.from_np(x.dtype), kind="ExternalInput").ap()
    out = nc.dram_tensor("out_0", _OUT_SHAPE, F32, kind="ExternalOutput").ap()
    build(nc, args, out)
    return run_bass_kernel_spmd(nc, [arrays], core_ids=[0]).results[0]["out_0"]
```

```python
from contextlib import ExitStack

import numpy as np

import concourse.bass as bass
from concourse import mybir

F32 = mybir.dt.float32
BF16 = mybir.dt.bfloat16
F32R = mybir.dt.float32r
U32 = mybir.dt.uint32
ALU = mybir.AluOpType
ACT = mybir.ActivationFunctionType
AX = mybir.AxisListType

P = 128
D = 1024
KD = D // P
META, SEQ, CHUNK = 16, 512, 64
T = META + SEQ
NT = SEQ // P
HALF = T // 2
LN_EPS, RMS_EPS, KK_EPS, LNX_EPS = EPSILONS = 1e-5, 1e-6, 1e-12, 64e-5
ALPHA = 2.0 ** 0.25
HEADS, HD = 8, 64
PAIRS = HEADS * HD // P
KV = 128
TOPK = min(256, SEQ // 4)
ISCALE = HEADS ** -0.5 * HD ** -0.5
ASCALE = HD ** -0.5
EXPERT_KEYS, PEER_HEADS, PEER_TOPK = 128, 8, 16
LOT = 16
PARKED = 64
MARK, FILL, LOW = -3.4e38, -3.3e38, -1.0e30

CT_QI, CT_KI, CT_CKV = 0, 4, 5
CT_R, CT_K, CT_V, CT_WA, CT_G = 6, 10, 14, 18, 19
CT_Q, CT_GATE = 20, 24
NCT = 40
PARTS = ((0, 0), (0, 1), (1, 0))
PW = T + 1

PARAMS = [("ln_in_g", 8), ("ln_in_b", 8), ("mu", 14), ("b_gate", 16), ("kv_g", 1), ("ki_g", 1), ("ki_b", 1),
          ("w0", 4), ("a0", 4), ("k_k", 4), ("k_a", 4), ("r_k", 4), ("lnx_g", 4), ("lnx_b", 4),
          ("ln1_g", 8), ("ln1_b", 8)]
PCOL, _n = {}, 0
for _name, _w in PARAMS:
    PCOL[_name] = _n
    _n += _w
NPARAM = _n

TILES = [(0, META)] + [(META + P * i, P) for i in range(NT)]
WIDTH = [META + P * (i + 1) for i in range(NT)]


def pieces(ps, bank, w):
    return [(ps[:, bank, 0:min(w, 512)], 0, min(w, 512))] + ([(ps[:, bank + 1, 0:w - 512], 512, w)] if w > 512 else [])


class Order:

    def __init__(self, eng, sem):
        self.eng, self.sem, self.n = eng, sem, 0

    def put(self, ins):
        ins.then_inc(self.sem, 1)
        self.n += 1
        return self.n

    def settle(self):
        if self.n:
            self.eng.wait_ge(self.sem, self.n)


def semaphores(nc, ctx, stage):
    made = []

    def sem(name):
        made.append(nc.alloc_semaphore(f"{stage}.{name}"))
        return made[-1]

    def retire():
        nc.clear_and_free_semaphores(made)
        nc.all_engine_barrier()

    ctx.callback(retire)
    return sem


def build(nc, a, out):
    with ExitStack() as ctx:
        def sb(name, shape, dt=F32, at=None):
            return (at or ctx).enter_context(nc.sbuf_tensor(name, shape, dt))

        def semaphore(name, at=None):
            return (at or ctx).enter_context(nc.semaphore(name))

        ps = ctx.enter_context(nc.psum_tensor("ps", [P, 8, 512], F32))
        params = sb("params", [P, NPARAM])
        ident = sb("ident", [P, P])
        ones = sb("ones", [P, P])
        pair_ones = sb("pair_ones", [P, P])
        h_tok = sb("h_tok", [P, NT, D])
        wi_tok = sb("wi_tok", [P, NT, HEADS])
        h1T = sb("h1T", [P, KD, SEQ])[:, :, :]
        flat_h1T = h1T.rearrange("p k t -> p (k t)")
        barred = [flat_h1T[:, 2 * D + sum(WIDTH[:i]):2 * D + sum(WIDTH[:i + 1])] for i in range(NT)]
        eps = sb("eps", [P, 4])

        dense = nc.dram_tensor("dense_gates", [SEQ // LOT, P, P * LOT], F32, kind="Internal").ap()
        gates_dram = nc.dram_tensor("branch_gates", [2 * KD, P, SEQ], F32, kind="Internal").ap()
        parked = nc.dram_tensor("parked_gelu", [PARKED, P, SEQ], F32, kind="Internal").ap()

        def par(name, i=0, rows=P):
            c = PCOL[name] + i
            return params[0:rows, c:c + 1]

        with ExitStack() as layer:
            arena = sb("arena", [P, CT_GATE * PW], at=layer)
            p_all = arena[:, :].rearrange("p (c t) -> p c t", c=CT_GATE)
            ab = sb("ab", [P, 2 * PAIRS, T], at=layer)
            out_gate = sb("out_gate", [P, PAIRS, T], at=layer)
            bonus = sb("bonus", [P, PAIRS, T], at=layer)
            chunk_decay = sb("chunk_decay", [P, PAIRS, 1 + SEQ // CHUNK], at=layer)
            attended_raw = sb("attended", [P, PAIRS * T], at=layer)[:, :]
            attended = attended_raw[:, 0:PAIRS * SEQ].rearrange("p (c t) -> p c t", c=PAIRS)
            project(nc, a, locals())
            attend(nc, a, locals())
            w_pa = sb("w_pa", [P, PAIRS, D], at=layer)
            scan_chunks(nc, a, locals())
            join(nc, a, locals())
        h_hl = sb("h_hl", [P, 2, KD, SEQ], F32R)
        route(nc, a, locals())
        experts(nc, a, locals(), out)


def project(nc, a, g):
    ps, params, ident, ones, pair_ones = g["ps"], g["params"], g["ident"], g["ones"], g["pair_ones"]
    h_tok, p_all, wi_tok, par, eps = g["h_tok"], g["p_all"], g["wi_tok"], g["par"], g["eps"]
    out_gate, bonus, chunk_decay, ab = g["out_gate"], g["bonus"], g["chunk_decay"], g["ab"]
    gates_dram = g["gates_dram"]
    PAIRS_ALL = NCT // 2
    KEPT = CT_GATE // 2
    INDEX = CT_R // 2
    OPERANDS = (CT_G + 1) // 2
    LOGITS_AFTER = (INDEX + 1, INDEX + 2, INDEX + 3, INDEX + 5)
    with ExitStack() as ctx:
        sb = lambda name, shape, dt=F32: ctx.enter_context(nc.sbuf_tensor(name, shape, dt))
        sem = semaphores(nc, ctx, "project")
        hT_hl = sb("hT_hl", [P, 2, KD, T], F32R)
        w_staged = sb("w_staged0", [P, 2, KD * P])
        w_hl = sb("w_hl0", [P, 2, 2, KD * P], F32R)
        wi_w = sb("wi_w", [P, KD, HEADS])
        wi_hl = sb("wi_hl", [P, 2, KD, HEADS], F32R)
        free = g["h1T"].rearrange("p k t -> p (k t)")
        meta_tok, g_row, b_row = free[0:META, 0:D], free[:, D:2 * D], free[:, 2 * D:3 * D]
        attended_raw = g["attended_raw"]
        whole = [free[:, 3 * D:4 * D].rearrange("p (k t) -> p k t", k=KD),
                 attended_raw[:, 0:D].rearrange("p (k t) -> p k t", k=KD)]
        gate_out = free[:, 0:2 * SEQ].rearrange("p (j t) -> p j t", j=2)
        stats, mv, std, rstd = sb("stats", [P, 5, 2, 6]), sb("mv", [P, 5, 2]), sb("std", [P, 5]), sb("rstd", [P, 5])
        lora = sb("lora", [P, 512])
        lora_g = sb("lora_g", [P, 512])
        decay = sb("decay", [P, PAIRS, T])
        work = sb("work", [P, PAIRS, T])
        keep = sb("keep", [P, PAIRS])
        first_kk = sb("first_kk", [P, PAIRS, 1 + SEQ // CHUNK])
        kk, rate = ab[:, 0:4, :], ab[:, 4:8, :]
        at_start = bonus[:, :, :]
        norm = attended_raw.rearrange("p (c t) -> p c t", c=PAIRS)
        r, k, v = (p_all[:, c:c + 4, 1:PW] for c in (CT_R, CT_K, CT_V))
        wa, gl = p_all[:, CT_WA, 1:PW], p_all[:, CT_G, 1:PW]
        qi = p_all[:, CT_QI:CT_QI + 4, 1 + META:PW]
        ckv, ki = p_all[:, CT_CKV, 1:PW], p_all[:, CT_KI, 1:PW]
        sq, root = work[:, 0:2, :], work[:, 2:4, :]
        relu, score = decay[:, 0:2, :], decay[:, 2, :]
        barred = g["barred"]
        wi_by_head = relu[0:HEADS, 0, 0:SEQ]
        best = sb("best", [P, 8])
        squared, summed, roots, ki_ready = sem("squared"), sem("summed"), sem("roots"), sem("ki_ready")
        logit_done, relu_done, relu_used = sem("logit_done"), sem("relu_done"), sem("relu_used")
        x_landed = [sem(f"x_landed{i}") for i in range(5)]
        params_landed, rows_landed, wiw_landed, lora_landed = (
            sem(n) for n in ("params_landed", "rows_landed", "wiw_landed", "lora_landed"))
        w_landed = [sem(f"w_landed{j}") for j in range(2)]
        consts_made, zeros_made, var_ready, std_ready = sem("consts_made"), sem("zeros_made"), sem("var_ready"), sem("std_ready")
        ln_done, hT_bank, hT_whole_v, hT_whole_s = sem("ln_done"), sem("hT_bank"), sem("hT_whole_v"), sem("hT_whole_s")
        hT_high, hT_low, w_high, w_low, wi_high, wi_low = (
            sem(n) for n in ("hT_high", "hT_low", "w_high", "w_low", "wi_high", "wi_low"))
        tile_done, tile_read, wi_done, wi_copied = sem("tile_done"), sem("tile_read"), sem("wi_done"), sem("wi_copied")
        wi_summed, wi_taken = sem("wi_summed"), sem("wi_taken")
        gate_stored = [sem(f"gate_stored{j}") for j in range(2)]
        pool_order, dve_order, hT_read, eps_made, rows_used = (
            sem(n) for n in ("pool_order", "dve_order", "hT_read", "eps_made", "rows_used"))
        shifted, squashed, low_done, low_read = sem("shifted"), sem("squashed"), sem("low_done"), sem("low_read")
        squares, norms_summed, norms_read = sem("squares"), sem("norms_summed"), sem("norms_read")
        decay_ready, rk_ready, rk_summed, bonus_made = (
            sem(n) for n in ("decay_ready", "rk_ready", "rk_summed", "bonus_made"))

        def tok(i):
            return meta_tok if i == 0 else h_tok[:, i - 1, :]

        in_halves = lambda x: x.rearrange("p (h t) -> p h t", h=2)
        low_banks = lambda n: ps[:, 2 * (n % 2):2 * (n % 2) + 2, 0:HALF]
        block = ctx.enter_context(nc.Block())

        @block.sync
        def _(sp):
            def load(s, j):
                sp.dma_start(w_staged[:, j, :], a["w_in_t"][s]).then_inc(w_landed[j], 16)

            sp.dma_start(meta_tok, a["meta"]).then_inc(x_landed[0], 16)
            for i in range(NT):
                sp.dma_start(h_tok[:, i, :], a["x"][0, P * i:P * (i + 1), :]).then_inc(x_landed[i + 1], 16)
            sp.dma_start(params[:, :], a["params"]).then_inc(params_landed, 16)
            load(0, 0)
            load(1, 1)
            sp.dma_start(wi_w[:, :, :], a["wi_w"]).then_inc(wiw_landed, 16)
            sp.dma_start(g_row, a["ln_in_g"].partition_broadcast(P)).then_inc(rows_landed, 16)
            sp.dma_start(b_row, a["ln_in_b"].partition_broadcast(P)).then_inc(rows_landed, 16)
            sp.dma_start(lora[0:HD, :], a["w2"][0]).then_inc(lora_landed, 16)
            sp.dma_start(lora[HD:P, :], a["a2"][0]).then_inc(lora_landed, 16)
            sp.dma_start(lora_g[:, :], a["g2"][0]).then_inc(lora_landed, 16)
            with sp.Fori(0, PAIRS_ALL - 1) as i:
                for j in range(2):
                    sp.wait_ge(w_low, i * 2 + (j + 1))
                    load(i * 2 + (j + 2), j)
            for j in range(2):
                sp.wait_ge(gate_stored[j], 16 * (PAIRS_ALL - KEPT + 1))

        @block.gpsimd
        def _(pool):
            order = Order(pool, pool_order)
            for n, e in enumerate(EPSILONS):
                nc.gpsimd.memset(eps[:, n:n + 1], e).then_inc(eps_made, 1)
            order.put(nc.gpsimd.memset(ident[:, :], 0.0))
            nc.gpsimd.memset(ones[:, :], 1.0).then_inc(consts_made, 1)
            order.settle()
            nc.gpsimd.affine_select(out=ident[:, :], in_=ident[:, :], compare_op=ALU.not_equal, fill=1.0, base=0,
                                    pattern=[[-1, P]], channel_multiplier=1).then_inc(consts_made, 1)
            nc.gpsimd.memset(p_all[:, :, 0:1], 0.0).then_inc(zeros_made, 1)
            pool.wait_ge(wi_high, 1)
            nc.gpsimd.tensor_tensor(wi_hl[:, 1], wi_w[:, :, :], wi_hl[:, 0].bitcast(F32), ALU.subtract).then_inc(wi_low, 1)

            def low(s, j):
                pool.wait_ge(w_high, s + 1)
                nc.gpsimd.tensor_tensor(w_hl[:, j, 1, :], w_staged[:, j, :], w_hl[:, j, 0, :].bitcast(F32),
                                        ALU.subtract).then_inc(w_low, 1)

            low(0, 0)
            low(1, 1)
            with pool.Fori(1, PAIRS_ALL) as i:
                for j in range(2):
                    low(i * 2 + j, j)

        @block.vector
        def _(dve):
            order = Order(dve, dve_order)
            put, settle = order.put, order.settle
            v_ = nc.vector
            put(v_.memset(pair_ones[:, :], 0.0))
            settle()
            for h in range(2):
                put(v_.memset(pair_ones[HD * h:HD * (h + 1), HD * h:HD * (h + 1)], 1.0))
            for i, (_, n) in enumerate(TILES):
                dve.wait_ge(x_landed[i], 16)
                for c in range(2):
                    put(v_.bn_stats(stats[0:n, i, c, :], tok(i)[:, 512 * c:512 * (c + 1)]))
            settle()
            for i, (_, n) in enumerate(TILES):
                v_.bn_aggr(mv[0:n, i, :], stats[0:n, i, :, :]).then_inc(var_ready, 1)
            for i, (_, n) in enumerate(TILES):
                dve.wait_ge(std_ready, i + 1)
                put(v_.reciprocal(rstd[0:n, i:i + 1], std[0:n, i:i + 1]))
            settle()
            for i, (_, n) in enumerate(TILES):
                v_.tensor_scalar(tok(i), tok(i), mv[0:n, i, 0:1], rstd[0:n, i:i + 1],
                                 ALU.subtract, ALU.mult).then_inc(ln_done, 1)
            dve.wait_ge(params_landed, 16)

            def low_h(i):
                t0, n = TILES[i]
                dve.wait_ge(hT_high, i + 1)
                v_.tensor_tensor(hT_hl[:, 1, :, t0:t0 + n], whole[i % 2][:, :, 0:n],
                                 hT_hl[:, 0, :, t0:t0 + n].bitcast(F32), ALU.subtract).then_inc(hT_low, 1)

            for i, (t0, n) in enumerate(TILES):
                dve.wait_ge(hT_bank, 2 * i + 1)
                if i >= 2:
                    dve.wait_ge(hT_low, i - 1)
                for c in range(4):
                    last = v_.tensor_scalar(whole[i % 2][:, c, 0:n], ps[:, 2 * (i % 2), P * c:P * c + n],
                                            par("ln_in_g", c), par("ln_in_b", c), ALU.mult, ALU.add)
                last.then_inc(hT_whole_v, 1)
                if i:
                    low_h(i - 1)
            low_h(NT)
            dve.wait_ge(rows_landed, 32)
            dve.wait_ge(hT_read, len(TILES))
            for row, op in ((g_row, ALU.mult), (b_row, ALU.add)):
                for i in range(NT):
                    put(v_.tensor_tensor(h_tok[:, i, :], h_tok[:, i, :], row, op))
                settle()
            dve.sem_inc(rows_used, 1)
            dve.wait_ge(wi_done, 1)
            v_.tensor_scalar(wi_tok[:, :, :], ps[:, 0, 0:NT * HEADS].rearrange("p (i h) -> p i h", i=NT),
                             ISCALE, None, ALU.mult).then_inc(wi_copied, 1)
            dve.wait_ge(tile_read, CT_CKV + 1 + 2)
            v_.tensor_tensor(sq[:, 0, :], ckv, ckv, ALU.mult).then_inc(squared, 1)
            dve.wait_ge(summed, 2)
            put(v_.scalar_tensor_tensor(in_halves(ki), ps[:, 2:4, 0:HALF], -1.0 / HD, in_halves(ki), ALU.mult, ALU.add))
            settle()
            v_.tensor_tensor(sq[:, 1, :], ki, ki, ALU.mult).then_inc(squared, 1)
            dve.wait_ge(roots, 1)
            put(v_.reciprocal(root[:, 0, :], root[:, 0, :]))
            settle()
            put(v_.scalar_tensor_tensor(ckv, ckv, par("kv_g"), root[:, 0, :], ALU.mult, ALU.mult))
            dve.wait_ge(roots, 2)
            put(v_.reciprocal(root[:, 1, :], root[:, 1, :]))
            settle()
            put(v_.scalar_tensor_tensor(ki, ki, par("ki_g"), root[:, 1, :], ALU.mult, ALU.mult))
            settle()
            v_.tensor_scalar(ki, ki, par("ki_b"), None, ALU.add).then_inc(ki_ready, 1)
            for i in range(NT):
                w = WIDTH[i]
                s = score[:, 0:w]
                hidden = slice(w - CHUNK, w)
                for h in range(HEADS):
                    dve.wait_ge(relu_done, HEADS * i + h + 1)
                    weight, src = wi_tok[:, i, h:h + 1], relu[:, h % 2, 0:w]
                    if h == 0:
                        ins = v_.tensor_scalar(s, src, weight, None, ALU.mult)
                    else:
                        dve.wait_ge(relu_used, HEADS * i + h)
                        ins = v_.scalar_tensor_tensor(s, src, weight, s, ALU.mult, ALU.add)
                    ins.then_inc(relu_used, 1)
                dve.wait_ge(relu_used, HEADS * (i + 1))
                put(v_.memset(s[0:HD, hidden], FILL))
                settle()
                for _ in range(TOPK // 8):
                    put(v_.max(best[:, :], s))
                    settle()
                    put(v_.match_replace(s, best[:, :], s, MARK))
                    settle()
                put(v_.tensor_scalar(barred[i], s, MARK, LOW, ALU.not_equal, ALU.mult))
                settle()
                put(v_.memset(barred[i][0:HD, hidden], LOW))
                settle()
            dve.wait_ge(zeros_made, 1)
            dve.wait_ge(tile_read, CT_G + 1 + 2)
            put(v_.tensor_scalar(keep[:, :], params[:, PCOL["k_a"]:PCOL["k_a"] + 4], -1.0, 1.0, ALU.mult, ALU.add))
            for c0, n, step in ((CT_WA, 2, decay), (CT_K, 4, work), (CT_R, 4, work), (CT_V, 4, work)):
                put(v_.tensor_tensor(step[:, 0:n, :], p_all[:, c0:c0 + n, 0:T], p_all[:, c0:c0 + n, 1:PW], ALU.subtract))
                settle()
                for c in range(n):
                    put(v_.scalar_tensor_tensor(p_all[:, c0 + c, 1:PW], step[:, c, :], par("mu", c0 + c - CT_R),
                                                p_all[:, c0 + c, 1:PW], ALU.mult, ALU.add))
                settle()
                if c0 == CT_WA:
                    dve.sem_inc(shifted, 1)
            for c in range(PAIRS):
                put(v_.tensor_scalar(kk[:, c, :], k[:, c, :], par("k_k", c), None, ALU.mult))
            settle()
            v_.tensor_tensor(work[:, :, :], kk, kk, ALU.mult).then_inc(squares, 1)
            put(v_.memset(at_start, 0.0))
            dve.wait_ge(decay_ready, 1)
            settle()
            starts = slice(META, T, CHUNK)
            put(v_.tensor_copy(at_start[:, :, 0:1], decay[:, :, 0:1]))
            put(v_.tensor_copy(at_start[:, :, starts], decay[:, :, starts]))
            settle()
            put(v_.memset(decay[:, :, 0:1], 0.0))
            put(v_.memset(decay[:, :, starts], 0.0))
            settle()
            flat = lambda x: x.rearrange("p c t -> p (c t)")
            put(v_.tensor_tensor_scan(flat(decay[:, :, :]), flat(decay[:, :, :]), flat(at_start), 0.0, ALU.mult, ALU.add))
            settle()
            put(v_.tensor_copy(chunk_decay[:, :, :], decay[:, :, META - 1:T:CHUNK]))
            inverse = at_start
            put(v_.reciprocal(inverse, decay[:, :, :]))
            dve.wait_ge(low_read, 8)
            dve.wait_ge(norms_summed, PAIRS)
            for c in range(PAIRS):
                put(v_.tensor_scalar(work[:, c, :], rate[:, c, :], par("k_a", c), keep[:, c:c + 1], ALU.mult, ALU.add))
            settle()
            put(v_.tensor_tensor(k, k, work[:, :, :], ALU.mult))
            settle()
            put(v_.tensor_tensor(work[:, :, :], r, k, ALU.mult))
            settle()
            for c in range(PAIRS):
                put(v_.tensor_scalar(work[:, c, :], work[:, c, :], par("r_k", c), None, ALU.mult))
            settle()
            dve.sem_inc(rk_ready, 1)
            dve.wait_ge(norms_read, PAIRS)
            put(v_.reciprocal(norm, norm))
            settle()
            put(v_.tensor_tensor(kk, kk, norm, ALU.mult))
            put(v_.tensor_tensor(r, r, decay[:, :, :], ALU.mult))
            put(v_.tensor_tensor(k, k, inverse, ALU.mult))
            settle()
            put(v_.tensor_tensor(rate, rate, kk, ALU.mult))
            put(v_.tensor_copy(first_kk[:, :, 0:1], kk[:, :, 0:1]))
            put(v_.tensor_copy(first_kk[:, :, 1:], kk[:, :, starts]))
            settle()
            put(v_.tensor_tensor(rate, rate, inverse, ALU.mult))
            put(v_.tensor_tensor(kk[:, :, 1:T], kk[:, :, 1:T], decay[:, :, 0:T - 1], ALU.mult))
            settle()
            put(v_.tensor_copy(kk[:, :, starts], first_kk[:, :, 1:]))
            for c in range(PAIRS):
                dve.wait_ge(rk_summed, c + 1)
                v_.tensor_tensor(in_halves(bonus[:, c, :]), low_banks(c), in_halves(v[:, c, :]), ALU.mult).then_inc(bonus_made, 1)

        @block.scalar
        def _(act):
            def high(s, j, landings, free=True):
                act.wait_ge(w_landed[j], landings * 16)
                if free:
                    act.wait_ge(tile_done, s - 1)
                nc.scalar.activation(w_hl[:, j, 0, :], w_staged[:, j, :], ACT.Copy).then_inc(w_high, 1)

            act.sem_inc(tile_read, 2)
            act.wait_ge(eps_made, len(EPSILONS))
            for i, (_, n) in enumerate(TILES):
                act.wait_ge(var_ready, i + 1)
                nc.scalar.activation(std[0:n, i:i + 1], mv[0:n, i, 1:2], ACT.Sqrt, bias=eps[0:n, 0:1]
                                     ).then_inc(std_ready, 1)
            high(0, 0, 1, free=False)
            high(1, 1, 1, free=False)
            act.wait_ge(wiw_landed, 16)
            nc.scalar.activation(wi_hl[:, 0], wi_w[:, :, :], ACT.Copy).then_inc(wi_high, 1)
            act.wait_ge(params_landed, 16)

            def high_h(i):
                t0, n = TILES[i]
                act.wait_ge(hT_whole_v, i + 1)
                act.wait_ge(hT_whole_s, i + 1)
                nc.scalar.activation(hT_hl[:, 0, :, t0:t0 + n], whole[i % 2][:, :, 0:n], ACT.Copy).then_inc(hT_high, 1)

            for i, (t0, n) in enumerate(TILES):
                act.wait_ge(hT_bank, 2 * i + 2)
                if i >= 2:
                    act.wait_ge(hT_low, i - 1)
                for c in range(4, KD):
                    last = nc.scalar.activation(whole[i % 2][:, c, 0:n], ps[:, 2 * (i % 2) + 1, P * (c - 4):P * (c - 4) + n],
                                                ACT.Identity, bias=par("ln_in_b", c), scale=par("ln_in_g", c))
                last.then_inc(hT_whole_s, 1)
                high_h(i)

            def pair(i, with_next=True):
                for j in range(2):
                    if with_next:
                        high(i * 2 + (j + 2), j, i + 2)
                    act.wait_ge(tile_done, i * 2 + (j + 1))
                    nc.scalar.activation(in_halves(p_all[:, i * 2 + j, 1:PW]), ps[:, 4 + 2 * j:6 + 2 * j, 0:HALF], ACT.Copy
                                         ).then_inc(tile_read, 1)

            def gate_pair(i, with_next=True):
                for j in range(2):
                    if with_next:
                        high(i * 2 + (j + 2), j, i + 2)
                    c = i * 2 + (j - CT_GATE)
                    column = PCOL["b_gate"] + c
                    act.wait_ge(tile_done, i * 2 + (j + 1))
                    act.wait_ge(gate_stored[j], i * 16 + 16 * (1 - KEPT))
                    nc.scalar.activation(gate_out[:, j, :], ps[:, 4 + 2 * j, :], ACT.Sigmoid,
                                         bias=params[:, column:column + 1] if isinstance(i, int) else params[:, bass.ds(column, 1)]
                                         ).then_inc(tile_read, 1)
                    act.wait_ge(tile_read, i * 2 + (j + 1 + 2))
                    nc.scalar.dma_start(gates_dram[c], gate_out[:, j, :]).then_inc(gate_stored[j], 16)

            def lows(first, last):
                for n in range(first, last):
                    act.wait_ge(low_done, n + 1)
                    c = n % 4
                    if n < 8:
                        dst, bias = (decay, "w0") if n < 4 else (rate, "a0")
                        nc.scalar.activation(in_halves(dst[:, c, :]), low_banks(n), ACT.Sigmoid, bias=par(bias, c)
                                             ).then_inc(low_read, 1)
                    else:
                        nc.scalar.activation(in_halves(out_gate[:, c, :]), low_banks(n), ACT.Copy).then_inc(low_read, 1)

            def root_of(n, bank, scale, e):
                act.wait_ge(summed, (1, 3)[n])
                nc.scalar.activation(in_halves(root[:, n, :]), ps[:, bank:bank + 2, 0:HALF], ACT.Sqrt, bias=eps[:, e:e + 1],
                                     scale=scale).then_inc(roots, 1)

            def relus(i):
                w = WIDTH[i]
                for h in range(HEADS):
                    n = HEADS * i + h
                    act.wait_ge(logit_done, n + 1)
                    if n >= 2:
                        act.wait_ge(relu_used, n - 1)
                    src = ps[:, 2 * (h % 2):2 * (h % 2) + 2, :].rearrange("p b t -> p (b t)")[:, 0:w]
                    nc.scalar.activation(relu[:, h % 2, 0:w], src, ACT.Relu).then_inc(relu_done, 1)

            act.wait_ge(wi_summed, 1)
            nc.scalar.activation(wi_by_head, ps[0:HEADS, 0, :], ACT.Copy).then_inc(wi_taken, 1)
            with act.Fori(0, INDEX) as i:
                pair(i)
            root_of(0, 0, 1.0 / KV, 1)
            pair(INDEX)
            root_of(1, 0, 1.0 / HD, 0)
            for i in range(INDEX + 1, OPERANDS):
                pair(i)
                if i in LOGITS_AFTER:
                    relus(LOGITS_AFTER.index(i))
            pair(OPERANDS)
            act.wait_ge(shifted, 1)
            nc.scalar.activation(wa[0:HD, :], wa[0:HD, :], ACT.Tanh).then_inc(squashed, 1)
            nc.scalar.activation(gl, gl, ACT.Sigmoid).then_inc(squashed, 1)
            pair(OPERANDS + 1)
            lows(0, 4)
            act.wait_ge(low_read, 4)
            nc.scalar.activation(decay[:, :, :], decay[:, :, :], ACT.Exp, scale=-float(np.exp(-0.5))).then_inc(decay_ready, 1)
            act.wait_ge(rows_used, 1)
            for j in range(2):
                act.sem_inc(gate_stored[j], 16)
            gate_pair(KEPT)
            lows(4, 8)
            gate_pair(KEPT + 1)
            lows(8, 12)
            for c in range(PAIRS):
                act.wait_ge(norms_summed, c + 1)
                nc.scalar.activation(in_halves(norm[:, c, :]), low_banks(c), ACT.Sqrt, bias=eps[:, 2:3]).then_inc(norms_read, 1)
            with act.Fori(KEPT + 2, PAIRS_ALL - 1) as i:
                gate_pair(i)
            gate_pair(PAIRS_ALL - 1, with_next=False)

        @block.tensor
        def _(pe):
            pe.wait_ge(consts_made, 2)
            for i, (t0, n) in enumerate(TILES):
                pe.wait_ge(ln_done, i + 1)
                if i >= 2:
                    pe.wait_ge(hT_whole_v, i - 1)
                    pe.wait_ge(hT_whole_s, i - 1)
                for k in range(KD):
                    last = nc.tensor.transpose(ps[:, 2 * (i % 2) + k // 4, P * (k % 4):P * (k % 4) + n],
                                               tok(i)[:, P * k:P * (k + 1)], ident[0:n, 0:n])
                    if k == 3:
                        last.then_inc(hT_bank, 1)
                last.then_inc(hT_bank, 1)
                pe.wait_ge(hT_bank, 2 * i + 2)
                pe.sem_inc(hT_read, 1)
            pe.wait_ge(hT_low, len(TILES))

            pe.wait_ge(wi_low, 1)
            for k in range(KD):
                for n, (x, y) in enumerate(PARTS):
                    last = nc.tensor.matmul(ps[0:HEADS, 0, :], wi_hl[:, x, k, :], hT_hl[:, y, k, META:T],
                                            start=(k == 0 and n == 0), stop=(k == KD - 1 and n == 2))
            last.then_inc(wi_summed, 1)

            def columns(i, j, spans):
                s = i * 2 + j
                pe.wait_ge(w_high, s + 1)
                pe.wait_ge(tile_read, s + 1)
                banks = [ps[:, 4 + 2 * j + b, 0:hi - lo] for b, (lo, hi) in enumerate(spans)]
                for b, (lo, hi) in enumerate(spans):
                    for k in range(KD):
                        for part in range(2):
                            nc.tensor.matmul(banks[b], w_hl[:, j, 0, P * k:P * (k + 1)], hT_hl[:, part, k, lo:hi],
                                             start=(k == 0 and part == 0), stop=False)
                pe.wait_ge(w_low, s + 1)
                for b, (lo, hi) in enumerate(spans):
                    for k in range(KD):
                        last = nc.tensor.matmul(banks[b], w_hl[:, j, 1, P * k:P * (k + 1)], hT_hl[:, 0, k, lo:hi],
                                                start=False, stop=(k == KD - 1))
                last.then_inc(tile_done, 1)

            def pair(i):
                for j in range(2):
                    columns(i, j, [(0, HALF), (HALF, T)])

            def gate_pair(i):
                for j in range(2):
                    columns(i, j, [(META, T)])

            def lows(first, last):
                for n in range(first, last):
                    c = n % 4
                    if n >= 2:
                        pe.wait_ge(low_read, n - 1)
                    w, x = ((lora[0:HD, :], wa[0:HD, :]), (lora[HD:P, :], wa[HD:P, :]), (lora_g[:, :], gl))[n // 4]
                    for half in range(2):
                        ins = nc.tensor.matmul(ps[:, 2 * (n % 2) + half, 0:HALF], w[:, P * c:P * (c + 1)],
                                               x[:, HALF * half:HALF * (half + 1)], start=True, stop=True)
                    ins.then_inc(low_done, 1)

            def head_sums(c, done):
                for half in range(2):
                    last = nc.tensor.matmul(ps[:, 2 * (c % 2) + half, 0:HALF], pair_ones[:, :],
                                            work[:, c, HALF * half:HALF * (half + 1)], start=True, stop=True)
                last.then_inc(done, 1)

            def sums(weights, src, bank):
                for half in range(2):
                    last = nc.tensor.matmul(ps[:, bank + half, 0:HALF], weights[:, :],
                                            src[:, HALF * half:HALF * (half + 1)], start=True, stop=True)
                last.then_inc(summed, 1)

            def logits(i):
                for h in range(HEADS):
                    n = HEADS * i + h
                    rows = slice(HD * (h % 2), HD * (h % 2 + 1))
                    if n >= 2:
                        pe.wait_ge(relu_done, n - 1)
                    for dst, lo, hi in pieces(ps, 2 * (h % 2), WIDTH[i]):
                        last = nc.tensor.matmul(dst, qi[rows, h // 2, P * i:P * (i + 1)], ki[rows, lo:hi],
                                                start=True, stop=True)
                    last.then_inc(logit_done, 1)

            with pe.Fori(0, INDEX) as i:
                pair(i)
            pe.wait_ge(wi_taken, 1)
            for i in range(NT):
                last = nc.tensor.transpose(ps[:, 0, HEADS * i:HEADS * (i + 1)], wi_by_head[:, P * i:P * (i + 1)],
                                           ident[0:HEADS, 0:HEADS])
            last.then_inc(wi_done, 1)
            pe.wait_ge(wi_copied, 1)
            pe.wait_ge(squared, 1)
            sums(ones, sq[:, 0, :], 0)
            sums(pair_ones, ki, 2)
            pair(INDEX)
            pe.wait_ge(squared, 2)
            pe.wait_ge(roots, 1)
            sums(pair_ones, sq[:, 1, :], 0)
            for i in range(INDEX + 1, OPERANDS):
                pair(i)
                if i in LOGITS_AFTER:
                    pe.wait_ge(ki_ready, 1)
                    logits(LOGITS_AFTER.index(i))
            pair(OPERANDS)
            pair(OPERANDS + 1)
            pe.wait_ge(lora_landed, 48)
            pe.wait_ge(squashed, 2)
            lows(0, 4)
            gate_pair(KEPT)
            lows(4, 8)
            gate_pair(KEPT + 1)
            lows(8, 12)
            pe.wait_ge(squares, 1)
            for c in range(PAIRS):
                if c < 2:
                    pe.wait_ge(low_read, 11 + c)
                else:
                    pe.wait_ge(norms_read, c - 1)
                head_sums(c, norms_summed)
            with pe.Fori(KEPT + 2, KEPT + 6) as i:
                gate_pair(i)
            pe.wait_ge(rk_ready, 1)
            pe.wait_ge(norms_read, PAIRS)
            head_sums(0, rk_summed)
            head_sums(1, rk_summed)
            with pe.Fori(KEPT + 6, PAIRS_ALL) as i:
                gate_pair(i)
            for c in range(2, PAIRS):
                pe.wait_ge(bonus_made, c - 1)
                head_sums(c, rk_summed)


def attend(nc, a, g):
    ps, ident, p_all, attended, barred = g["ps"], g["ident"], g["p_all"], g["attended"], g["barred"]
    with ExitStack() as ctx:
        sb = lambda name, shape: ctx.enter_context(nc.sbuf_tensor(name, shape, F32))
        sem = semaphores(nc, ctx, "attend")
        w_uk = sb("w_uk", [P, PAIRS, KV])
        w_uv = sb("w_uv", [P, HEADS * HD])
        cT, c_tok = p_all[:, CT_CKV, 1:PW], sb("c_tok", [P, 1 + NT, KV])
        q_abs = sb("q_abs", [P, HEADS, SEQ])
        probs = sb("prob", [P, 2, HEADS, T])
        peak, low_peak, total, share = (sb(n, [P, HEADS]) for n in ("peak", "low_peak", "total", "share"))
        probT = sb("probT", [P, 1 + NT, 4 * P])
        lat = sb("lat", [P, HEADS, P])
        landed = sem("uk_landed")
        c_turned, c_copied, abs_done, abs_copied = sem("c_turned"), sem("c_copied"), sem("abs_done"), sem("abs_copied")
        att_done, att_read, exped, shared, scaled_s, scaled_v = (
            sem(n) for n in ("att_done", "att_read", "exped", "shared", "scaled_s", "scaled_v"))
        turned, turn_copied, lat_done, lat_copied, out_done, out_copied = (
            sem(n) for n in ("p_turned", "p_copied", "lat_done", "lat_copied", "oa_done", "oa_copied"))
        order_sem = sem("dve_order2")
        q = p_all[:, CT_Q:CT_Q + 4, 1 + META:PW]
        blocks = lambda i: list(enumerate(TILES[:i + 2]))
        turns_before = lambda i: sum(2 * (x + 2) for x in range(i))
        block = ctx.enter_context(nc.Block())

        @block.sync
        def _(sp):
            sp.dma_start(w_uk[:, :, :], a["w_uk"]).then_inc(landed, 16)
            sp.dma_start(w_uv[:, :], a["w_uv"]).then_inc(landed, 16)
            sp.wait_ge(landed, 32)

        @block.scalar
        def _(act):
            act.wait_ge(c_turned, 1)
            nc.scalar.activation(c_tok[:, 1:1 + NT, :], ps[:, 6, :].rearrange("p (b r) -> p b r", b=NT), ACT.Copy
                                 ).then_inc(c_copied, 1)
            nc.scalar.activation(c_tok[0:META, 0, :], ps[0:META, 7, 0:KV], ACT.Copy).then_inc(c_copied, 1)
            for h in range(HEADS):
                act.wait_ge(abs_done, h + 1)
                nc.scalar.activation(q_abs[:, h, :], ps[:, h % 4, :], ACT.Copy).then_inc(abs_copied, 1)

            def softmax(i):
                w, prob = WIDTH[i], probs[:, i % 2]
                for h in range(HEADS):
                    act.wait_ge(att_read, HEADS * i + h + 1)
                    nc.scalar.activation(prob[:, h, 0:w], prob[:, h, 0:w], ACT.Exp, bias=low_peak[:, h:h + 1],
                                         accum_out=total[:, h:h + 1]).then_inc(exped, 1)
                    if h % 2:
                        act.wait_ge(shared, HEADS * i + h)
                        nc.scalar.activation(prob[:, h - 1, 0:w], prob[:, h - 1, 0:w], ACT.Copy,
                                             scale=share[:, h - 1:h]).then_inc(scaled_s, 1)

            softmax(0)
            for i in range(NT):
                if i + 1 < NT:
                    softmax(i + 1)
                n = turns_before(i)
                for half in range(2):
                    for b, (_, m) in blocks(i):
                        act.wait_ge(turned, n + 1)
                        if n:
                            act.wait_ge(lat_done, 2 * i + half)
                        nc.scalar.activation(probT[0:m, b, :], ps[0:m, 4 + n % 2, :], ACT.Copy).then_inc(turn_copied, 1)
                        n += 1
                    act.wait_ge(lat_done, 2 * i + half + 1)
                    if i:
                        act.wait_ge(out_done, i)
                    nc.scalar.activation(lat[:, 4 * half:4 * half + 4, :], ps[:, 6, :].rearrange("p (h q) -> p h q", h=4),
                                         ACT.Copy).then_inc(lat_copied, 1)
                act.wait_ge(out_done, i + 1)
                nc.scalar.activation(attended[:, :, P * i:P * (i + 1)], ps[:, 7, :].rearrange("p (j q) -> p j q", j=4),
                                     ACT.Copy).then_inc(out_copied, 1)

        @block.tensor
        def _(pe):
            for b, (t0, n) in enumerate(TILES):
                dst = ps[0:n, 7, 0:KV] if b == 0 else ps[0:n, 6, KV * (b - 1):KV * b]
                last = nc.tensor.transpose(dst, cT[:, t0:t0 + n], ident[:, :])
            last.then_inc(c_turned, 1)
            pe.wait_ge(landed, 32)
            for h in range(HEADS):
                e, j = h % 2, h // 2
                if h >= 4:
                    pe.wait_ge(abs_copied, h - 3)
                rows = slice(HD * e, HD * (e + 1))
                nc.tensor.matmul(ps[:, h % 4, :], w_uk[rows, j, :], q[rows, j, :], start=True, stop=True
                                 ).then_inc(abs_done, 1)

            pe.wait_ge(abs_copied, HEADS)
            pe.wait_ge(c_copied, 2)

            def scores(i):
                for h in range(HEADS):
                    n = HEADS * i + h
                    if n >= 2:
                        pe.wait_ge(att_read, n - 1)
                    for dst, lo, hi in pieces(ps, 2 * (h % 2), WIDTH[i]):
                        last = nc.tensor.matmul(dst, q_abs[:, h, P * i:P * (i + 1)], cT[:, lo:hi], start=True, stop=True)
                    last.then_inc(att_done, 1)

            scores(0)
            for i in range(NT):
                prob = probs[:, i % 2]
                if i + 1 < NT:
                    scores(i + 1)
                n = turns_before(i)
                for half in range(2):
                    pe.wait_ge(scaled_s, 4 * i + 2 * half + 2)
                    pe.wait_ge(scaled_v, 4 * i + 2 * half + 2)
                    for b, (k0, m) in blocks(i):
                        if n >= 2:
                            pe.wait_ge(turn_copied, n - 1)
                        for h in range(4):
                            last = nc.tensor.transpose(ps[0:m, 4 + n % 2, P * h:P * (h + 1)],
                                                       prob[:, 4 * half + h, k0:k0 + m], ident[:, :])
                        last.then_inc(turned, 1)
                        n += 1
                    pe.wait_ge(turn_copied, n)
                    if i or half:
                        pe.wait_ge(lat_copied, 2 * i + half)
                    for b, (k0, m) in blocks(i):
                        last = nc.tensor.matmul(ps[:, 6, :], c_tok[0:m, b, :], probT[0:m, b, :],
                                                start=(b == 0), stop=(b == i + 1))
                    last.then_inc(lat_done, 1)
                pe.wait_ge(lat_copied, 2 * i + 2)
                if i:
                    pe.wait_ge(out_copied, i)
                for h in range(HEADS):
                    e, j = h % 2, h // 2
                    last = nc.tensor.matmul(ps[HD * e:HD * (e + 1), 7, P * j:P * (j + 1)], w_uv[:, HD * h:HD * (h + 1)],
                                            lat[:, h, :], start=True, stop=True)
                last.then_inc(out_done, 1)

        @block.vector
        def _(dve):
            order = Order(dve, order_sem)
            put, settle = order.put, order.settle
            v_ = nc.vector

            def share_out(i, h):
                w, prob = WIDTH[i], probs[:, i % 2]
                dve.wait_ge(exped, HEADS * i + h + 1)
                v_.reciprocal(share[:, h:h + 1], total[:, h:h + 1]).then_inc(shared, 1)
                if h % 2:
                    dve.wait_ge(shared, HEADS * i + h + 1)
                    v_.tensor_scalar(prob[:, h, 0:w], prob[:, h, 0:w], share[:, h:h + 1], None, ALU.mult
                                     ).then_inc(scaled_v, 1)

            for i in range(NT):
                w, prob = WIDTH[i], probs[:, i % 2]
                if i >= 2:
                    dve.wait_ge(turned, turns_before(i - 1))
                for h in range(HEADS):
                    dve.wait_ge(att_done, HEADS * i + h + 1)
                    src = ps[:, 2 * (h % 2):2 * (h % 2) + 2, :].rearrange("p b t -> p (b t)")[:, 0:w]
                    put(v_.tensor_tensor_reduce(prob[:, h, 0:w], src, barred[i], ASCALE, FILL, ALU.add, ALU.max,
                                                peak[:, h:h + 1]))
                    settle()
                    v_.tensor_scalar(low_peak[:, h:h + 1], peak[:, h:h + 1], -1.0, None, ALU.mult).then_inc(att_read, 1)
                    if h:
                        share_out(i, h - 1)
                share_out(i, HEADS - 1)


def scan_chunks(nc, a, g):
    ps, ident, ones, pair_ones = g["ps"], g["ident"], g["ones"], g["pair_ones"]
    p_all, par, eps, chunk_decay = g["p_all"], g["par"], g["eps"], g["chunk_decay"]
    with ExitStack() as ctx:
        sb = lambda name, shape: ctx.enter_context(nc.sbuf_tensor(name, shape, F32))
        sem = semaphores(nc, ctx, "scan_chunks")
        below16, above16 = sb("below16", [P, P]), sb("above16", [P, P])
        below32, below64 = sb("below32", [P, P]), sb("below64", [P, P])
        above64, upto64 = sb("above64", [P, P]), sb("upto64", [P, P])
        scratch = g["h1T"].rearrange("p k t -> p (k t)")
        k_hat, b_hat = (scratch[:, 512 * x:512 * (x + 1)].rearrange("p (c t) -> p c t", c=PAIRS) for x in range(2))
        k_tok, b_tok = sb("k_tok", [P, 2, 512]), sb("b_tok", [P, 2, 512])
        v_tok = sb("v_tok", [P, 512])
        grams = {n: sb(n, [P, 2, 4, P]) for n in ("low16", "low32", "low64", "up16", "inv", "rb", "ak", "rk")}
        pw = [sb(f"pw{i}", [P, 2, 4, P]) for i in range(4)]
        x_sb, u_sb = scratch[:, 1024:1536], scratch[:, 1536:2048]
        state = scratch[:, 2048:2048 + 3 * 512].rearrange("p (s c t) -> p s c t", s=3, c=PAIRS)
        faded = scratch[:, 3584:].rearrange("p (c t) -> p c t", c=PAIRS)
        masks_made, tok_zero = sem("masks_made"), sem("tok_zero")
        hats, turned, tok_copied = sem("hats"), sem("turned"), sem("tok_copied")
        gram_done, gram_read = sem("gram_done"), sem("gram_read")
        step_done, step_s, step_v = sem("step_done"), sem("step_s"), sem("step_v")
        x_done, x_read, u_done, u_read, s_done, s_read, y_done, y_read = (
            sem(n) for n in ("x_done", "x_read", "u_done", "u_read", "s_done", "s_read", "y_done", "y_read"))
        order_sem, pool_order, u16_made = sem("dve_order4"), sem("pool_order4"), sem("u16_made")
        kT, rT, vT = (p_all[:, c:c + 4, 1:PW] for c in (CT_K, CT_R, CT_V))
        aT, bT = g["ab"][:, 0:4, :], g["ab"][:, 4:8, :]
        w_pa_landed = sem("w_pa_landed")
        block = ctx.enter_context(nc.Block())

        @block.sync
        def _(sp):
            sp.dma_start(g["w_pa"][:, :, :], a["w_pa"][0].rearrange("(k p) n -> p k n", p=P)).then_inc(w_pa_landed, 16)
            sp.wait_ge(w_pa_landed, 16)

        low16, low32, low64, up16, inv = (grams[n] for n in ("low16", "low32", "low64", "up16", "inv"))
        GRAMS = [(aT, bT, [(low16, below16), (low32, below32), (low64, below64)]),
                 (bT, aT, [(up16, above16)]),
                 (kT, aT, [(grams["ak"], above64)]),
                 (bT, rT, [(grams["rb"], upto64)]),
                 (kT, rT, [(grams["rk"], upto64)])]
        STEPS = [(up16, low16, pw[0], "s", "copy", 0, 0),
                 (low16, up16, pw[1], "s", "copy", 0, 0),
                 (pw[0], inv, inv, "v", "add", 1, 0),
                 (pw[1], pw[0], pw[2], "s", "copy", 2, 0),
                 (pw[0], pw[1], pw[3], "s", "copy", 2, 0),
                 (pw[2], inv, inv, "v", "add", 3, 1),
                 (pw[3], pw[2], pw[0], "s", "copy", 4, 1),
                 (pw[0], inv, inv, "v", "add", 5, 2),
                 (low32, inv, pw[1], "s", "copy", 5, 3),
                 (inv, None, pw[2], "v", "copy", 5, 3),
                 (pw[2], pw[1], inv, "v", "subtract", 6, 4),
                 (low64, inv, pw[3], "s", "copy", 6, 5),
                 (inv, None, pw[0], "v", "copy", 6, 5),
                 (pw[0], pw[3], inv, "v", "subtract", 7, 6)]
        S16 = 8

        def steps_of(tt):
            return STEPS[:S16] if TILES[tt][1] == META else STEPS

        def before(tt, engine):
            return sum(2 * sum(s[3] == engine for s in steps_of(i)) for i in range(tt))

        def chunks_of(tt):
            return [(0, 0, META)] if tt == 0 else [(2 * tt - 1, 0, CHUNK), (2 * tt, CHUNK, CHUNK)]

        @block.gpsimd
        def _(pool):
            order = Order(pool, pool_order)

            def within(dst, w):
                view = dst[:, :].rearrange("p (b w) -> p b w", w=w)
                order.put(nc.gpsimd.affine_select(out=view, in_=ones[:, :].rearrange("p (b w) -> p b w", w=w),
                                                  compare_op=ALU.is_ge, fill=0.0, base=0,
                                                  pattern=[[-w, P // w], [0, w]], channel_multiplier=1))
                order.settle()
                order.put(nc.gpsimd.affine_select(out=view, in_=view, compare_op=ALU.is_ge, fill=0.0, base=w - 1,
                                                  pattern=[[w, P // w], [0, w]], channel_multiplier=-1))

            def side(dst, src, mult, strict):
                return nc.gpsimd.affine_select(out=dst[:, :], in_=src[:, :], compare_op=ALU.is_ge, fill=0.0,
                                               base=-strict, pattern=[[mult, P]], channel_multiplier=-mult)

            within(above16, 16)
            within(above64, 64)
            within(below32, 32)
            order.settle()
            order.put(nc.gpsimd.tensor_tensor(below64[:, :], above64[:, :], below32[:, :], ALU.subtract))
            order.settle()
            order.put(nc.gpsimd.tensor_tensor(below32[:, :], below32[:, :], above16[:, :], ALU.subtract))
            order.put(side(below16, above16, -1, 1))
            order.put(side(upto64, above64, 1, 0))
            order.settle()
            order.put(side(above16, above16, 1, 1))
            order.put(side(above64, above64, 1, 1))
            order.put(side(below32, below32, -1, 1))
            order.put(side(below64, below64, -1, 1))
            order.settle()
            pool.sem_inc(masks_made, 1)

        @block.vector
        def _(dve):
            order = Order(dve, order_sem)
            put, settle = order.put, order.settle
            v_ = nc.vector
            def set_up():
                for x in (k_tok, b_tok, state):
                    put(v_.memset(x[:, :, :], 0.0))
                put(v_.memset(x_sb[:, :], 0.0))
                put(v_.memset(u_sb[:, :], 0.0))
                put(v_.memset(v_tok[:, :], 0.0))
                settle()
                dve.sem_inc(tok_zero, 1)
                dve.wait_ge(masks_made, 1)

            for tt, (t0, n) in enumerate(TILES):
                if tt:
                    dve.wait_ge(turned, 3 * tt)
                for src, dst in ((kT, k_hat), (bT, b_hat)):
                    for c, p0, m in chunks_of(tt):
                        put(v_.tensor_tensor(dst[:, :, p0:p0 + m], src[:, :, t0 + p0:t0 + p0 + m],
                                             chunk_decay[:, :, c:c + 1].broadcast_to([P, PAIRS, m]), ALU.mult))
                settle()
                dve.sem_inc(hats, 1)
                if tt == 0:
                    set_up()
                if tt:
                    dve.wait_ge(y_done, tt)
                for i, (_, _, copies) in enumerate(GRAMS):
                    for e in range(2):
                        dve.wait_ge(gram_done, 10 * tt + 2 * i + e + 1)
                        bank = ps[0:n, (2 * i + e) % 4, :].rearrange("p (j t) -> p j t", j=4)[:, :, 0:n]
                        for dst, mask in copies:
                            put(v_.tensor_tensor(dst[0:n, e, :, 0:n], bank,
                                                 mask[0:n, 0:n].unsqueeze(1).broadcast_to([n, 4, n]), ALU.mult))
                        settle()
                        if i == 1:
                            put(v_.tensor_tensor(inv[0:n, e, :, 0:n], ident[0:n, 0:n].unsqueeze(1).broadcast_to([n, 4, n]),
                                                 up16[0:n, e, :, 0:n], ALU.subtract))
                            settle()
                        dve.sem_inc(gram_read, 1)
                steps = steps_of(tt)
                for i, (_, _, dst, engine, how, _, _) in enumerate(steps):
                    for e in range(2):
                        if engine != "v":
                            continue
                        dve.wait_ge(step_done, 2 * sum(len(steps_of(x)) for x in range(tt)) + 2 * i + e + 1)
                        bank = ps[0:n, 4 + 2 * e + i % 2, :].rearrange("p (j t) -> p j t", j=4)[:, :, 0:n]
                        d = dst[0:n, e, :, 0:n]
                        if how == "copy":
                            v_.tensor_copy(d, bank).then_inc(step_v, 1)
                        else:
                            v_.tensor_tensor(d, d, bank, ALU.add if how == "add" else ALU.subtract).then_inc(step_v, 1)
                for c, p0, m in chunks_of(tt):
                    now, after = state[:, c % 3], state[:, (c + 1) % 3]
                    dve.wait_ge(x_done, c + 1)
                    v_.tensor_copy(x_sb[p0:p0 + m, :], ps[p0:p0 + m, 0, :]).then_inc(x_read, 1)
                    put(v_.tensor_tensor(faded[:, :, :], now[:, :, :],
                                         chunk_decay[:, :, c:c + 1].broadcast_to([P, PAIRS, P]), ALU.mult))
                    settle()
                    dve.wait_ge(s_done, c + 1)
                    for e in range(2):
                        rows = slice(HD * e, HD * (e + 1))
                        put(v_.tensor_tensor(after[rows, :, rows], faded[rows, :, rows],
                                             ps[rows, 2, :].rearrange("p (j v) -> p j v", j=4)[:, :, rows], ALU.add))
                    settle()
                    dve.sem_inc(s_read, 1)

        @block.scalar
        def _(act):
            act.wait_ge(tok_zero, 1)
            for tt, (t0, n) in enumerate(TILES):
                for i, dst in enumerate((k_tok, b_tok, None)):
                    act.wait_ge(turned, 3 * tt + i + 1)
                    if dst is None:
                        nc.scalar.activation(v_tok[0:n, :], ps[0:n, 6, :], ACT.Copy).then_inc(tok_copied, 1)
                        continue
                    for x, (_, p0, m) in enumerate(chunks_of(tt)):
                        last = nc.scalar.activation(dst[p0:p0 + m, x, :], ps[p0:p0 + m, 4 + i, :], ACT.Copy)
                    last.then_inc(tok_copied, 1)
                steps = steps_of(tt)
                for i, (_, _, dst, engine, _, _, _) in enumerate(steps):
                    for e in range(2):
                        if engine != "s":
                            continue
                        act.wait_ge(step_done, 2 * sum(len(steps_of(x)) for x in range(tt)) + 2 * i + e + 1)
                        bank = ps[0:n, 4 + 2 * e + i % 2, :].rearrange("p (j t) -> p j t", j=4)[:, :, 0:n]
                        nc.scalar.activation(dst[0:n, e, :, 0:n], bank, ACT.Copy).then_inc(step_s, 1)
                for c, p0, m in chunks_of(tt):
                    act.wait_ge(u_done, c + 1)
                    nc.scalar.activation(u_sb[p0:p0 + m, :], ps[p0:p0 + m, 1, :], ACT.Copy, scale=-1.0).then_inc(u_read, 1)
                act.wait_ge(y_done, tt + 1)
                nc.scalar.activation(aT[:, :, t0:t0 + n], ps[:, 3, :].rearrange("p (j t) -> p j t", j=4)[:, :, 0:n],
                                     ACT.Copy).then_inc(y_read, 1)

        @block.tensor
        def _(pe):
            for tt, (t0, n) in enumerate(TILES):
                span = slice(t0, t0 + n)
                chunks = chunks_of(tt)
                pe.wait_ge(hats, tt + 1)
                if tt:
                    pe.wait_ge(step_v, before(tt, "v"))
                    pe.wait_ge(step_s, before(tt, "s"))
                for i in range(3):
                    for j in range(PAIRS):
                        src = (k_hat[:, j, 0:n], b_hat[:, j, 0:n], vT[:, j, span])[i]
                        last = nc.tensor.transpose(ps[0:n, 4 + i, P * j:P * (j + 1)], src, ident[:, :])
                    last.then_inc(turned, 1)
                if tt:
                    pe.wait_ge(y_read, tt)
                for i, (lhs, rhs, _) in enumerate(GRAMS):
                    for e in range(2):
                        at = 2 * i + e
                        if at >= 4:
                            pe.wait_ge(gram_read, 10 * tt + at - 3)
                        for j in range(PAIRS):
                            last = nc.tensor.matmul(ps[0:n, at % 4, P * j:P * j + n], lhs[HD * e:HD * (e + 1), j, span],
                                                    rhs[HD * e:HD * (e + 1), j, span], start=True, stop=True)
                        last.then_inc(gram_done, 1)
                pe.wait_ge(tok_copied, 3 * (tt + 1))
                s0, v0 = before(tt, "s"), before(tt, "v")
                for i, (lhs, rhs, _, _, _, need_s, need_v) in enumerate(steps_of(tt)):
                    for e in range(2):
                        if i == 0:
                            pe.wait_ge(gram_read, 10 * tt + 3 + e)
                        if need_s:
                            pe.wait_ge(step_s, s0 + 2 * need_s - 1 + e)
                        if need_v:
                            pe.wait_ge(step_v, v0 + 2 * need_v - 1 + e)
                        if i >= 2:
                            who = steps_of(tt)[i - 2][3]
                            taken = sum(s[3] == who for s in STEPS[:i - 1])
                            pe.wait_ge(step_s if who == "s" else step_v, (s0 if who == "s" else v0) + 2 * taken - 1 + e)
                        for j in range(4):
                            dst = ps[0:n, 4 + 2 * e + i % 2, P * j:P * j + n]
                            if rhs is None:
                                last = nc.tensor.transpose(dst, lhs[0:n, e, j, 0:n], ident[0:n, 0:n])
                            else:
                                last = nc.tensor.matmul(dst, lhs[0:n, e, j, 0:n], rhs[0:n, e, j, 0:n], start=True, stop=True)
                        last.then_inc(step_done, 1)
                pe.wait_ge(gram_read, 10 * (tt + 1))
                pe.wait_ge(step_v, before(tt + 1, "v"))
                for x, (c, p0, m) in enumerate(chunks):
                    rows = slice(p0, p0 + m)
                    now = state[:, c % 3]
                    for e in range(2):
                        for j in range(PAIRS):
                            h = 2 * j + e
                            nc.tensor.matmul(ps[rows, 0, HD * h:HD * (h + 1)], grams["ak"][0:n, e, j, rows],
                                             v_tok[0:n, HD * h:HD * (h + 1)], start=(h == 0), stop=False,
                                             skip_group_check=True)
                    if c:
                        pe.wait_ge(s_read, c)
                    for j in range(PAIRS):
                        last = nc.tensor.matmul(ps[rows, 0, P * j:P * (j + 1)], aT[:, j, t0 + p0:t0 + p0 + m],
                                                now[:, j, :], start=False, stop=(j == PAIRS - 1), skip_group_check=True)
                    last.then_inc(x_done, 1)
                    pe.wait_ge(x_read, c + 1)
                    for e in range(2):
                        for j in range(PAIRS):
                            h = 2 * j + e
                            last = nc.tensor.matmul(ps[rows, 1, HD * h:HD * (h + 1)], inv[0:n, e, j, rows],
                                                    x_sb[0:n, HD * h:HD * (h + 1)], start=True, stop=True)
                    last.then_inc(u_done, 1)
                    for j in range(PAIRS):
                        nc.tensor.matmul(ps[:, 2, P * j:P * (j + 1)], k_tok[0:n, x, P * j:P * (j + 1)],
                                         v_tok[0:n, P * j:P * (j + 1)], start=(j == 0), stop=False, skip_group_check=True)
                    pe.wait_ge(u_read, c + 1)
                    for j in range(PAIRS):
                        last = nc.tensor.matmul(ps[:, 2, P * j:P * (j + 1)], b_tok[0:n, x, P * j:P * (j + 1)],
                                                u_sb[0:n, P * j:P * (j + 1)], start=False, stop=(j == PAIRS - 1),
                                                skip_group_check=True)
                    last.then_inc(s_done, 1)
                for j in range(PAIRS):
                    for name, src in (("rk", v_tok), ("rb", u_sb)):
                        for e in range(2):
                            h = 2 * j + e
                            nc.tensor.matmul(ps[HD * e:HD * (e + 1), 3, P * j:P * j + n], src[0:n, HD * h:HD * (h + 1)],
                                             grams[name][0:n, e, j, 0:n], start=(name == "rk"), stop=False,
                                             skip_group_check=True)
                    for x, (c, p0, m) in enumerate(chunks):
                        last = nc.tensor.matmul(ps[:, 3, P * j + p0:P * j + p0 + m], state[:, c % 3, j, :],
                                                rT[:, j, t0 + p0:t0 + p0 + m], start=False, stop=(x == len(chunks) - 1),
                                                skip_group_check=True)
                last.then_inc(y_done, 1)


def join(nc, a, g):
    ps, ident, pair_ones, h_tok, h1T = g["ps"], g["ident"], g["pair_ones"], g["h_tok"], g["h1T"]
    p_all, par, eps, attended = g["p_all"], g["par"], g["eps"], g["attended"]
    out_gate, bonus = g["out_gate"], g["bonus"]
    with ExitStack() as ctx:
        sb = lambda name, shape: ctx.enter_context(nc.sbuf_tensor(name, shape, F32))
        sem = semaphores(nc, ctx, "join")
        w_pa, w_pb, w_o = g["w_pa"], sb("w_pb", [P, PAIRS, D]), sb("w_o", [P, KD, D])
        stats, mv, std, rstd = sb("stats1", [P, NT, 2, 6]), sb("mv1", [P, NT, 2]), sb("std1", [P, NT]), sb("rstd1", [P, NT])
        flat = g["arena"]
        gates = flat[:, 0:2 * KD * SEQ].rearrange("p (c t) -> p c t", c=2 * KD)
        y = g["ab"][:, 0:4, META:T]
        root = g["ab"][:, 4:8, META:T]
        gate = lambda c: gates[:, c, :]
        gates_a, gates_b = gates[:, 0:KD, :], gates[:, KD:2 * KD, :]
        pb_landed, o_landed = sem("w_pb_landed"), sem("w_o_landed")
        sums_done, squares, roots, ob_ready = (sem(n) for n in ("y_sums", "y_squares", "y_roots", "ob_ready"))
        gates_landed = [sem("gates_a_landed"), sem("gates_b_landed")]
        branch_done, branch_read, mixed_ready = sem("branch_done"), sem("branch_read"), sem("mixed_ready")
        wo_done, var_ready, std_ready, ln_done = sem("wo_done"), sem("var1"), sem("std1_ready"), sem("ln1_done")
        wo_read = sem("wo_read")
        turned, copied_v, copied_s, order_sem = (
            sem(n) for n in ("h1_turned", "h1_copied_v", "h1_copied_s", "dve_order5"))
        block = ctx.enter_context(nc.Block())

        @block.sync
        def _(sp):
            def load_gates(half):
                sp.dma_start(gates[:, KD * half:KD * (half + 1), :],
                             g["gates_dram"][KD * half:KD * (half + 1)].rearrange("c p t -> p c t")
                             ).then_inc(gates_landed[half], 16)

            load_gates(0)
            sp.dma_start(w_pb[:, :, :], a["w_pb"][0].rearrange("(k p) n -> p k n", p=P)).then_inc(pb_landed, 16)
            load_gates(1)
            sp.dma_start(w_o[:, :, :], a["w_o"][0].rearrange("(k p) n -> p k n", p=P)).then_inc(o_landed, 16)

        @block.scalar
        def _(act):
            for c in range(PAIRS):
                act.wait_ge(sums_done, PAIRS + c + 1)
                nc.scalar.activation(root[:, c, :], ps[:, c, :], ACT.Sqrt, bias=eps[:, 3:4], scale=1.0 / HD).then_inc(roots, 1)

            def root_of(i):
                act.wait_ge(var_ready, i + 1)
                nc.scalar.activation(std[:, i:i + 1], mv[:, i, 1:2], ACT.Sqrt, bias=eps[:, 0:1]).then_inc(std_ready, 1)

            root_of(0)
            for i in range(NT):
                if i + 1 < NT:
                    root_of(i + 1)
                act.wait_ge(turned, 2 * i + 2)
                for k in range(4, KD):
                    last = nc.scalar.activation(h1T[:, k, P * i:P * (i + 1)], ps[:, 4 + 2 * (i % 2) + 1, P * (k - 4):P * (k - 3)],
                                                ACT.Identity, bias=par("ln1_b", k), scale=par("ln1_g", k))
                last.then_inc(copied_s, 1)

        @block.tensor
        def _(pe):
            def head_sums(src):
                for c in range(PAIRS):
                    nc.tensor.matmul(ps[:, c, :], pair_ones[:, :], src[:, c, :], start=True, stop=True).then_inc(sums_done, 1)

            def branch(w, x, base, columns):
                for c in columns:
                    n = base + c
                    if n >= 4:
                        pe.wait_ge(branch_read, n - 3)
                    for k in range(PAIRS):
                        last = nc.tensor.matmul(ps[:, 4 + n % 4, :], w[:, k, P * c:P * (c + 1)], x[:, k, :],
                                                start=(k == 0), stop=(k == PAIRS - 1))
                    last.then_inc(branch_done, 1)

            def turn(i):
                pe.wait_ge(ln_done, i + 1)
                if i >= 2:
                    pe.wait_ge(copied_v, i - 1)
                    pe.wait_ge(copied_s, i - 1)
                for k in range(KD):
                    last = nc.tensor.transpose(ps[:, 4 + 2 * (i % 2) + k // 4, P * (k % 4):P * (k % 4 + 1)],
                                               h_tok[:, i, P * k:P * (k + 1)], ident[:, :])
                    if k % 4 == 3:
                        last.then_inc(turned, 1)

            head_sums(y)
            branch(w_pa, attended, 0, range(2))
            pe.wait_ge(squares, 1)
            head_sums(root)
            branch(w_pa, attended, 0, range(2, KD))
            pe.wait_ge(pb_landed, 16)
            pe.wait_ge(ob_ready, 1)
            branch(w_pb, y, KD, range(KD))
            pe.wait_ge(o_landed, 16)
            pe.wait_ge(mixed_ready, 1)
            for i in range(NT):
                for half in range(2):
                    n = 2 * i + half
                    if n >= 4:
                        pe.wait_ge(wo_read, n - 3)
                    for k in range(KD):
                        last = nc.tensor.matmul(ps[:, n % 4, :], gates_a[:, k, P * i:P * (i + 1)],
                                                w_o[:, k, 512 * half:512 * (half + 1)], start=(k == 0), stop=(k == KD - 1))
                    last.then_inc(wo_done, 1)
                if i:
                    turn(i - 1)
            turn(NT - 1)

        @block.vector
        def _(dve):
            order = Order(dve, order_sem)
            put, settle = order.put, order.settle
            v_ = nc.vector
            for c in range(PAIRS):
                dve.wait_ge(sums_done, c + 1)
                put(v_.scalar_tensor_tensor(y[:, c, :], ps[:, c, :], -1.0 / HD, y[:, c, :], ALU.mult, ALU.add))
            settle()
            v_.tensor_tensor(root, y, y, ALU.mult).then_inc(squares, 1)

            def take_branch(n):
                if n % KD == 0:
                    dve.wait_ge(gates_landed[n // KD], 16)
                dve.wait_ge(branch_done, n + 1)
                v_.tensor_tensor(gate(n), ps[:, 4 + n % 4, :], gate(n), ALU.mult).then_inc(branch_read, 1)

            take_branch(0)
            take_branch(1)
            for c in range(PAIRS):
                dve.wait_ge(roots, c + 1)
                put(v_.reciprocal(root[:, c, :], root[:, c, :]))
                take_branch(2 + c)
            settle()
            put(v_.tensor_tensor(y, y, root, ALU.mult))
            settle()
            for c in range(PAIRS):
                put(v_.tensor_scalar(y[:, c, :], y[:, c, :], par("lnx_g", c), par("lnx_b", c), ALU.mult, ALU.add))
            settle()
            put(v_.tensor_tensor(y, y, bonus[:, :, META:T], ALU.add))
            settle()
            v_.tensor_tensor(y, y, out_gate[:, :, META:T], ALU.mult).then_inc(ob_ready, 1)
            for n in range(2 + PAIRS, 2 * KD):
                take_branch(n)
            dve.wait_ge(branch_read, 2 * KD)
            v_.tensor_tensor(gates_a, gates_a, gates_b, ALU.add).then_inc(mixed_ready, 1)

            def take_turned(i):
                dve.wait_ge(turned, 2 * i + 1)
                for k in range(4):
                    last = v_.tensor_scalar(h1T[:, k, P * i:P * (i + 1)], ps[:, 4 + 2 * (i % 2), P * k:P * (k + 1)],
                                            par("ln1_g", k), par("ln1_b", k), ALU.mult, ALU.add)
                last.then_inc(copied_v, 1)

            for i in range(NT):
                for half in range(2):
                    dve.wait_ge(wo_done, 2 * i + half + 1)
                    part = h_tok[:, i, 512 * half:512 * (half + 1)]
                    v_.scalar_tensor_tensor(part, part, ALPHA, ps[:, (2 * i + half) % 4, :], ALU.mult, ALU.add
                                            ).then_inc(wo_read, 1)
                dve.wait_ge(wo_read, 2 * i + 2)
                for half in range(2):
                    put(v_.bn_stats(stats[:, i, half, :], h_tok[:, i, 512 * half:512 * (half + 1)]))
                settle()
                v_.bn_aggr(mv[:, i, :], stats[:, i, :, :]).then_inc(var_ready, 1)
                dve.wait_ge(std_ready, i + 1)
                put(v_.reciprocal(rstd[:, i:i + 1], std[:, i:i + 1]))
                settle()
                v_.tensor_scalar(h_tok[:, i, :], h_tok[:, i, :], mv[:, i, 0:1], rstd[:, i:i + 1],
                                 ALU.subtract, ALU.mult).then_inc(ln_done, 1)
                if i:
                    take_turned(i - 1)
            take_turned(NT - 1)


def route(nc, a, g):
    ps, ident, h1T, h_hl, dense, parked = g["ps"], g["ident"], g["h1T"], g["h_hl"], g["dense"], g["parked"]
    NP = PEER_HEADS * PEER_TOPK
    K = PEER_TOPK
    LOTS = SEQ // LOT
    TILES_OF_HEAD = 4
    DURING_TOPK = PEER_HEADS * TILES_OF_HEAD
    BETWEEN = 16
    GATES_AT = 10
    LOTS_IN_LOOP = 4
    FOUR = 4
    with ExitStack() as ctx:
        sb = lambda name, shape, dt=F32: ctx.enter_context(nc.sbuf_tensor(name, shape, dt))
        sem = semaphores(nc, ctx, "route")
        staged = sb("w_staged", [P, 4, KD * P])
        w_hl = sb("w_hl", [P, 4, 2, KD * P], F32R)
        free = h1T.rearrange("p k t -> p (k t)")
        hot1 = free[:, 0:4 * FOUR * P].rearrange("p (r n k) -> p r n k", r=4, n=FOUR)
        act_out, qT = (free[:, 2048 + 1024 * x:3072 + 1024 * x].rearrange("p (j t) -> p j t", j=2) for x in range(2))
        sub_keys = sb("sub_keys", [P, 2 * PEER_HEADS, P])
        s_head = sb("s_head", [P, 2, 2, NT, P])
        top = sb("top", [P, 2, NT, K])
        top_at = sb("top_at", [P, 2, NT, K], U32)
        keys = sb("keys", [P, 2, NT, K])
        cand = sb("cand", [P, NT, K * K])
        best = sb("best6", [P, NT, K])
        best_at = sb("best_at", [P, NT, K], U32)
        split_at = sb("split_at", [P, 2, NT, K], U32)
        place = sb("place", [P, 2, NT, K])
        is_place = sb("is_place", [P, 2, NT, K, K])
        picks = sb("picks", [P, 3, NT, NP])
        picksT = sb("picksT", [P, 3, SEQ])
        small = sb("small", [P, NT * PEER_HEADS])
        count16, count128 = sb("count16", [P, K]), sb("count128", [P, P])
        now = sb("now", [P, 3, LOTS_IN_LOOP * LOT])
        hot2 = sb("hot2", [P, 4, FOUR, P], F32R)
        hot1_hl = sb("hot1_hl", [P, 4, 2, FOUR, P], F32R)
        lot = sb("lot", [P, 2, P, LOT])
        g_row, b_row = (lot[:, 0].rearrange("p k n -> p (k n)")[:, D * x:D * (x + 1)] for x in range(2))
        rows_landed, rows_order = sem("rows_landed"), sem("rows_order")
        landed = [sem(f"w_landed{j}") for j in range(4)]
        h_high, h_low = sem("h_high"), sem("h_low")
        w_high, w_low, tile_done, gelu_made = sem("w_high"), sem("w_low"), sem("tile_done"), sem("gelu_made")
        act_parked = [sem(f"act_parked{j}") for j in range(2)]
        keys_landed, counted = sem("sub_keys_landed"), sem("counted")
        q_copied, s_done, s_copied, topped = (sem(n) for n in ("q_copied", "s_done", "s_copied", "topped"))
        order_sem, softmax_sem, now_ready = sem("dve_order6"), sem("softmax_order"), sem("now_ready")
        lowered, raised, gates_ready, picks_turned, picks_copied = (
            sem(n) for n in ("lowered", "raised", "gates_ready", "picks_turned", "picks_copied"))
        hot_ready, hot_high, hot_low = sem("hot_ready"), sem("hot_high"), sem("hot_low")
        four_done, four_copied = sem("four_done"), sem("four_copied")
        lot_stored = [sem(f"lot_stored{j}") for j in range(2)]
        block = ctx.enter_context(nc.Block())
        LOOPS = LOTS // LOTS_IN_LOOP
        UNTIL_DENSE = DURING_TOPK + BETWEEN
        EXPERTS_BEFORE = UNTIL_DENSE - 2 * PEER_HEADS
        tile_bank = lambda j, is_query: j % 2 if is_query else 2 + j % 2

        @block.sync
        def _(sp):
            def load(s, j):
                sp.dma_start(staged[:, j, :], a["stream"][s]).then_inc(landed[j], 16)

            for j in range(4):
                load(j, j)
            sp.dma_start(g_row, a["ln1_g"].partition_broadcast(P)).then_inc(rows_landed, 16)
            sp.dma_start(b_row, a["ln1_b"].partition_broadcast(P)).then_inc(rows_landed, 16)
            sp.dma_start(sub_keys[:, :, :], a["sub_keys"]).then_inc(keys_landed, 16)
            with sp.Fori(0, UNTIL_DENSE // 8) as i:
                for j in range(8):
                    sp.wait_ge(w_low, i * 8 + (j + 1))
                    load(i * 8 + (j + 4), j % 4)

            def lots(i, last=False):
                for j in range(LOTS_IN_LOOP):
                    if not last:
                        sp.wait_ge(w_low, i * 4 + (UNTIL_DENSE + j + 1))
                        load(i * 4 + (UNTIL_DENSE + j + 4), j)
                    sp.wait_ge(four_copied, i * (4 * LOTS_IN_LOOP) + (4 * j + 4 + 4))
                    sp.dma_start(dense[i * LOTS_IN_LOOP + j], lot[:, j % 2, :, :].rearrange("p k n -> p (k n)")
                                 ).then_inc(lot_stored[j % 2], 16)

            with sp.Fori(0, LOOPS - 1) as i:
                lots(i)
            lots(LOOPS - 1, last=True)
            for j in range(2):
                sp.wait_ge(lot_stored[j], 16 * (LOTS // 2 + 1))
                sp.wait_ge(act_parked[j], 16 * (PARKED // 2 + 1))

        @block.gpsimd
        def _(pool):
            nc.gpsimd.iota(count16[:, :], [[1, K]], 0, 0, allow_small_or_imprecise_dtypes=True).then_inc(counted, 1)
            nc.gpsimd.iota(count128[:, :], [[1, P]], 0, 0, allow_small_or_imprecise_dtypes=True).then_inc(counted, 1)

            def low(s, j):
                pool.wait_ge(w_high, s + 1)
                nc.gpsimd.tensor_tensor(w_hl[:, j % 4, 1, :], staged[:, j % 4, :], w_hl[:, j % 4, 0, :].bitcast(F32),
                                        ALU.subtract).then_inc(w_low, 1)

            def hot_lows(u, q):
                r = q % 4
                pool.wait_ge(hot_high, u + 1)
                nc.gpsimd.tensor_tensor(hot1_hl[:, r, 1], hot1[:, r], hot1_hl[:, r, 0].bitcast(F32),
                                        ALU.subtract).then_inc(hot_low, 1)

            for j in range(3):
                low(j, j)
            with pool.Fori(0, UNTIL_DENSE // 8) as i:
                for j in range(8):
                    low(i * 8 + (j + 3), j + 3)
            for q in range(3):
                hot_lows(q, q)

            def lots(i, last=False):
                for j in range(LOTS_IN_LOOP):
                    for q in range(3, 7):
                        if not (last and j == LOTS_IN_LOOP - 1 and q > 3):
                            hot_lows(i * (4 * LOTS_IN_LOOP) + (4 * j + q), q)
                        if q == 3 and not (last and j >= 1):
                            low(i * 4 + (UNTIL_DENSE + j + 3), j + 3)

            with pool.Fori(0, LOOPS - 1) as i:
                lots(i)
            lots(LOOPS - 1, last=True)

        @block.scalar
        def _(act):
            act.sem_inc(s_copied, 4)
            act.sem_inc(four_copied, 4)
            act.sem_inc(gelu_made, 2)
            act.sem_inc(q_copied, 2)
            for j in range(2):
                act.sem_inc(act_parked[j], 16)
                act.sem_inc(lot_stored[j], 16)
            for k in range(KD):
                nc.scalar.activation(h_hl[:, 0, k, :], h1T[:, k, :], ACT.Copy).then_inc(h_high, 1)

            def high(s, j, landings, free=True):
                act.wait_ge(landed[j % 4], landings * 16)
                if free:
                    act.wait_ge(tile_done, s - 2)
                nc.scalar.activation(w_hl[:, j % 4, 0, :], staged[:, j % 4, :], ACT.Copy).then_inc(w_high, 1)

            def gelu(s, n, j, turn):
                act.wait_ge(tile_done, s + 2)
                act.wait_ge(act_parked[j % 2], turn * 16)
                nc.scalar.activation(act_out[:, j % 2, :], ps[:, tile_bank(j, False), :], ACT.Gelu).then_inc(gelu_made, 1)
                act.wait_ge(gelu_made, n + 3)
                nc.scalar.dma_start(parked[n], act_out[:, j % 2, :]).then_inc(act_parked[j % 2], 16)

            for j in range(3):
                high(j, j, 1, free=False)
            act.wait_ge(h_low, KD)
            with act.Fori(0, PEER_HEADS // 2) as i:
                for r in range(2):
                    for x in range(2):
                        j = 4 * r + x
                        high(i * 8 + (j + 3), j + 3, i * 2 + ((j + 3) // 4 + 1))
                        act.wait_ge(tile_done, i * 8 + (j + 2))
                        nc.scalar.activation(qT[:, x, :], ps[:, tile_bank(j, True), :], ACT.Copy).then_inc(q_copied, 1)
                    j = 4 * r + 2
                    high(i * 8 + (j + 3), j + 3, i * 2 + ((j + 3) // 4 + 1))
                    gelu(i * 8 + j, i * 4 + 2 * r, j, i * 2 + (r + 1))
                    act.wait_ge(topped, i * 2 + (r + 1))
                    for x in range(2):
                        act.wait_ge(s_done, i * 4 + (2 * r + x + 1))
                        nc.scalar.activation(s_head[:, r, x], ps[:, 4 + 2 * r + x, :].rearrange("p (t k) -> p t k", t=NT),
                                             ACT.Copy).then_inc(s_copied, 1)
                    j = 4 * r + 3
                    high(i * 8 + (j + 3), j + 3, i * 2 + ((j + 3) // 4 + 1))
                    gelu(i * 8 + j, i * 4 + (2 * r + 1), j, i * 2 + (r + 1))
            for j in range(BETWEEN):
                high(DURING_TOPK + j + 3, j + 3, (DURING_TOPK + j + 3) // 4 + 1)
                gelu(DURING_TOPK + j, 2 * PEER_HEADS + j, j, PEER_HEADS + j // 2 + 1)
                if j == GATES_AT - 3:
                    act.wait_ge(lowered, 1)
                    nc.scalar.activation(picks[:, 2], picks[:, 2], ACT.Exp).then_inc(raised, 1)

            def hot_highs(u, q):
                act.wait_ge(hot_ready, u + 1)
                nc.scalar.activation(hot1_hl[:, q % 4, 0], hot1[:, q % 4], ACT.Copy).then_inc(hot_high, 1)

            def copy(u, q, j):
                act.wait_ge(four_done, u + (1 + 4))
                nc.scalar.activation(lot[:, j % 2, :, FOUR * q:FOUR * (q + 1)].rearrange("p k n -> p n k"),
                                     ps[:, 4 + q, :].rearrange("p (n k) -> p n k", n=FOUR), ACT.Copy
                                     ).then_inc(four_copied, 1)

            for q in range(3):
                hot_highs(q, q)

            def lots(i, last=False):
                for j in range(LOTS_IN_LOOP):
                    for q in range(4):
                        u = i * (4 * LOTS_IN_LOOP) + (4 * j + q)
                        if not (last and j == LOTS_IN_LOOP - 1 and q):
                            hot_highs(u + 3, q + 3)
                        if q == 0:
                            if not (last and j >= 1):
                                high(i * 4 + (UNTIL_DENSE + j + 3), j + 3, i + ((UNTIL_DENSE + j + 3) // 4 + 1))
                            gelu(i * 4 + (UNTIL_DENSE + j), i * 4 + (EXPERTS_BEFORE + j), j,
                                 i * 2 + ((EXPERTS_BEFORE + j) // 2 + 1))
                            act.wait_ge(lot_stored[j % 2], i * 32 + 16 * (j // 2 + 1))
                        copy(u, q, j)

            with act.Fori(0, LOOPS - 1) as i:
                lots(i)
            lots(LOOPS - 1, last=True)

        @block.tensor
        def _(pe):
            pe.sem_inc(four_done, 4)
            pe.sem_inc(tile_done, 1)

            def tile(s, j, is_query, before):
                pe.wait_ge(w_high, s + 1)
                pe.wait_ge(*before)
                bank = ps[:, tile_bank(j, is_query), :]
                for k in range(KD):
                    for part in range(2):
                        nc.tensor.matmul(bank, w_hl[:, j % 4, 0, P * k:P * (k + 1)], h_hl[:, part, k, :],
                                         start=(k == 0 and part == 0), stop=False)
                pe.wait_ge(w_low, s + 1)
                for k in range(KD):
                    last = nc.tensor.matmul(bank, w_hl[:, j % 4, 1, P * k:P * (k + 1)], h_hl[:, 0, k, :],
                                            start=False, stop=(k == KD - 1))
                last.then_inc(tile_done, 1)

            def scores(i, r):
                pe.wait_ge(keys_landed, 16)
                for x in range(2):
                    pe.wait_ge(q_copied, i * 4 + (2 * r + x + 3))
                    pe.wait_ge(s_copied, i * 4 + (2 * r + x + 1))
                    for t in range(NT):
                        last = nc.tensor.matmul(ps[:, 4 + 2 * r + x, P * t:P * (t + 1)], qT[:, x, P * t:P * (t + 1)],
                                                sub_keys[:, i * 4 + (2 * r + x), :], start=True, stop=True)
                    last.then_inc(s_done, 1)

            pe.wait_ge(h_high, KD)
            pe.wait_ge(h_low, KD)

            with pe.Fori(0, PEER_HEADS // 2) as i:
                for r in range(2):
                    for x in range(2):
                        tile(i * 8 + (4 * r + x), 4 * r + x, True, (q_copied, i * 4 + (2 * r + x + 1)))
                    tile(i * 8 + (4 * r + 2), 2, False, (gelu_made, i * 4 + (2 * r + 1)))
                    scores(i, r)
                    tile(i * 8 + (4 * r + 3), 3, False, (gelu_made, i * 4 + (2 * r + 2)))
            for j in range(BETWEEN):
                if j == GATES_AT:
                    pe.wait_ge(s_copied, 2 * PEER_HEADS + 4)
                    pe.wait_ge(gates_ready, 1)
                    for x in range(3):
                        for t in range(NT):
                            last = nc.tensor.transpose(ps[:, 4 + x, P * t:P * (t + 1)], picks[:, x, t, :], ident[:, :])
                        last.then_inc(picks_turned, 1)
                tile(DURING_TOPK + j, j, False, (gelu_made, 2 * PEER_HEADS + j + 1))
            pe.wait_ge(picks_copied, 3)

            def four(u, q):
                pe.wait_ge(four_copied, u + 1)
                pe.wait_ge(hot_low, u + 1)
                for n in range(FOUR):
                    for part in range(2):
                        last = nc.tensor.matmul(ps[:, 4 + q, P * n:P * (n + 1)], hot2[:, q, n, :],
                                                hot1_hl[:, q, part, n, :], start=(part == 0), stop=(part == 1))
                last.then_inc(four_done, 1)

            with pe.Fori(0, LOOPS) as i:
                for j in range(LOTS_IN_LOOP):
                    tile(i * 4 + (UNTIL_DENSE + j), j, False, (gelu_made, i * 4 + (EXPERTS_BEFORE + j + 1)))
                    for q in range(4):
                        four(i * (4 * LOTS_IN_LOOP) + (4 * j + q), q)

        @block.vector
        def _(dve):
            v_ = nc.vector
            for k in range(KD):
                dve.wait_ge(h_high, k + 1)
                v_.tensor_tensor(h_hl[:, 1, k, :], h1T[:, k, :], h_hl[:, 0, k, :].bitcast(F32), ALU.subtract).then_inc(h_low, 1)
            dve.sem_inc(topped, 2)
            rows = Order(dve, rows_order)
            dve.wait_ge(rows_landed, 32)
            for row, op in ((g_row, ALU.mult), (b_row, ALU.add)):
                for i in range(NT):
                    rows.put(v_.tensor_tensor(g["h_tok"][:, i, :], g["h_tok"][:, i, :], row, op))
                rows.settle()
            dve.wait_ge(counted, 2)

            def rank(i, r):
                done = [0]

                def put(ins):
                    ins.then_inc(order_sem, 1)
                    done[0] += 1

                def settle():
                    dve.wait_ge(order_sem, done[0])

                def best_two_rounds(values, out, at, streams):
                    lo, hi = slice(0, 8), slice(8, 16)
                    for x in streams:
                        put(v_.max(out(x)[:, lo], values(x)))
                    settle()
                    for x in streams:
                        put(v_.max_index(at(x)[:, lo], out(x)[:, lo], values(x)))
                    settle()
                    for x in streams:
                        put(v_.match_replace(values(x), out(x)[:, lo], values(x), MARK))
                    settle()
                    for x in streams:
                        put(v_.max(out(x)[:, hi], values(x)))
                    settle()
                    for x in streams:
                        put(v_.max_index(at(x)[:, hi], out(x)[:, hi], values(x)))

                dve.sem_clear(order_sem)
                dve.wait_ge(s_copied, i * 4 + (2 * r + 2 + 4))
                dve.sem_inc(order_sem, 1)
                done[0] += 1
                best_two_rounds(lambda x: s_head[:, r, x // NT, x % NT, :], lambda x: top[:, x // NT, x % NT, :],
                                lambda x: top_at[:, x // NT, x % NT, :], range(2 * NT))
                settle()
                dve.sem_inc(topped, 1)
                put(v_.tensor_copy(keys[:, :], top_at[:, :]))
                put(v_.tensor_tensor(cand[:, :, :].rearrange("p t (x y) -> p t x y", x=K),
                                     top[:, 0].unsqueeze(3).broadcast_to([P, NT, K, K]),
                                     top[:, 1].unsqueeze(2).broadcast_to([P, NT, K, K]), ALU.add))
                settle()
                best_two_rounds(lambda t: cand[:, t, :], lambda t: best[:, t, :], lambda t: best_at[:, t, :], range(NT))
                settle()
                put(v_.tensor_scalar(split_at[:, 0], best_at[:, :], 4, None, ALU.logical_shift_right))
                put(v_.tensor_scalar(split_at[:, 1], best_at[:, :], K - 1, None, ALU.bitwise_and))
                put(v_.tensor_copy(picks[:, 2, :, bass.ds(i * (2 * K) + r * K, K)], best[:, :]))
                settle()
                put(v_.tensor_copy(place[:, :], split_at[:, :]))
                settle()
                for x in range(2):
                    put(v_.tensor_tensor(is_place[:, x].rearrange("p t k j -> p (t k) j"),
                                         place[:, x].rearrange("p t k -> p (t k)").unsqueeze(2).broadcast_to([P, NT * K, K]),
                                         count16[:, :].unsqueeze(1).broadcast_to([P, NT * K, K]), ALU.is_equal))
                settle()
                for x in range(2):
                    put(v_.tensor_tensor(is_place[:, x], is_place[:, x],
                                         keys[:, x].unsqueeze(2).broadcast_to([P, NT, K, K]), ALU.mult))
                settle()
                put(v_.tensor_reduce(picks[:, 0:2, :, bass.ds(i * (2 * K) + r * K, K)], is_place[:, :], AX.X, ALU.add))
                settle()

            with dve.Fori(0, PEER_HEADS // 2) as i:
                rank(i, 0)
                rank(i, 1)
            gate = picks[:, 2].rearrange("p t (h k) -> p (t h) k", h=PEER_HEADS)
            v_.tensor_copy(small[:, :], gate[:, :, 0]).then_inc(softmax_sem, 1)
            dve.wait_ge(softmax_sem, 1)
            wide = small[:, :].unsqueeze(2).broadcast_to([P, NT * PEER_HEADS, K])
            v_.tensor_tensor(gate, gate, wide, ALU.subtract).then_inc(lowered, 1)
            dve.wait_ge(raised, 1)
            v_.tensor_reduce(small[:, :], gate, AX.X, ALU.add).then_inc(softmax_sem, 1)
            dve.wait_ge(softmax_sem, 2)
            v_.reciprocal(small[:, :], small[:, :]).then_inc(softmax_sem, 1)
            dve.wait_ge(softmax_sem, 3)
            v_.tensor_tensor(gate, gate, wide, ALU.mult).then_inc(gates_ready, 1)
            for x in range(3):
                dve.wait_ge(picks_turned, x + 1)
                v_.tensor_copy(picksT[:, x, :], ps[:, 4 + x, :]).then_inc(picks_copied, 1)
            dve.wait_ge(picks_copied, 3)
            with dve.Fori(0, LOOPS) as i:
                v_.tensor_copy(now[:, :, :], picksT[:, :, bass.ds(i * (LOTS_IN_LOOP * LOT), LOTS_IN_LOOP * LOT)]
                               ).then_inc(now_ready, 1)
                dve.wait_ge(now_ready, i + 1)
                for u in range(4 * LOTS_IN_LOOP):
                    dve.wait_ge(four_done, i * (4 * LOTS_IN_LOOP) + (u + 1))
                    for n in range(FOUR):
                        t = FOUR * u + n
                        v_.tensor_scalar(hot1[:, u % 4, n, :], count128[:, :], now[:, 0, t:t + 1],
                                         now[:, 2, t:t + 1], ALU.is_equal, ALU.mult)
                    v_.tensor_tensor(hot2[:, u % 4], count128[:, :].unsqueeze(1).broadcast_to([P, FOUR, P]),
                                     now[:, 1, FOUR * u:FOUR * (u + 1)].unsqueeze(2).broadcast_to([P, FOUR, P]),
                                     ALU.is_equal).then_inc(hot_ready, 1)
                dve.wait_ge(hot_ready, i * (4 * LOTS_IN_LOOP) + 4 * LOTS_IN_LOOP)


def experts(nc, a, g, out):
    ps, h_tok, h_hl, dense, parked, eps = g["ps"], g["h_tok"], g["h_hl"], g["dense"], g["parked"], g["eps"]
    GT = 4
    LOOP = 2 * GT
    LOTS = SEQ // LOT
    FIRST, LOOPS = PARKED // LOOP, EXPERT_KEYS // LOOP
    BANKS = 2 * NT
    STREAM = 2 * PEER_HEADS
    with ExitStack() as ctx:
        sb = lambda name, shape, dt=F32: ctx.enter_context(nc.sbuf_tensor(name, shape, dt))
        sem = semaphores(nc, ctx, "experts")
        u_staged = g["h1T"].rearrange("p k t -> p (k t)").rearrange("p (j w) -> p j w", j=4)
        u_hl = sb("u_hl", [P, 2, 2, KD * P], F32R)
        v_staged = sb("v_staged", [P, 2, D])
        v_hl = sb("v_hl", [P, 2, GT, 2, D], F32R)
        gates = sb("gates", [P, LOTS, LOOP * LOT])
        coef = sb("coef", [P, 2, SEQ])
        coef_hl = sb("coef_hl", [P, 2, GT, 2, SEQ], F32R)
        stats, mv, std, rstd = sb("stats2", [P, NT, 2, 6]), sb("mv2", [P, NT, 2]), sb("std2", [P, NT]), sb("rstd2", [P, NT])
        g_row, b_row = v_staged[:, 0, :], v_staged[:, 1, :]
        u_landed = [sem(f"u_landed{j}") for j in range(4)]
        v_landed, act_landed = [sem(f"v_landed{j}") for j in range(2)], [sem(f"act_landed{j}") for j in range(2)]
        gates_landed = sem("gates_landed")
        u_high, u_low, v_high, v_low, coef_high, coef_low = (
            sem(n) for n in ("u_high", "u_low", "v_high", "v_low", "coef_high", "coef_low"))
        hid_done, gelu_made, weighed, sum_done, sum_read = (
            sem(n) for n in ("hid_done", "gelu_made", "weighed", "sum_done", "sum_read"))
        scaled, order_sem, var_ready, std_ready, row_landed, ready = (
            sem(n) for n in ("h_scaled", "dve_order7", "var2", "std2_ready", "row2_landed", "out_ready"))
        stored = sem("out_stored")
        block = ctx.enter_context(nc.Block())

        fresh = lambda i, j: i * LOOP + (j - PARKED)

        @block.sync
        def _(sp):
            def load_u(i, j, wait=True):
                if wait:
                    sp.wait_ge(u_low, fresh(i, j - 3))
                sp.dma_start(u_staged[:, j % 4, :], a["stream"][i * LOOP + (STREAM + j)]).then_inc(u_landed[j % 4], 16)

            def load_v(i, j):
                sp.wait_ge(v_low, i * LOOP + (j + 1))
                sp.dma_start(v_staged[:, j % 2, :], a["v"][i * LOOP + j]).then_inc(v_landed[j % 2], 16)

            def load_gates(i):
                sp.wait_ge(weighed, i * LOOP + LOOP)
                sp.dma_start(gates[:, :, :], dense[:, :, bass.ds(i * (LOOP * LOT), LOOP * LOT)]
                             .rearrange("l p k -> p l k")).then_inc(gates_landed, 16)

            def load_parked(i, j):
                sp.wait_ge(coef_low, i * LOOP + (j + 1))
                sp.dma_start(coef[:, j % 2, :], parked[i * LOOP + j]).then_inc(act_landed[j % 2], 16)

            load_u(FIRST, 0, wait=False)
            load_u(FIRST, 1, wait=False)
            load_gates(0)
            for j in range(LOOP):
                load_parked(0, j)
                load_v(0, j)
                if j == 1:
                    load_u(FIRST, 2, wait=False)
                    load_u(FIRST, 3, wait=False)
            with sp.Fori(1, FIRST) as i:
                load_gates(i)
                for j in range(LOOP):
                    load_parked(i, j)
                    load_v(i, j)
            load_gates(FIRST)

            def both(i, last=False):
                for j in range(GT):
                    load_u(i, GT + j)
                for j in range(GT):
                    load_v(i, j)
                if not last:
                    for j in range(GT):
                        load_u(i, LOOP + j)
                for j in range(GT):
                    load_v(i, GT + j)
                if not last:
                    load_gates(i + 1)

            with sp.Fori(FIRST, LOOPS - 1) as i:
                both(i)
            both(LOOPS - 1, last=True)
            sp.wait_ge(v_low, EXPERT_KEYS + 2)
            sp.dma_start(g_row, a["ln2_g"].partition_broadcast(P)).then_inc(row_landed, 16)
            sp.dma_start(b_row, a["ln2_b"].partition_broadcast(P)).then_inc(row_landed, 16)
            for t in range(NT):
                sp.wait_ge(ready, t + 1)
                sp.dma_start(out[0, P * t:P * (t + 1), :], h_tok[:, t, :]).then_inc(stored, 16)
            sp.wait_ge(stored, 16 * NT)

        @block.gpsimd
        def _(pool):
            def low(i, j):
                pool.wait_ge(u_high, fresh(i, j + 1))
                nc.gpsimd.tensor_tensor(u_hl[:, j % 2, 1, :], u_staged[:, j % 4, :], u_hl[:, j % 2, 0, :].bitcast(F32),
                                        ALU.subtract).then_inc(u_low, 1)

            low(FIRST, 0)
            low(FIRST, 1)
            with pool.Fori(FIRST, LOOPS - 1) as i:
                for j in range(LOOP):
                    low(i, j + 2)
            for j in range(LOOP - 2):
                low(LOOPS - 1, j + 2)

        @block.scalar
        def _(act):
            def high_u(i, j, free=True):
                act.wait_ge(u_landed[j % 4], i * 32 + (16 * (j // 4 + 1) - 32 * FIRST))
                if free:
                    act.wait_ge(hid_done, fresh(i, j - 1))
                nc.scalar.activation(u_hl[:, j % 2, 0, :], u_staged[:, j % 4, :], ACT.Copy).then_inc(u_high, 1)

            def high_v(i, j):
                act.wait_ge(v_landed[j % 2], i * 64 + (16 * (j // 2) + 16))
                if j % GT == 0:
                    act.wait_ge(sum_done, i * (2 * BANKS) + (BANKS * (j // GT) + BANKS))
                nc.scalar.activation(v_hl[:, j // GT, j % GT, 0, :], v_staged[:, j % 2, :], ACT.Copy).then_inc(v_high, 1)

            def high_coef(i, j):
                act.wait_ge(weighed, i * LOOP + (j + 1 + LOOP))
                nc.scalar.activation(coef_hl[:, j // GT, j % GT, 0, :], coef[:, j % 2, :], ACT.Copy).then_inc(coef_high, 1)

            high_u(FIRST, 0, free=False)
            high_u(FIRST, 1, free=False)
            high_u(FIRST, 2)
            for j in range(LOOP):
                high_v(0, j)
                high_coef(0, j)
                if j == 0:
                    high_u(FIRST, 3)
            with act.Fori(1, FIRST) as i:
                for j in range(LOOP):
                    high_v(i, j)
                    high_coef(i, j)

            def both(i, first=False, last=False):
                for r in range(2):
                    for j in range(GT * r, GT * (r + 1)):
                        if not (last and j >= LOOP - 2) and not (first and j < 2):
                            high_u(i, j + 2)
                        act.wait_ge(hid_done, fresh(i, j + 1))
                        act.wait_ge(coef_low, i * LOOP + (j + 1))
                        nc.scalar.activation(coef[:, j % 2, :], ps[:, j % 4, :], ACT.Gelu).then_inc(gelu_made, 1)
                        high_coef(i, j)
                    for j in range(GT * r, GT * (r + 1)):
                        high_v(i, j)

            both(FIRST, first=True)
            with act.Fori(FIRST + 1, LOOPS - 1) as i:
                both(i)
            both(LOOPS - 1, last=True)
            for t in range(NT):
                act.wait_ge(var_ready, t + 1)
                nc.scalar.activation(std[:, t:t + 1], mv[:, t, 1:2], ACT.Sqrt, bias=eps[:, 0:1]).then_inc(std_ready, 1)

        @block.tensor
        def _(pe):
            pe.sem_inc(sum_done, 2 * BANKS)

            def hidden(i, r, first=False):
                for j in range(GT * r, GT * (r + 1)):
                    pe.wait_ge(u_high, fresh(i, j + 1))
                    if not first:
                        pe.wait_ge(gelu_made, fresh(i, j - 3))
                    bank = ps[:, j % 4, :]
                    for k in range(KD):
                        for part in range(2):
                            nc.tensor.matmul(bank, u_hl[:, j % 2, 0, P * k:P * (k + 1)], h_hl[:, part, k, :],
                                             start=(k == 0 and part == 0), stop=False)
                    pe.wait_ge(u_low, fresh(i, j + 1))
                    for k in range(KD):
                        last = nc.tensor.matmul(bank, u_hl[:, j % 2, 1, P * k:P * (k + 1)], h_hl[:, 0, k, :],
                                                start=False, stop=(k == KD - 1))
                    last.then_inc(hid_done, 1)

            def sums(i, r):
                pe.wait_ge(coef_low, i * LOOP + (GT * r + GT + 2))
                pe.wait_ge(v_low, i * LOOP + (GT * r + GT + 2))
                for b in range(BANKS):
                    pe.wait_ge(sum_read, i * (2 * BANKS) + (BANKS * r + b + 1))
                    for j in range(GT):
                        for n, (c, v) in enumerate(((0, 0), (0, 1), (1, 0))):
                            last = nc.tensor.matmul(ps[:, 4 + b % 4, :], coef_hl[:, r, j, c, P * (b // 2):P * (b // 2 + 1)],
                                                    v_hl[:, r, j, v, 512 * (b % 2):512 * (b % 2 + 1)],
                                                    start=(j == 0 and n == 0), stop=(j == GT - 1 and n == 2))
                    last.then_inc(sum_done, 1)

            hidden(FIRST, 0, first=True)
            with pe.Fori(0, FIRST) as i:
                sums(i, 0)
                sums(i, 1)
            with pe.Fori(FIRST, LOOPS - 1) as i:
                hidden(i, 1)
                sums(i, 0)
                hidden(i + 1, 0)
                sums(i, 1)
            hidden(LOOPS - 1, 1)
            sums(LOOPS - 1, 0)
            sums(LOOPS - 1, 1)

        @block.vector
        def _(dve):
            v_ = nc.vector
            order = Order(dve, order_sem)
            put, settle = order.put, order.settle
            dve.sem_inc(weighed, LOOP)
            dve.sem_inc(coef_low, 2)
            dve.sem_inc(v_low, 2)
            dve.sem_inc(sum_read, 4)
            for t in range(NT):
                v_.tensor_scalar(h_tok[:, t, :], h_tok[:, t, :], ALPHA, None, ALU.mult).then_inc(scaled, 1)

            def weigh(i, j, is_parked):
                if j == 0:
                    dve.wait_ge(gates_landed, i * 16 + 16)
                if is_parked:
                    dve.wait_ge(act_landed[j % 2], i * 64 + (16 * (j // 2) + 16))
                else:
                    dve.wait_ge(gelu_made, fresh(i, j + 1))
                x = coef[:, j % 2, :].rearrange("p (l n) -> p l n", l=LOTS)
                v_.tensor_tensor(x, x, gates[:, :, LOT * j:LOT * (j + 1)], ALU.mult).then_inc(weighed, 1)

            def low_coef(i, j):
                dve.wait_ge(coef_high, i * LOOP + (j + 1))
                v_.tensor_tensor(coef_hl[:, j // GT, j % GT, 1, :], coef[:, j % 2, :],
                                 coef_hl[:, j // GT, j % GT, 0, :].bitcast(F32), ALU.subtract).then_inc(coef_low, 1)

            def low_v(i, j):
                dve.wait_ge(v_high, i * LOOP + (j + 1))
                v_.tensor_tensor(v_hl[:, j // GT, j % GT, 1, :], v_staged[:, j % 2, :],
                                 v_hl[:, j // GT, j % GT, 0, :].bitcast(F32), ALU.subtract).then_inc(v_low, 1)

            def gather(i, j):
                r = j // GT
                for b in range(2 * (j % GT), 2 * (j % GT) + 2):
                    dve.wait_ge(sum_done, i * (2 * BANKS) + (BANKS * r + b + 1 + 2 * BANKS))
                    part = h_tok[:, b // 2, 512 * (b % 2):512 * (b % 2 + 1)]
                    v_.tensor_tensor(part, part, ps[:, 4 + b % 4, :], ALU.add).then_inc(sum_read, 1)

            def parked_tile(i, j, gathered):
                weigh(i, j, True)
                low_v(i, j)
                low_coef(i, j)
                if gathered:
                    gather(*gathered)

            dve.wait_ge(scaled, NT)
            for j in range(LOOP):
                parked_tile(0, j, (0, j - GT) if j >= GT else None)
            with dve.Fori(1, FIRST) as i:
                for j in range(LOOP):
                    parked_tile(i, j, (i, j - GT) if j >= GT else (i - 1, j + GT))

            def both(i, first=False):
                for r in range(2):
                    for j in range(GT * r, GT * (r + 1)):
                        weigh(i, j, False)
                        low_coef(i, j)
                    for j in range(GT * r, GT * (r + 1)):
                        low_v(i, j)
                        if not (first and r == 0):
                            gather(*((i, j - GT) if r else (i - 1, j + GT)))

            for j in range(GT):
                gather(FIRST - 1, GT + j)
            both(FIRST, first=True)
            with dve.Fori(FIRST + 1, LOOPS) as i:
                both(i)
            dve.wait_ge(row_landed, 32)

            def normed(t):
                dve.wait_ge(std_ready, t + 1)
                put(v_.reciprocal(rstd[:, t:t + 1], std[:, t:t + 1]))
                settle()
                put(v_.tensor_scalar(h_tok[:, t, :], h_tok[:, t, :], mv[:, t, 0:1], rstd[:, t:t + 1],
                                     ALU.subtract, ALU.mult))
                settle()
                put(v_.tensor_tensor(h_tok[:, t, :], h_tok[:, t, :], g_row, ALU.mult))
                settle()
                v_.tensor_tensor(h_tok[:, t, :], h_tok[:, t, :], b_row, ALU.add).then_inc(ready, 1)

            for t in range(NT):
                gather(LOOPS - 1, GT + t)
                dve.wait_ge(sum_read, BANKS * (EXPERT_KEYS // GT - 1) + 2 * t + 2 + 4)
                for half in range(2):
                    put(v_.bn_stats(stats[:, t, half, :], h_tok[:, t, 512 * half:512 * (half + 1)]))
                settle()
                v_.bn_aggr(mv[:, t, :], stats[:, t, :, :]).then_inc(var_ready, 1)
                if t:
                    normed(t - 1)
            normed(NT - 1)


_OUT_SHAPE = (1, SEQ, D)


def lay_out(v):
    w = v["w_in"][0]
    A = HEADS * HD
    at = [0, A, A + KV, 2 * A + KV, 2 * A + KV + HD, 2 * A + KV + HD + HEADS]
    q, ckv, qi, ki, wi = (w[:, at[n]:at[n + 1]] for n in range(5))
    b = w[:, at[5]:at[5] + 3 * A + 256]
    gates = w[:, at[5] + 3 * A + 256:]
    cols = np.concatenate([qi, ki, ki, ckv, b, q, gates], axis=1)

    def by_columns(w):
        return np.ascontiguousarray(w.reshape(KD, P, -1, P).transpose(2, 1, 0, 3).reshape(-1, P, KD * P))

    wi_w = np.ascontiguousarray(wi.reshape(KD, P, HEADS).transpose(1, 0, 2))

    def columns(x):
        return x.reshape(-1, P).T

    twice = lambda x: np.concatenate([x, x])
    wq, u = by_columns(v["peer_wq"][0]), by_columns(v["peer_u"][0].T)
    order = [t for h in range(PEER_HEADS) for t in (wq[2 * h], wq[2 * h + 1], u[2 * h], u[2 * h + 1])]
    stream = np.concatenate([np.stack(order), u[2 * PEER_HEADS:]])
    named = {"ln_in_g": v["ln_in_g"], "ln_in_b": v["ln_in_b"], "mu": v["b_mu"][0], "b_gate": v["b_gate"][0],
             "kv_g": v["a_kv_norm_g"][0], "ki_g": twice(v["a_kidx_g"][0]), "ki_b": twice(v["a_kidx_b"][0]),
             "w0": v["b_w0"][0], "a0": v["b_a0"][0], "k_k": v["b_k_k"][0], "k_a": v["b_k_a"][0],
             "r_k": v["b_r_k"][0], "lnx_g": v["b_lnx_g"][0], "lnx_b": v["b_lnx_b"][0],
             "ln1_g": v["ln1_g"][0], "ln1_b": v["ln1_b"][0]}
    params = np.ascontiguousarray(np.concatenate([columns(named[n]) for n, _ in PARAMS], axis=1))
    return {"x": v["x"], "meta": v["meta"], "w_in_t": by_columns(cols), "wi_w": wi_w, "params": params,
            "ln_in_g": v["ln_in_g"], "ln_in_b": v["ln_in_b"],
            "w2": v["b_w2"], "a2": v["b_a2"], "g2": v["b_g2"],
            "w_uk": np.ascontiguousarray(v["a_w_uk"][0].reshape(KV, PAIRS, P).transpose(2, 1, 0)),
            "w_pa": v["w_pa"], "w_pb": v["w_pb"], "w_o": v["w_o"], "ln1_g": v["ln1_g"][0], "ln1_b": v["ln1_b"][0],
            "ln2_g": v["ln2_g"][0], "ln2_b": v["ln2_b"][0],
            "stream": stream, "v": v["peer_v"].reshape(EXPERT_KEYS, P, D),
            "sub_keys": np.ascontiguousarray(v["peer_subkeys"][0].reshape(2 * PEER_HEADS, EXPERT_KEYS, P).transpose(2, 0, 1)),
            "w_uv": v["a_w_uv"][0].reshape(KV, HEADS * HD)}


def kernel(**inputs):
    import concourse.bacc as bacc
    from concourse.bass_utils import run_bass_kernel_spmd

    nc = bacc.Bacc("TRN2", target_bir_lowering=False, num_devices=1)
    arrays, args = {}, {}
    for name, x in lay_out({k: np.asarray(x) for k, x in inputs.items()}).items():
        arrays[f"in_{name}"] = np.ascontiguousarray(x)
        args[name] = nc.dram_tensor(f"in_{name}", x.shape, mybir.dt.from_np(x.dtype), kind="ExternalInput").ap()
    out = nc.dram_tensor("out_0", _OUT_SHAPE, F32, kind="ExternalOutput").ap()
    build(nc, args, out)
    return run_bass_kernel_spmd(nc, [arrays], core_ids=[0]).results[0]["out_0"]
```
